# Optimizing a Trainium2 kernel written in Bass

```python
import jax, jax.numpy as jnp
from jax import lax
import numpy as np

D_MODEL = 1024
BATCH = 1
SEQ = 2048
DEPTH = 1

GRID_W = 64
CTX_LEN = 256
HEAD_DIM = 64
N_Q_HEADS = 8
N_KV_HEADS = 2
GQA_GROUP = N_Q_HEADS // N_KV_HEADS
ATTN_W = N_Q_HEADS * HEAD_DIM
KV_W = N_KV_HEADS * HEAD_DIM
N_FOURIER_GROUPS = 4
FOURIER_GROUP_W = 128
FOURIER_W = N_FOURIER_GROUPS * FOURIER_GROUP_W
D_MIX = ATTN_W + FOURIER_W
ROPE_FREQS = HEAD_DIM // 4
ROPE_THETA = 10000.0
Q_BLOCK = 128
EPS = 1e-6

Q0 = 0
K0 = Q0 + ATTN_W
V0 = K0 + KV_W
GA0 = V0 + KV_W
F0 = GA0 + ATTN_W
GF0 = F0 + FOURIER_W
D_IN = GF0 + FOURIER_W

kernel_name = 'hybrid_fourier_gqa_dit_block'

def rmsnorm(x, g):
    xf = x.astype(jnp.float32)
    y = xf * lax.rsqrt(jnp.mean(xf * xf, axis=-1, keepdims=True) + EPS)
    return (y * g.astype(jnp.float32)).astype(x.dtype)

def modulation(cond, w_mod, b_mod):
    m = jax.nn.silu(cond) @ w_mod + b_mod
    shift, scale, gate = jnp.split(m, 3, axis=-1)
    return shift, scale, gate

def axial_rope_tables(rows):
    row = jnp.repeat(jnp.arange(rows, dtype=jnp.float32), GRID_W)
    col = jnp.tile(jnp.arange(GRID_W, dtype=jnp.float32), rows)
    inv = ROPE_THETA ** (-jnp.arange(ROPE_FREQS, dtype=jnp.float32) / ROPE_FREQS)
    ang = jnp.stack([row[:, None] * inv, col[:, None] * inv], axis=1)
    return jnp.cos(ang)[:, None], jnp.sin(ang)[:, None]

def apply_axial_rope(t, cos, sin):
    b, n, h, _ = t.shape
    tf = t.astype(jnp.float32).reshape(b, n, h, 2, 2, ROPE_FREQS)
    t1, t2 = tf[..., 0, :], tf[..., 1, :]
    out = jnp.stack([t1 * cos - t2 * sin, t2 * cos + t1 * sin], axis=-2)
    return out.reshape(b, n, h, HEAD_DIM).astype(t.dtype)

def split_heads(t, n_heads):
    return t.reshape(t.shape[0], t.shape[1], n_heads, HEAD_DIM)

def blocked_gqa(q, k, v):
    b, n = q.shape[:2]
    nb = n // Q_BLOCK
    qb = (q * HEAD_DIM ** -0.5).reshape(b, nb, Q_BLOCK, N_KV_HEADS, GQA_GROUP, HEAD_DIM)
    qb = jnp.moveaxis(qb, 1, 0)

    def one_block(qblk):
        s = jnp.einsum('bqkgd,bskd->bkgqs', qblk, k, preferred_element_type=jnp.float32)
        p = jax.nn.softmax(s.astype(jnp.float32), axis=-1).astype(v.dtype)
        return jnp.einsum('bkgqs,bskd->bqkgd', p, v)

    ob = lax.map(one_block, qb)
    return jnp.moveaxis(ob, 0, 1).reshape(b, n, ATTN_W)

def fourier_mix(u, w_f):
    b, n, _ = u.shape
    ug = u.reshape(b, n, N_FOURIER_GROUPS, FOURIER_GROUP_W).astype(jnp.float32)
    z = jnp.fft.fft2(ug, axes=(1, 3), norm='ortho').real.astype(u.dtype)
    y = jnp.einsum('bngc,gcd->bngd', z, w_f)
    return y.reshape(b, n, FOURIER_W)

def gated_merge(p, attn_out, w_f, w_o):
    ga = p[..., GA0:F0]
    fu = p[..., F0:GF0]
    gf = p[..., GF0:D_IN]
    y = jnp.concatenate([attn_out * jax.nn.silu(ga), fourier_mix(fu, w_f) * jax.nn.silu(gf)], axis=-1)
    return y @ w_o

def setup_inputs(seed: int = 0) -> dict:
    key = jax.random.key(seed)
    ks = jax.random.split(key, 13)
    f32 = jnp.float32
    x = jax.random.normal(ks[0], (BATCH, SEQ, D_MODEL), f32)
    c = jax.random.normal(ks[1], (BATCH, D_MODEL), f32)
    ctx = jax.random.normal(ks[2], (BATCH, CTX_LEN, D_MODEL), f32)
    c_ctx = 0.5 * jax.random.normal(ks[3], (D_MODEL,), f32)
    norm_g = 1.0 + 0.02 * jax.random.normal(ks[4], (DEPTH, D_MODEL), f32)
    w_mod = 0.5 * D_MODEL ** -0.5 * jax.random.normal(ks[5], (DEPTH, D_MODEL, 3 * D_MODEL), f32)
    b_mod = 0.01 * jax.random.normal(ks[6], (DEPTH, 3 * D_MODEL), f32)
    w_in = D_MODEL ** -0.5 * jax.random.normal(ks[7], (DEPTH, D_MODEL, D_IN), f32)
    q_g = 1.0 + 0.02 * jax.random.normal(ks[8], (DEPTH, HEAD_DIM), f32)
    k_g = 1.0 + 0.02 * jax.random.normal(ks[9], (DEPTH, HEAD_DIM), f32)
    w_f = FOURIER_GROUP_W ** -0.5 * jax.random.normal(ks[10], (DEPTH, N_FOURIER_GROUPS, FOURIER_GROUP_W, FOURIER_GROUP_W), f32)
    w_o = D_MIX ** -0.5 * jax.random.normal(ks[11], (DEPTH, D_MIX, D_MODEL), f32)
    final_g = 1.0 + 0.02 * jax.random.normal(ks[12], (D_MODEL,), f32)
    return {'x': x, 'c': c, 'ctx': ctx, 'c_ctx': c_ctx, 'norm_g': norm_g, 'w_mod': w_mod, 'b_mod': b_mod,
            'w_in': w_in, 'q_g': q_g, 'k_g': k_g, 'w_f': w_f, 'w_o': w_o, 'final_g': final_g}

def reference(x, c, ctx, c_ctx, norm_g, w_mod, b_mod, w_in, q_g, k_g, w_f, w_o, final_g):
    rows = x.shape[1] // GRID_W
    cos, sin = axial_rope_tables(rows)
    for l in range(DEPTH):
        shift, scale, gate = modulation(c, w_mod[l], b_mod[l])
        shift_c, scale_c, gate_c = modulation(c_ctx, w_mod[l], b_mod[l])
        h = rmsnorm(x, norm_g[l]) * (1 + scale[:, None]) + shift[:, None]
        hc = rmsnorm(ctx, norm_g[l]) * (1 + scale_c) + shift_c
        update_ctx = l + 1 < DEPTH

        if update_ctx:
            pc = hc @ w_in[l]
            pc_kv = pc[..., K0:GA0]
        else:
            pc_kv = hc @ w_in[l][:, K0:GA0]
        k_ctx = rmsnorm(split_heads(pc_kv[..., :KV_W], N_KV_HEADS), k_g[l])
        v_ctx = split_heads(pc_kv[..., KV_W:], N_KV_HEADS)

        p = h @ w_in[l]
        q = apply_axial_rope(rmsnorm(split_heads(p[..., Q0:K0], N_Q_HEADS), q_g[l]), cos, sin)
        k = apply_axial_rope(rmsnorm(split_heads(p[..., K0:V0], N_KV_HEADS), k_g[l]), cos, sin)
        v = split_heads(p[..., V0:GA0], N_KV_HEADS)
        attn = blocked_gqa(q, jnp.concatenate([k, k_ctx], axis=1), jnp.concatenate([v, v_ctx], axis=1))
        x_new = x + gate[:, None] * gated_merge(p, attn, w_f[l], w_o[l])

        if update_ctx:
            qc = rmsnorm(split_heads(pc[..., Q0:K0], N_Q_HEADS), q_g[l])
            attn_c = blocked_gqa(qc, k_ctx, v_ctx)
            ctx = ctx + gate_c * gated_merge(pc, attn_c, w_f[l], w_o[l])
        x = x_new
    return rmsnorm(x, final_g)


_drawn_inputs = setup_inputs


def setup_inputs(seed=0):
    import zlib

    import numpy as np

    out = dict(_drawn_inputs(seed))
    spreads = {}
    factors = {'ctx': 8.0,
     'c_ctx': 8.0,
     'norm_g': 8.0,
     'b_mod': 8.0,
     'q_g': 8.0,
     'k_g': 8.0,
     'final_g': 2.89}
    for name, (base, spread) in spreads.items():
        noise = np.random.default_rng([zlib.crc32(name.encode()), seed]).standard_normal(out[name].shape)
        drawn = base * np.exp(spread * noise) if base else spread * noise
        out[name] = __import__('jax').numpy.asarray(drawn.astype(out[name].dtype))
    for name, factor in factors.items():
        out[name] = (out[name] * factor).astype(out[name].dtype)
    return out
```

```python
import concourse.bass as bass
from concourse import mybir
from contextlib import ExitStack

F32 = mybir.dt.float32
F32R = mybir.dt.float32r
ALU = mybir.AluOpType
ACT = mybir.ActivationFunctionType
X_AXIS = mybir.AxisListType.X

P = 128
D = 1024
KD = D // P
SEQ = 2048
CTX = 256
TT = SEQ // P
KEYS = SEQ + CTX
KT = KEYS // P
HD = 64
HQ = 8
HKV = 2
HN = HQ + HKV
ATTN_W = HQ * HD
KV_W = HKV * HD
QKV_W = ATTN_W + 2 * KV_W
GA0 = QKV_W
F0 = GA0 + ATTN_W
FOUR_W = 512
GF0 = F0 + FOUR_W
GROUPS = 4
REST_W = ATTN_W + 2 * FOUR_W
MT = REST_W // P
QB = 512
NQB = SEQ // QB
NB = HQ * NQB
EPS = 1e-6
RADIX = 4
SUB = SEQ // RADIX
SUBT = SUB // P


def split_matmul(pe, out, lhs_hi, lhs_lo, rhs_hi, rhs_lo, first, last):
    pe.matmul(out, lhs_hi, rhs_hi, start=first, stop=False)
    pe.matmul(out, lhs_hi, rhs_lo, start=False, stop=False)
    return pe.matmul(out, lhs_lo, rhs_hi, start=False, stop=last)


def modulation(nc, k, d):
    with ExitStack() as ctx:
        def sb(name, shape, dt=F32):
            return ctx.enter_context(nc.sbuf_tensor(name, shape, dt))

        w_mod = [sb(f"w_mod{g}", [P, KD, D]) for g in range(2)]
        cond = sb("cond", [P, 2, KD])
        cond_act = sb("cond_act", [P, KD, 2])
        cond_rep = sb("cond_rep", [P, KD, P])
        mod_bias = sb("mod_bias", [P, 2, KD])
        norm_col = sb("norm_col", [P, KD])
        gate_bias = sb("gate_bias", [1, D])
        final_row = sb("final_row", [1, D])
        head_row = sb("head_row", [1, HN, HD])
        ones_row = sb("ones_row", [1, P])
        w_raw = w_mod[1][:, :, 0:QKV_W]
        col_ps = ctx.enter_context(nc.psum_tensor("col_ps", [P, 2, KD, 2], F32))
        row_ps = [ctx.enter_context(nc.psum_tensor(f"row_ps{i}", [P, 512], F32)) for i in range(6)]
        S = k.sem
        s_mod = [S("w_mod0_loaded"), S("w_mod1_loaded")]
        s_small, s_wqkv, s_whi = S("small_loaded"), S("wqkv_loaded"), S("wqkv_hi_loaded")
        s_cond, s_rep, s_ones = S("cond_ready"), S("cond_rep_ready"), S("ones_ready")
        s_cols, s_rows, s_gate_ps = S("mod_cols_done"), S("rows_done"), S("gate_rows_done")
        s_scale, s_gated, s_end = S("scale_biased"), S("shift_ready"), S("modulation_copied")
        s_hrow = S("head_row_ready")
        w_mod_v = d["w_mod"][0].rearrange("(k p) (g n) -> g p k n", p=P, g=3)
        b_mod_v = d["b_mod"][0].rearrange("(g k p) -> p g k", p=P, g=3)
        w_qkv_v = d["w_in"][0][:, 0:QKV_W].rearrange("(k p) n -> p k n", p=P)

        block = ctx.enter_context(nc.Block())

        @block.sync
        def _(sp):
            with nc.allow_non_contiguous_dma(reason="small vectors laid out one element per partition"):
                sp.dma_start(cond[:, 0, :], d["c"][0].rearrange("(k p) -> p k", p=P)).then_inc(s_small, 16)
                sp.dma_start(cond[:, 1, :], d["c_ctx"].rearrange("(k p) -> p k", p=P)).then_inc(s_small, 16)
                sp.dma_start(w_mod[0][:], w_mod_v[0]).then_inc(s_mod[0], 16)
                sp.dma_start(w_mod[1][:], w_mod_v[1]).then_inc(s_mod[1], 16)
                for g in range(2):
                    sp.dma_start(mod_bias[:, g, :], b_mod_v[:, g, :]).then_inc(s_small, 16)
                sp.dma_start(norm_col[:], d["norm_g"][0].rearrange("(k p) -> p k", p=P)).then_inc(s_small, 16)
            sp.dma_start(gate_bias[:], d["b_mod"][0:1, 2 * D:3 * D]).then_inc(s_small, 16)
            sp.dma_start(final_row[:], d["final_g"].rearrange("(a n) -> a n", a=1)).then_inc(s_small, 16)
            for h in range(HN):
                sp.dma_start(head_row[:, h, :], (d["q_g"] if h < HQ else d["k_g"])[0:1, :]).then_inc(s_small, 16)
            sp.dma_start(k.ident[:], d["ident"]).then_inc(s_small, 16)
            sp.wait_ge(s_cols, 1)
            sp.dma_start(w_mod[0][:], w_mod_v[2]).then_inc(s_mod[0], 16)
            sp.wait_ge(s_cols, 2)
            sp.dma_start(w_raw, w_qkv_v).then_inc(s_wqkv, 16)

        small = 16 * (2 + 2 + 1 + 2 + HN + 1)

        @block.gpsimd
        def _(pool):
            pool.dma_start(k.wqkv_hi[:], w_qkv_v).then_inc(s_whi, 16)
            pool.wait_ge(s_whi, 16)

        @block.scalar
        def _(act):
            act.wait_ge(s_small, small)
            nc.scalar.activation(cond_act[:].rearrange("p k c -> p c k"), cond[:], ACT.Silu).then_inc(s_cond, 1)
            act.wait_ge(s_cond, 1)
            nc.scalar.activation(cond_rep[:], cond_act[:, :, 0:1].broadcast_to([P, KD, P]),
                                 ACT.Copy).then_inc(s_rep, 1)
            act.wait_ge(s_rows, 4)
            for i in range(2):
                nc.scalar.activation(k.final_bc[:, i * 512:(i + 1) * 512], row_ps[i][:], ACT.Copy)
            nc.scalar.activation(k.head_bc[:, 0:ATTN_W], row_ps[2][:], ACT.Copy)
            nc.scalar.activation(k.head_bc[:, ATTN_W:HN * HD], row_ps[3][:, 0:KV_W], ACT.Copy).then_inc(s_end, 1)
            act.wait_ge(s_gate_ps, 2)
            for i in range(2):
                last = nc.scalar.activation(k.gate_bc[:, i * 512:(i + 1) * 512], row_ps[4 + i][:], ACT.Copy)
            last.then_inc(s_end, 1)
            act.wait_ge(s_end, 2)

        @block.vector
        def _(dve):
            nc.vector.memset(ones_row[:], 1.0).then_inc(s_ones, 1)
            nc.vector.memset(k.ones_sq[:].bitcast(F32), 1.0)
            nc.vector.memset(k.zero_one[:, 0:HD].bitcast(F32), 0.0)
            nc.vector.memset(k.zero_one[:, HD:P].bitcast(F32), 1.0)
            nc.vector.memset(k.k_lo1[HD:HD + 1, :, :].bitcast(F32), 1.0)
            dve.wait_ge(s_small, small)
            nc.vector.tensor_scalar(head_row[:, 0:HQ, :], head_row[:, 0:HQ, :], HD ** -0.5, None,
                                    ALU.mult).then_inc(s_hrow, 1)
            dve.wait_ge(s_cols, 2)
            for side in range(2):
                nc.vector.tensor_tensor(k.shift[:, side, :], col_ps[:, 0, :, side], mod_bias[:, 0, :], ALU.add)
                last = nc.vector.tensor_tensor(k.scale[:, side, :], col_ps[:, 1, :, side], mod_bias[:, 1, :],
                                               ALU.add)
            last.then_inc(s_scale, 1)
            dve.wait_ge(s_scale, 1)
            for side in range(2):
                last = nc.vector.scalar_tensor_tensor(k.scale[:, side, :], k.scale[:, side, :], 1.0, norm_col[:],
                                                      ALU.add, ALU.mult)
            last.then_inc(s_gated, 1)
            dve.wait_ge(s_wqkv, 16)
            dve.wait_ge(s_whi, 16)
            nc.vector.tensor_tensor(k.wqkv_lo[:], w_raw, k.wqkv_hi[:].bitcast(F32), ALU.subtract).then_inc(s_gated, 1)
            dve.wait_ge(s_gated, 2)

        @block.tensor
        def _(pe):
            pe.wait_ge(s_ones, 1)
            pe.wait_ge(s_small, small)
            pe.wait_ge(s_hrow, 1)
            head_flat = head_row[:].rearrange("a h d -> a (h d)")
            for i in range(2):
                nc.tensor.matmul(row_ps[i][:], ones_row[:], final_row[:, i * 512:(i + 1) * 512],
                                 start=True, stop=True).then_inc(s_rows, 1)
            nc.tensor.matmul(row_ps[2][:], ones_row[:], head_flat[:, 0:ATTN_W], start=True, stop=True).then_inc(s_rows, 1)
            nc.tensor.matmul(row_ps[3][:, 0:KV_W], ones_row[:], head_flat[:, ATTN_W:HN * HD],
                             start=True, stop=True).then_inc(s_rows, 1)
            pe.wait_ge(s_cond, 1)
            for g in range(2):
                pe.wait_ge(s_mod[g], 16)
                for f in range(KD):
                    for c in range(KD):
                        last = nc.tensor.matmul(col_ps[:, g, f, :], w_mod[g][:, c, f * P:(f + 1) * P],
                                                cond_act[:, c, :], start=(c == 0), stop=(c == KD - 1))
                last.then_inc(s_cols, 1)
            pe.wait_ge(s_rep, 1)
            pe.wait_ge(s_mod[0], 32)
            for i in range(2):
                nc.tensor.matmul(row_ps[4 + i][:], ones_row[:], gate_bias[:, i * 512:(i + 1) * 512],
                                 start=True, stop=False)
                for c in range(KD):
                    last = nc.tensor.matmul(row_ps[4 + i][:], cond_rep[:, c, :], w_mod[0][:, c, i * 512:(i + 1) * 512],
                                            start=False, stop=(c == KD - 1))
                last.then_inc(s_gate_ps, 1)


def project_qkv(nc, k, d):
    with ExitStack() as ctx:
        def sb(name, shape, dt=F32):
            return ctx.enter_context(nc.sbuf_tensor(name, shape, dt))

        def ps(name, shape):
            return ctx.enter_context(nc.psum_tensor(name, shape, F32))

        W = 2 * P
        x = [sb(f"x{i}", [P, 2, D]) for i in range(2)]
        h = sb("h", [P, KD, W])
        h_hi = [sb(f"h_hi{i}", [P, KD, W], F32R) for i in range(2)]
        h_lo = [sb(f"h_lo{i}", [P, KD, W], F32R) for i in range(2)]
        square = sb("square", [P, 2, D], mybir.dt.bfloat16)
        stat = [sb(f"stat{i}", [P, 2]) for i in range(2)]
        stat_eps = [sb(f"stat_eps{i}", [P, 2]) for i in range(2)]
        rstd = [sb(f"rstd{i}", [P, 2]) for i in range(2)]
        minus_half = sb("minus_half", [P, HN])
        qkv = [sb(f"qkv{i}", [P, QKV_W]) for i in range(2)]
        qk_sq = sb("qk_sq", [P, HN, HD])
        qk_g = sb("qk_g", [P, HN, HD])
        qk_n = sb("qk_n", [P, HN, HD])
        qk_sin = sb("qk_sin", [P, HN, HD])
        qk_rot = sb("qk_rot", [P, HN, 2, HD])
        hstat = sb("hstat", [P, HN])
        hrstd = sb("hrstd", [P, HN])
        cos_t = [sb(f"cos{i}", [P, 2, HD]) for i in range(2)]
        sin_t = [sb(f"sin{i}", [P, 2, HD]) for i in range(2)]
        q_hilo = [sb(f"q_hilo{i}", [P, HQ, P], F32R) for i in range(2)]
        xt_ps = [ps(f"xt_ps{i}", [P, 2, W]) for i in range(2)]
        q_ps = ps("q_ps", [P, ATTN_W])
        kv_ps = ps("kv_ps", [P, 2 * KV_W])
        tr_ps = [ps(f"tr_ps{i}", [P, 4, P]) for i in range(3)]

        S = k.sem
        s_x = [S("x_loaded0"), S("x_loaded1")]
        s_table = [S("rope_loaded0"), S("rope_loaded1")]
        s_const = S("minus_half_set")
        s_sum, s_eps, s_rstd, s_xhat = S("x_square_sums"), S("x_eps_added"), S("x_rstd_ready"), S("x_normed")
        s_xt, s_h, s_hhi, s_hsplit = S("x_transposed"), S("h_ready"), S("h_hi_ready"), S("h_split")
        s_qp, s_kvp, s_qc, s_kvc = S("q_projected"), S("kv_projected"), S("q_copied"), S("kv_copied")
        s_sq, s_hsum, s_hmean, s_hrstd = S("head_squares"), S("head_sums"), S("head_means"), S("head_rstd_ready")
        s_g, s_n, s_c, s_r, s_dup = (S("head_gained"), S("head_normed"), S("rope_multiplied"), S("head_rotated"),
                                     S("head_doubled"))
        s_tr, s_trhi, s_trlo = S("qk_transposed"), S("qk_hi_ready"), S("qk_lo_ready")
        s_vhi, s_v = S("v_hi_ready"), S("v_ready")
        s_qst = [S("q_stored0"), S("q_stored1")]
        s_hst = [S("h_stored0"), S("h_stored1")]
        x_v = d["x"][0].rearrange("(s t p) n -> s p t n", t=2, p=P)
        ctx_v = d["ctx"][0].rearrange("(t p) n -> p t n", p=P)
        cos_v = d["cos"].rearrange("(s t p) n -> s p t n", t=2, p=P)
        sin_v = d["sin"].rearrange("(s t p) n -> s p t n", t=2, p=P)
        q_v = k.q_dram.rearrange("(h b) p q -> b p h q", b=NQB)
        h_v = k.h_dram.rearrange("e k p (s t) -> s e p k t", t=W)
        N_IT = TT // 4

        def run(engine, body):
            with engine.Fori(0, N_IT - 1) as i:
                body(i, False)
            body(N_IT - 1, True)

        def heads(is_ctx):
            return (HQ, HN) if is_ctx else (0, HN)

        block = ctx.enter_context(nc.Block())

        @block.sync
        def _(sp):
            def load_x(p, slot):
                sp.dma_start(x[slot][:], x_v[p]).then_inc(s_x[slot], 16)

            def load_tables(p, slot):
                sp.dma_start(cos_t[slot][:], cos_v[p]).then_inc(s_table[slot], 16)
                sp.dma_start(sin_t[slot][:], sin_v[p]).then_inc(s_table[slot], 16)

            def store_h(s, slot, p):
                sp.wait_ge(s_hsplit, s + 1)
                sp.dma_start(h_v[p][0], h_hi[slot][:].bitcast(F32)).then_inc(s_hst[slot], 16)
                sp.dma_start(h_v[p][1], h_lo[slot][:].bitcast(F32)).then_inc(s_hst[slot], 16)

            def store_q(t, slot, i, tau):
                sp.wait_ge(s_trlo, t + 1)
                sp.dma_start(q_v[i][:, :, tau * P:(tau + 1) * P], q_hilo[slot][:].bitcast(F32)).then_inc(s_qst[slot], 16)

            sp.dma_start(x[0][:], ctx_v).then_inc(s_x[0], 16)
            load_x(0, 1)
            load_tables(0, 1)
            sp.wait_ge(s_xt, 4)
            load_x(1, 0)

            def body(i, last):
                if not last:
                    sp.wait_ge(s_xt, 4 * (i * 2 + 2))
                    load_x(i * 2 + 2, 1)
                sp.wait_ge(s_c, 4 * i + 2)
                load_tables(i * 2 + 1, 0)
                store_h(i * 2 + 1, 1, i * 2)
                store_q(4 * i + 2, 0, i, 0)
                store_h(i * 2 + 2, 0, i * 2 + 1)
                if not last:
                    sp.wait_ge(s_xt, 4 * (i * 2 + 3))
                    load_x(i * 2 + 3, 0)
                    sp.wait_ge(s_c, 4 * i + 4)
                    load_tables(i * 2 + 2, 1)
                for tau in range(1, 4):
                    store_q(4 * i + (2 + tau), tau % 2, i, tau)

            run(sp, body)
            for slot in range(2):
                sp.wait_ge(s_qst[slot], 16 * (TT // 2 + 1))
                sp.wait_ge(s_hst[slot], 32 * (TT // 4 + 1))

        @block.gpsimd
        def _(pool):
            nc.gpsimd.memset(minus_half[:], -0.5).then_inc(s_const, 1)
            pool.wait_ge(s_const, 1)

            def x_rstd(s, slot):
                pool.wait_ge(s_eps, s + 1)
                nc.gpsimd.tensor_tensor(rstd[slot][:], stat_eps[slot][:], minus_half[:, 0:2], ALU.pow).then_inc(s_rstd, 1)

            def head_gain(t, slot, is_ctx=False):
                h0, h1 = heads(is_ctx)
                pool.wait_ge(s_qc, t + 1)
                pool.wait_ge(s_kvc, t + 1)
                if not is_ctx or t:
                    pool.wait_ge(s_n, t)
                nc.gpsimd.tensor_tensor(qk_g[:, h0:h1, :].rearrange("p h d -> p (h d)"),
                                        qkv[slot][:, h0 * HD:h1 * HD], k.head_bc[:, h0 * HD:h1 * HD],
                                        ALU.mult).then_inc(s_g, 1)
                pool.wait_ge(s_hmean, t + 1)
                nc.gpsimd.tensor_tensor(hrstd[:, h0:h1], hstat[:, h0:h1], minus_half[:, h0:h1],
                                        ALU.pow).then_inc(s_hrstd, 1)

            x_rstd(0, 0)
            x_rstd(1, 1)
            head_gain(0, 0, True)
            head_gain(1, 1, True)
            x_rstd(2, 0)

            def body(i, last):
                head_gain(4 * i + 2, 0)
                if not last:
                    x_rstd(i * 2 + 3, 1)
                head_gain(4 * i + 3, 1)
                head_gain(4 * i + 4, 0)
                head_gain(4 * i + 5, 1)
                if not last:
                    x_rstd(i * 2 + 4, 0)

            run(pool, body)

        @block.scalar
        def _(act):
            act.sem_inc(s_qst[0], 16)
            act.sem_inc(s_qst[1], 16)
            act.sem_inc(s_h, 2)

            def x_squares(s, slot, loads):
                act.wait_ge(s_x[slot], 16 * loads)
                nc.scalar.activation(square[:, 0, :], x[slot][:, 0, :], ACT.Square, accum_out=stat[slot][:, 0:1])
                nc.scalar.activation(square[:, 1, :], x[slot][:, 1, :], ACT.Square,
                                     accum_out=stat[slot][:, 1:2]).then_inc(s_sum, 1)

            def h_evacuate(s, side):
                if side == 0:
                    act.wait_ge(s_hsplit, s)
                for u in range(4):
                    act.wait_ge(s_xt, 4 * s + (u + 1))
                    for e in range(2):
                        f = 2 * u + e
                        last = nc.scalar.activation(h[:, f, :], xt_ps[u % 2][:, e, :], ACT.Identity,
                                                    scale=k.scale[:, side, f:f + 1], bias=k.shift[:, side, f:f + 1])
                    last.then_inc(s_h, 1)

            def copy_qkv(t, slot, is_ctx=False):
                h0, h1 = heads(is_ctx)
                if not is_ctx:
                    act.wait_ge(s_g, t - 1)
                    act.wait_ge(s_v, t - 1)
                    act.wait_ge(s_qp, t + 1)
                    nc.scalar.activation(qkv[slot][:, 0:ATTN_W], q_ps[:], ACT.Copy).then_inc(s_qc, 1)
                else:
                    act.sem_inc(s_qc, 1)
                act.wait_ge(s_kvp, t + 1)
                nc.scalar.activation(qkv[slot][:, ATTN_W:QKV_W], kv_ps[:], ACT.Copy).then_inc(s_kvc, 1)
                act.wait_ge(s_kvc, t + 1)
                if not is_ctx:
                    act.wait_ge(s_qc, t + 1)
                if not is_ctx or t:
                    act.wait_ge(s_hsum, t)
                nc.scalar.activation(qk_sq[:, h0:h1, :].rearrange("p h d -> p (h d)"),
                                     qkv[slot][:, h0 * HD:h1 * HD], ACT.Square).then_inc(s_sq, 1)

            def double_heads(t, is_ctx=False):
                h0, h1 = heads(is_ctx)
                act.wait_ge(s_r, t + 1)
                nc.scalar.activation(qk_rot[:, h0:h1, 1, :], qk_rot[:, h0:h1, 0, :], ACT.Copy).then_inc(s_dup, 1)

            def qk_hi(t, slot, key0, uses=None):
                act.wait_ge(s_tr, t + 1)
                if uses is not None:
                    act.wait_ge(s_qst[slot], 16 * uses)
                    nc.scalar.activation(q_hilo[slot][:, 0:4, :], tr_ps[0][:], ACT.Copy)
                    nc.scalar.activation(q_hilo[slot][:, 4:8, :], tr_ps[1][:], ACT.Copy)
                nc.scalar.activation(k.k_hi2[:, :, bass.ds(key0, P)], tr_ps[2][:, 0:HKV, :],
                                     ACT.Copy).then_inc(s_trhi, 1)

            x_squares(0, 0, 1)
            h_evacuate(0, 1)
            x_squares(1, 1, 1)
            h_evacuate(1, 0)
            copy_qkv(0, 0, True)
            double_heads(0, True)
            qk_hi(0, 0, SEQ)
            copy_qkv(1, 1, True)
            double_heads(1, True)
            qk_hi(1, 1, SEQ + P)
            x_squares(2, 0, 2)

            def body(i, last):
                h_evacuate(i * 2 + 2, 0)
                copy_qkv(4 * i + 2, 0)
                if not last:
                    x_squares(i * 2 + 3, 1, i + 2)
                double_heads(4 * i + 2)
                copy_qkv(4 * i + 3, 1)
                qk_hi(4 * i + 2, 0, i * (4 * P), 2 * i + 1)
                if not last:
                    h_evacuate(i * 2 + 3, 0)
                double_heads(4 * i + 3)
                copy_qkv(4 * i + 4, 0)
                qk_hi(4 * i + 3, 1, i * (4 * P) + P, 2 * i + 1)
                double_heads(4 * i + 4)
                copy_qkv(4 * i + 5, 1)
                qk_hi(4 * i + 4, 0, i * (4 * P) + 2 * P, 2 * i + 2)
                if not last:
                    x_squares(i * 2 + 4, 0, i + 3)
                double_heads(4 * i + 5)
                qk_hi(4 * i + 5, 1, i * (4 * P) + 3 * P, 2 * i + 2)

            run(act, body)

        @block.vector
        def _(dve):
            dve.sem_inc(s_hst[0], 32)
            dve.sem_inc(s_hst[1], 32)

            def x_norm(s, slot):
                dve.wait_ge(s_sum, s + 1)
                nc.vector.tensor_scalar(stat_eps[slot][:], stat[slot][:], 1.0 / D, EPS, ALU.mult, ALU.add).then_inc(s_eps, 1)
                dve.wait_ge(s_rstd, s + 1)
                for e in range(2):
                    last = nc.vector.tensor_scalar(x[slot][:, e, :], x[slot][:, e, :], rstd[slot][:, e:e + 1], None,
                                                   ALU.mult)
                last.then_inc(s_xhat, 1)

            def h_split(s, slot, uses=None, s_prev_tiles=None):
                dve.wait_ge(s_h, 4 * s + 6)
                if uses is not None:
                    dve.wait_ge(s_hst[slot], 32 * uses)
                if s_prev_tiles is not None:
                    dve.wait_ge(s_kvp, s_prev_tiles)
                nc.vector.tensor_copy(h_hi[slot][:], h[:]).then_inc(s_hhi, 1)
                dve.wait_ge(s_hhi, s + 1)
                nc.vector.tensor_tensor(h_lo[slot][:], h[:], h_hi[slot][:].bitcast(F32), ALU.subtract).then_inc(s_hsplit, 1)

            def head_norm(t, slot, key_tile, rope=None):
                is_ctx = rope is None
                h0, h1 = heads(is_ctx)
                n = h1 - h0
                dve.wait_ge(s_kvc, t + 1)
                v = qkv[slot][:, ATTN_W + KV_W:QKV_W].rearrange("p (h d) -> p h d", h=HKV)
                v_hl = k.v_hl[:, bass.ds(key_tile, 1), :, :].rearrange("p a h d -> p (a h) d")
                nc.vector.tensor_copy(v_hl[:, :, 0:HD], v).then_inc(s_vhi, 1)
                dve.wait_ge(s_sq, t + 1)
                if not is_ctx or t:
                    dve.wait_ge(s_hrstd, t)
                nc.vector.reduce_sum(hstat[:, h0:h1], qk_sq[:, h0:h1, :], X_AXIS).then_inc(s_hsum, 1)
                dve.wait_ge(s_vhi, t + 1)
                nc.vector.tensor_tensor(v_hl[:, :, HD:P], v, v_hl[:, :, 0:HD].bitcast(F32), ALU.subtract).then_inc(s_v, 1)
                dve.wait_ge(s_hsum, t + 1)
                nc.vector.tensor_scalar(hstat[:, h0:h1], hstat[:, h0:h1], 1.0 / HD, EPS, ALU.mult,
                                        ALU.add).then_inc(s_hmean, 1)
                dve.wait_ge(s_g, t + 1)
                dve.wait_ge(s_hrstd, t + 1)
                if is_ctx:
                    if t:
                        dve.wait_ge(s_tr, t)
                    dve.sem_inc(s_c, 1)
                    nc.vector.tensor_tensor(qk_rot[:, h0:h1, 0, :], qk_g[:, h0:h1, :],
                                            hrstd[:, h0:h1].unsqueeze(2).broadcast_to([P, n, HD]),
                                            ALU.mult).then_inc(s_n, 1)
                    dve.wait_ge(s_n, t + 1)
                    dve.sem_inc(s_r, 1)
                    return
                nc.vector.tensor_tensor(qk_n[:], qk_g[:], hrstd[:].unsqueeze(2).broadcast_to([P, HN, HD]),
                                        ALU.mult).then_inc(s_n, 1)
                tslot, e, loads = rope
                dve.wait_ge(s_table[tslot], 32 * loads)
                dve.wait_ge(s_n, t + 1)
                nc.vector.tensor_tensor(qk_sin[:], qk_n[:], sin_t[tslot][:, e:e + 1, :].broadcast_to([P, HN, HD]), ALU.mult)
                nc.vector.tensor_tensor(qk_n[:], qk_n[:], cos_t[tslot][:, e:e + 1, :].broadcast_to([P, HN, HD]),
                                        ALU.mult).then_inc(s_c, 1)
                dve.wait_ge(s_c, t + 1)
                dve.wait_ge(s_tr, t)
                def half(buf, n_half):
                    return buf.rearrange("p h (a f) -> p h a f", a=2)[:, :, :, n_half * HD // 4:(n_half + 1) * HD // 4]
                rot = qk_rot[:, :, 0, :]
                nc.vector.tensor_tensor(half(rot, 0), half(qk_n[:], 0), half(qk_sin[:], 1), ALU.subtract)
                nc.vector.tensor_tensor(half(rot, 1), half(qk_n[:], 1), half(qk_sin[:], 0), ALU.add).then_inc(s_r, 1)

            def qk_lo(t, slot, key0, is_ctx=False):
                dve.wait_ge(s_trhi, t + 1)
                if not is_ctx:
                    for g in range(2):
                        lo = q_hilo[slot][HD:P, 4 * g:4 * g + 4, :]
                        nc.vector.tensor_tensor(lo, tr_ps[g][HD:P], lo.bitcast(F32), ALU.subtract)
                nc.vector.tensor_tensor(k.k_lo1[0:HD, :, bass.ds(key0, P)], tr_ps[2][0:HD, 0:HKV, :],
                                        k.k_hi2[0:HD, :, bass.ds(key0, P)].bitcast(F32), ALU.subtract).then_inc(s_trlo, 1)

            x_norm(0, 0)
            h_split(0, 0)
            x_norm(1, 1)
            h_split(1, 1, 1)
            head_norm(0, 0, TT)
            qk_lo(0, 0, SEQ, True)
            head_norm(1, 1, TT + 1)
            qk_lo(1, 1, SEQ + P, True)
            x_norm(2, 0)

            def body(i, last):
                h_split(i * 2 + 2, 0, i + 1, 4 * i + 2)
                head_norm(4 * i + 2, 0, 4 * i, (1, 0, i + 1))
                if not last:
                    x_norm(i * 2 + 3, 1)
                head_norm(4 * i + 3, 1, 4 * i + 1, (1, 1, i + 1))
                qk_lo(4 * i + 2, 0, i * (4 * P))
                if not last:
                    h_split(i * 2 + 3, 1, i + 2, 4 * i + 4)
                head_norm(4 * i + 4, 0, 4 * i + 2, (0, 0, i + 1))
                qk_lo(4 * i + 3, 1, i * (4 * P) + P)
                head_norm(4 * i + 5, 1, 4 * i + 3, (0, 1, i + 1))
                qk_lo(4 * i + 4, 0, i * (4 * P) + 2 * P)
                if not last:
                    x_norm(i * 2 + 4, 0)
                qk_lo(4 * i + 5, 1, i * (4 * P) + 3 * P)

            run(dve, body)

        @block.tensor
        def _(pe):
            def x_transpose(s, slot):
                pe.wait_ge(s_xhat, s + 1)
                for u in range(4):
                    pe.wait_ge(s_h, 4 * s + (u + 1))
                    for e in range(2):
                        for t in range(2):
                            f = 2 * u + e
                            last = nc.tensor.transpose(xt_ps[u % 2][:, e, t * P:(t + 1) * P],
                                                       x[slot][:, t, f * P:(f + 1) * P], k.ident[:])
                    last.then_inc(s_xt, 1)

            def project(s, t, slot, e, is_ctx=False):
                pe.wait_ge(s_hsplit, s + 1)
                hs = slice(e * P, (e + 1) * P)
                if not is_ctx:
                    pe.wait_ge(s_qc, t)
                    for c in range(KD):
                        last = split_matmul(nc.tensor, q_ps[:], h_hi[slot][:, c, hs], h_lo[slot][:, c, hs],
                                            k.wqkv_hi[:, c, 0:ATTN_W], k.wqkv_lo[:, c, 0:ATTN_W], c == 0, c == KD - 1)
                    last.then_inc(s_qp, 1)
                else:
                    pe.sem_inc(s_qp, 1)
                if not is_ctx or t:
                    pe.wait_ge(s_kvc, t)
                for c in range(KD):
                    last = split_matmul(nc.tensor, kv_ps[:], h_hi[slot][:, c, hs], h_lo[slot][:, c, hs],
                                        k.wqkv_hi[:, c, ATTN_W:QKV_W], k.wqkv_lo[:, c, ATTN_W:QKV_W],
                                        c == 0, c == KD - 1)
                last.then_inc(s_kvp, 1)

            def head_transpose(t, is_ctx=False):
                pe.wait_ge(s_dup, t + 1)
                if not is_ctx or t:
                    pe.wait_ge(s_trlo, t)
                for hh in range(*heads(is_ctx)):
                    last = nc.tensor.transpose(tr_ps[hh // 4][:, hh % 4, :],
                                               qk_rot[:, hh, :, :].rearrange("p e d -> p (e d)"), k.ident[:])
                last.then_inc(s_tr, 1)

            x_transpose(0, 0)
            x_transpose(1, 1)
            project(0, 0, 0, 0, True)
            head_transpose(0, True)
            project(0, 1, 0, 1, True)
            head_transpose(1, True)

            def body(i, last):
                x_transpose(i * 2 + 2, 0)
                project(i * 2 + 1, 4 * i + 2, 1, 0)
                project(i * 2 + 1, 4 * i + 3, 1, 1)
                head_transpose(4 * i + 2)
                if not last:
                    x_transpose(i * 2 + 3, 1)
                project(i * 2 + 2, 4 * i + 4, 0, 0)
                head_transpose(4 * i + 3)
                project(i * 2 + 2, 4 * i + 5, 0, 1)
                head_transpose(4 * i + 4)
                head_transpose(4 * i + 5)

            run(pe, body)


MAX_CHUNKS = [512, 512, 512, 512, 256]
MAX_USES = QB // P * len(MAX_CHUNKS)
MAX_AT = [3, 4, 3, 4, 3, 3, 0, 0, 0]
MAX_ROW_AT = 6
PAIRS = KT // 2
POOL_LO = (0, 2, 4, 6)


def attention(nc, k, d):
    with ExitStack() as ctx:
        def sb(name, shape, dt=F32):
            return ctx.enter_context(nc.sbuf_tensor(name, shape, dt))

        def ps(name, shape):
            return ctx.enter_context(nc.psum_tensor(name, shape, F32))

        q_hilo = [sb(f"blk_q_hilo{i}", [P, QB], F32R) for i in range(2)]
        q_negm = [sb(f"blk_q_negm{i}", [P, QB], F32R) for i in range(2)]
        chunk_max = sb("chunk_max", [P, QB // P, len(MAX_CHUNKS)])
        neg_max = sb("neg_max", [P, QB // P])
        diag = sb("diag", [P, QB], F32R)
        prob = [sb(f"prob{i}", [P, 2 * QB]) for i in range(3)]
        prob_hi = [sb(f"prob_hi{i}", [P, 2 * QB], F32R) for i in range(3)]
        prob_lo = [sb(f"prob_lo{i}", [P, 2 * QB], F32R) for i in range(3)]
        v_one = sb("v_one", [P, KT, HKV, P], F32R)
        part = sb("part", [HD, QB])
        hi_part = sb("hi_part", [HD, QB])
        lo_part = sb("lo_part", [HD, QB])
        att = [sb(f"att{i}", [HD, QB]) for i in range(2)]
        den = [sb(f"den{i}", [1, QB]) for i in range(2)]
        max_ps = [ps(f"max_ps{i}", [P, QB]) for i in range(2)]
        s_ps = [ps(f"s_ps{i}", [P, 2 * QB]) for i in range(2)]
        hi_ps = ps("hi_ps", [P, QB])
        lo_ps = ps("lo_ps", [P, QB])

        S = k.sem
        s_q = [S("blk_q_loaded0"), S("blk_q_loaded1")]
        s_mfull, s_mfree, s_mx = S("max_bank_full"), S("max_bank_free"), S("chunk_max_done")
        s_vone = S("v_one_ready")
        s_neg, s_diag = S("neg_max_done"), S("diag_ready")
        s_score, s_exp = S("scores_ready"), S("scores_exponentiated")
        s_lo_dve, s_lo_pool = S("prob_lo_dve"), S("prob_lo_pool")
        s_pv, s_part, s_lopart, s_sum = S("pv_done"), S("part_copied"), S("lo_part_copied"), S("hi_part_summed")
        s_att, s_den = S("att_ready"), S("den_ready")
        s_st = [S("att_stored0"), S("att_stored1")]
        att_v, den_v, q_v = k.att_dram, k.den_dram, k.q_dram

        HALF = NB // HKV
        N_IT = HALF // 2

        def run(engine, body):
            for kvh in range(HKV):
                with engine.Fori(0, N_IT - 1) as i:
                    body(i * 2 + HALF * kvh, 0, kvh, kvh)
                    body(i * 2 + (HALF * kvh + 1), 1, kvh, kvh)
                body(HALF * kvh + HALF - 2, 0, kvh, kvh)
                body(HALF * kvh + HALF - 1, 1, kvh, kvh + 1 if kvh + 1 < HKV else None)

        def slot2(slot, j):
            return (slot * PAIRS + j) % 2

        def slot3(j):
            return j % 3

        block = ctx.enter_context(nc.Block())

        @block.sync
        def _(sp):
            def load(b, slot):
                sp.dma_start(q_hilo[slot][:].bitcast(F32), q_v[b]).then_inc(s_q[slot], 16)
                sp.dma_start(q_negm[slot][0:HD, :].bitcast(F32), q_v[b][0:HD, :]).then_inc(s_q[slot], 16)

            load(0, 0)
            load(1, 1)

            def body(b, slot, kvh, next_kvh):
                sp.wait_ge(s_score, b * PAIRS + PAIRS)
                if next_kvh is not None and not (isinstance(b, int) and b + 2 >= NB):
                    load(b + 2, slot)
                sp.wait_ge(s_att, b + 2)
                sp.dma_start(att_v[b], att[slot][:]).then_inc(s_st[slot], 16)
                sp.wait_ge(s_den, b + 2)
                sp.dma_start(den_v[b], den[slot][:]).then_inc(s_st[slot], 16)

            run(sp, body)
            for slot in range(2):
                sp.wait_ge(s_st[slot], 32 * (NB // 2 + 1))

        @block.gpsimd
        def _(pool):
            pool.sem_inc(s_att, 1)
            pool.sem_inc(s_st[0], 32)
            pool.sem_inc(s_st[1], 32)

            def lo(b, j):
                pool.wait_ge(s_exp, b * PAIRS + (j + 3))
                nc.gpsimd.tensor_tensor(prob_lo[slot3(j)][:], prob[slot3(j)][:], prob_hi[slot3(j)][:].bitcast(F32),
                                        ALU.subtract).then_inc(s_lo_pool, 1)

            lo(0, 0)

            def body(b, slot, kvh, next_kvh):
                for j in POOL_LO[1:]:
                    lo(b, j)
                if next_kvh is not None:
                    lo(b + 1, POOL_LO[0])
                pool.wait_ge(s_lopart, b + 1)
                pool.wait_ge(s_sum, b + 2)
                pool.wait_ge(s_st[slot], (b - slot) * 16 + 32)
                nc.gpsimd.tensor_tensor(att[slot][:], hi_part[:], lo_part[:], ALU.add).then_inc(s_att, 1)

            run(pool, body)

        @block.scalar
        def _(act):
            act.sem_inc(s_exp, 2)
            act.sem_inc(s_den, 1)

            def exponentials(b, slot, j):
                act.wait_ge(s_score, b * PAIRS + (j + 1))
                act.wait_ge(s_pv, b * PAIRS + (j + 1))
                s = s_ps[slot2(slot, j)]
                nc.scalar.activation(prob_hi[slot3(j)][:], s[:], ACT.Exp)
                nc.scalar.activation(prob[slot3(j)][:], s[:], ACT.Exp).then_inc(s_exp, 1)

            def evacuate(b, slot):
                act.wait_ge(s_pv, b * PAIRS + (PAIRS + 3))
                act.wait_ge(s_sum, b + 1)
                nc.scalar.activation(part[:], hi_ps[HD:P, :], ACT.Copy).then_inc(s_part, 1)
                act.wait_ge(s_st[slot], (b - slot) * 16 + 32)
                nc.scalar.activation(den[slot][:], lo_ps[HD:HD + 1, :], ACT.Copy).then_inc(s_den, 1)

            exponentials(0, 0, 0)

            def body(b, slot, kvh, next_kvh):
                for j in range(1, PAIRS):
                    exponentials(b, slot, j)
                if next_kvh is not None:
                    exponentials(b + 1, 1 - slot, 0)
                evacuate(b, slot)

            run(act, body)

        @block.vector
        def _(dve):
            dve.sem_inc(s_mfree, 2)
            dve.sem_inc(s_sum, 1)

            def reduce(b, slot, u):
                qt, kc = divmod(u, len(MAX_CHUNKS))
                bank = max_ps[(slot * (MAX_USES + 1) + u) % 2]
                dve.wait_ge(s_mfull, b * (MAX_USES + 1) + (u + 1))
                last = nc.vector.reduce_max(chunk_max[:, qt, kc:kc + 1], bank[:, 0:MAX_CHUNKS[kc]], X_AXIS)
                return last.then_inc(s_mfree, 1)

            def negate(b, slot):
                dve.wait_ge(s_mfree, b * (MAX_USES + 1) + (MAX_USES + 2))
                nc.vector.tensor_reduce(neg_max[:], chunk_max[:], X_AXIS, ALU.max, negate=True).then_inc(s_neg, 1)
                dve.wait_ge(s_neg, b + 1)
                for qt in range(QB // P):
                    last = nc.vector.tensor_scalar(diag[:, qt * P:(qt + 1) * P], k.ident[:], neg_max[:, qt:qt + 1],
                                                   None, ALU.mult)
                last.then_inc(s_diag, 1)

            def max_row(b, slot):
                bank = max_ps[(slot * (MAX_USES + 1) + MAX_USES) % 2]
                dve.wait_ge(s_mfull, b * (MAX_USES + 1) + (MAX_USES + 1))
                dve.wait_ge(s_q[slot], (b - slot) * 16 + 32)
                nc.vector.tensor_copy(q_negm[slot][HD:HD + 1, :], bank[HD:HD + 1, :]).then_inc(s_mfree, 1)

            def lo(b, slot, j):
                if j in POOL_LO:
                    return
                dve.wait_ge(s_exp, b * PAIRS + (j + 3))
                nc.vector.tensor_tensor(prob_lo[slot3(j)][:], prob[slot3(j)][:], prob_hi[slot3(j)][:].bitcast(F32),
                                        ALU.subtract).then_inc(s_lo_dve, 1)

            def evacuate(b, slot):
                dve.wait_ge(s_pv, b * PAIRS + (PAIRS + 3))
                dve.wait_ge(s_att, b + 1)
                nc.vector.tensor_copy(lo_part[:], lo_ps[0:HD, :]).then_inc(s_lopart, 1)
                dve.wait_ge(s_part, b + 1)
                nc.vector.tensor_tensor(hi_part[:], hi_ps[0:HD, :], part[:], ALU.add).then_inc(s_sum, 1)

            nc.vector.memset(v_one[:, :, :, HD:P].bitcast(F32), 1.0)
            nc.vector.tensor_copy(v_one[:, :, :, 0:HD], k.v_hl[:, :, :, 0:HD].bitcast(F32)).then_inc(s_vone, 1)
            for u in range(MAX_USES):
                reduce(0, 0, u)
            negate(0, 0)
            max_row(0, 0)

            def body(b, slot, kvh, next_kvh):
                u = 0
                for j in range(PAIRS):
                    n_max = MAX_AT[j] if next_kvh is not None else 0
                    for n in range(max(n_max, 1)):
                        if n < n_max:
                            reduce(b + 1, 1 - slot, u)
                            u += 1
                        if n == 0 and j + 1 < PAIRS:
                            lo(b, slot, j + 1)
                    if n_max and u == MAX_USES:
                        negate(b + 1, 1 - slot)
                    if next_kvh is not None and j == MAX_ROW_AT:
                        max_row(b + 1, 1 - slot)
                evacuate(b, slot)

            run(dve, body)

        @block.tensor
        def _(pe):
            pe.sem_inc(s_pv, 3)

            def max_use(b, slot, kvh, u):
                qt, kc = divmod(u, len(MAX_CHUNKS))
                bank = max_ps[(slot * (MAX_USES + 1) + u) % 2]
                if u == 0:
                    pe.wait_ge(s_q[slot], (b - slot) * 16 + 32)
                pe.wait_ge(s_mfree, b * (MAX_USES + 1) + (u + 1))
                key0 = sum(MAX_CHUNKS[:kc])
                nc.tensor.matmul(bank[:, 0:MAX_CHUNKS[kc]], q_hilo[slot][:, qt * P:(qt + 1) * P],
                                 k.k_hi2[:, kvh, key0:key0 + MAX_CHUNKS[kc]], start=True, stop=True).then_inc(s_mfull, 1)

            def broadcast_max(b, slot):
                pe.wait_ge(s_diag, b + 1)
                pe.wait_ge(s_mfree, b * (MAX_USES + 1) + (MAX_USES + 1))
                bank = max_ps[(slot * (MAX_USES + 1) + MAX_USES) % 2]
                nc.tensor.matmul(bank[:], k.ones_sq[:], diag[:], start=True, stop=True).then_inc(s_mfull, 1)

            def scores(b, slot, kvh, j, e):
                if j == 0 and e == 0:
                    pe.wait_ge(s_mfree, (b + 1) * (MAX_USES + 1) + 2)
                if e == 0:
                    pe.wait_ge(s_exp, b * PAIRS + (j + 1))
                keys = slice((2 * j + e) * P, (2 * j + e + 1) * P)
                out = s_ps[slot2(slot, j)][:, e * QB:(e + 1) * QB]
                nc.tensor.matmul(out, k.k_hi2[:, kvh, keys], q_hilo[slot][:], start=True, stop=False)
                last = nc.tensor.matmul(out, k.k_lo1[0:HD + 1, kvh, keys], q_negm[slot][0:HD + 1, :],
                                        start=False, stop=True)
                if e == 1:
                    last.then_inc(s_score, 1)

            def pv(b, slot, kvh, j, e):
                if j == 0 and e == 0:
                    pe.wait_ge(s_sum, b + 1)
                    pe.wait_ge(s_den, b + 1)
                if e == 0:
                    pe.wait_ge(s_exp, b * PAIRS + (j + 3))
                    if j in POOL_LO:
                        pe.wait_ge(s_lo_pool, b * len(POOL_LO) + (POOL_LO.index(j) + 1))
                    else:
                        before = sum(1 for m in range(j) if m not in POOL_LO)
                        pe.wait_ge(s_lo_dve, b * (PAIRS - len(POOL_LO)) + (before + 1))
                kt = 2 * j + e
                q = slice(e * QB, (e + 1) * QB)
                hi, lo = prob_hi[slot3(j)][:, q], prob_lo[slot3(j)][:, q]
                first, final = kt == 0, kt == KT - 1
                nc.tensor.matmul(hi_ps[:], k.v_hl[:, kt, kvh, :], hi, start=first, stop=final)
                nc.tensor.matmul(lo_ps[:], k.zero_one[:], hi, start=first, stop=False)
                last = nc.tensor.matmul(lo_ps[:], v_one[:, kt, kvh, :], lo, start=False, stop=final)
                if e == 1:
                    last.then_inc(s_pv, 1)

            for u in range(MAX_USES):
                max_use(0, 0, 0, u)
            pe.wait_ge(s_vone, 1)
            broadcast_max(0, 0)
            for j in range(2):
                for e in range(2):
                    scores(0, 0, 0, j, e)

            def body(b, slot, kvh, next_kvh):
                u = 0
                for j in range(PAIRS):
                    n_max = MAX_AT[j] if next_kvh is not None else 0
                    if j + 2 < PAIRS:
                        ahead = [(scores, b, slot, kvh, j + 2, e) for e in range(2)]
                    elif next_kvh is not None:
                        ahead = [(scores, b + 1, 1 - slot, next_kvh, j + 2 - PAIRS, e) for e in range(2)]
                    else:
                        ahead = []
                    here = [(pv, b, slot, kvh, j, e) for e in range(2)]
                    for n, (f, *args) in enumerate(ahead + here):
                        if n == 2 and next_kvh is not None and j == MAX_ROW_AT:
                            broadcast_max(b + 1, 1 - slot)
                        f(*args)
                        if n < n_max:
                            max_use(b + 1, 1 - slot, next_kvh, u)
                            u += 1

            run(pe, body)


def project_gates(nc, k, d):
    with ExitStack() as ctx:
        def sb(name, shape, dt=F32):
            return ctx.enter_context(nc.sbuf_tensor(name, shape, dt))

        TG = 512
        N_TG = SEQ // TG
        CH = 2 * P
        w_hi = sb("w_rest_hi", [P, KD, REST_W], F32R)
        w_lo = sb("w_rest_lo", [P, KD, REST_W], F32R)
        w_raw = [sb(f"w_rest_raw{i}", [P, KD, CH]) for i in range(2)]
        hh = [sb(f"hh{i}", [P, KD, TG], F32R) for i in range(2)]
        hl = [sb(f"hl{i}", [P, KD, TG], F32R) for i in range(2)]
        stage = [sb(f"stage{i}", [P, TG]) for i in range(3)]
        acc = [ctx.enter_context(nc.psum_tensor(f"acc{i}", [P, TG], F32)) for i in range(4)]
        S = k.sem
        NCH = REST_W // CH
        s_raw = [S("w_rest_loaded0"), S("w_rest_loaded1")]
        s_whi = [S(f"w_rest_hi{c}") for c in range(NCH)]
        s_wlo = S("w_rest_lo_ready")
        s_hh = [S("hh_loaded0"), S("hh_loaded1")]
        s_acc, s_free = S("rest_projected"), S("rest_bank_read")
        s_st = [S(f"rest_stored{i}") for i in range(3)]
        w_v = d["w_in"][0][:, GA0:GA0 + REST_W].rearrange("(k p) (c n) -> c p k n", p=P, n=CH)
        h_v = k.h_dram.rearrange("e k p (g t) -> g e p k t", t=TG)
        r_v = k.rest_dram.rearrange("m p (g t) -> g m p t", t=TG)

        def run(engine, body):
            with engine.Fori(0, N_TG // 2) as i:
                for slot in range(2):
                    body(i * 2 + slot, slot, i)

        block = ctx.enter_context(nc.Block())

        @block.sync
        def _(sp):
            def load_h(tg):
                sp.dma_start(hh[tg % 2][:].bitcast(F32), h_v[tg][0]).then_inc(s_hh[tg % 2], 16)
                sp.dma_start(hl[tg % 2][:].bitcast(F32), h_v[tg][1]).then_inc(s_hh[tg % 2], 16)

            sp.dma_start(w_raw[0][:], w_v[0]).then_inc(s_raw[0], 16)
            load_h(0)
            for c in range(1, NCH):
                if c >= 2:
                    sp.wait_ge(s_wlo, c - 1)
                sp.dma_start(w_raw[c % 2][:], w_v[c]).then_inc(s_raw[c % 2], 16)
            load_h(1)
            for tg in range(N_TG):
                for m in range(MT):
                    sp.wait_ge(s_free, tg * MT + (m + 5))
                    sp.dma_start(r_v[tg][m], stage[m % 3][:]).then_inc(s_st[m % 3], 16)
                if tg + 2 < N_TG:
                    sp.wait_ge(s_acc, (tg + 1) * MT)
                    load_h(tg + 2)
            for i in range(3):
                sp.wait_ge(s_st[i], 16 * (N_TG * MT // 3 + 1))

        @block.gpsimd
        def _(pool):
            for c in range(NCH):
                pool.dma_start(w_hi[:, :, c * CH:(c + 1) * CH], w_v[c]).then_inc(s_whi[c], 16)
            for c in range(NCH):
                pool.wait_ge(s_whi[c], 16)

        @block.vector
        def _(dve):
            for c in range(NCH):
                cols = slice(c * CH, (c + 1) * CH)
                dve.wait_ge(s_raw[c % 2], 16 * (c // 2 + 1))
                dve.wait_ge(s_whi[c], 16)
                nc.vector.tensor_tensor(w_lo[:, :, cols], w_raw[c % 2][:], w_hi[:, :, cols].bitcast(F32),
                                        ALU.subtract).then_inc(s_wlo, 1)
            dve.wait_ge(s_wlo, NCH)

        @block.scalar
        def _(act):
            act.sem_inc(s_free, 4)
            for i in range(3):
                act.sem_inc(s_st[i], 16)

            def body(tg, slot, i):
                for m in range(MT):
                    act.wait_ge(s_acc, tg * MT + (m + 1))
                    act.wait_ge(s_st[m % 3], tg * (16 * MT // 3) + 16 * (m // 3 + 1))
                    func = ACT.Copy if ATTN_W // P <= m < (ATTN_W + FOUR_W) // P else ACT.Silu
                    nc.scalar.activation(stage[m % 3][:], acc[m % 4][:], func).then_inc(s_free, 1)

            run(act, body)

        @block.tensor
        def _(pe):
            def body(tg, slot, i):
                pe.wait_ge(s_hh[slot], i * 32 + 32)
                for m in range(MT):
                    cols = slice(m * P, (m + 1) * P)
                    pe.wait_ge(s_wlo, m // 2 + 1)
                    pe.wait_ge(s_free, tg * MT + (m + 1))
                    for c in range(KD):
                        last = split_matmul(nc.tensor, acc[m % 4][:], w_hi[:, c, cols], w_lo[:, c, cols],
                                            hh[slot][:, c, :], hl[slot][:, c, :], c == 0, c == KD - 1)
                    last.then_inc(s_acc, 1)

            run(pe, body)


def fourier(nc, k, d):
    with ExitStack() as ctx:
        def sb(name, shape, dt=F32):
            return ctx.enter_context(nc.sbuf_tensor(name, shape, dt))

        def ps(name, shape):
            return ctx.enter_context(nc.psum_tensor(name, shape, F32))

        ORDER = (0, 2, 1, 3)
        PARTS = {0: ((0, 1),), 2: ((1, 1),), 1: ((2, 1), (3, 0)), 3: ((2, 1), (3, 2))}
        NTAB = 6
        u = sb("u", [P, GROUPS, RADIX, SUB])
        c_hi = sb("c_hi", [P, 2, GROUPS, SUB], F32R)
        c_lo = sb("c_lo", [P, 2, GROUPS, SUB], F32R)
        ab_hi = sb("ab_hi", [P, SUBT, GROUPS, 2 * P], F32R)
        ab_lo = sb("ab_lo", [P, SUBT, GROUPS, 2 * P], F32R)
        tab = [sb(f"tab{i}", [P, 2, 2, SUB], F32R) for i in range(NTAB)]
        wf = sb("wf", [P, GROUPS, P])
        chan = sb("chan", [P, 2, P])
        m_hi = sb("m_hi", [P, GROUPS, 4, P], F32R)
        m_lo = sb("m_lo", [P, GROUPS, 4, P], F32R)
        y = sb("y", [P, GROUPS, SUB, RADIX])
        ab_ps = [ps(f"ab_ps{i}", [P, 2, 2 * P]) for i in range(4)]
        dft_ps = [ps(f"dft_ps{i}", [P, SUB]) for i in range(GROUPS)]
        m_ps = dft_ps[0:2]
        y_flat = y[:].rearrange("p g n r -> p g (n r)")
        m_raw = y_flat[:, :, 0:4 * P].rearrange("p g (a c) -> p g a c", a=4)
        e = [y_flat[:, :, (i + 1) * SUB:(i + 2) * SUB] for i in range(2)]

        S = k.sem
        s_in, s_u = S("fourier_small_loaded"), S("u_loaded")
        s_tab = [S(f"table_loaded{i}") for i in range(NTAB)]
        s_tabfree = S("table_used")
        s_m, s_mraw, s_mhi, s_mlo = S("channel_product"), S("m_raw_ready"), S("m_hi_ready"), S("m_lo_ready")
        s_e, s_comb = S("first_sums"), S("position_sums")
        s_chi, s_clo = S("sum_hi_ready"), S("sum_lo_ready")
        s_ab, s_abhi, s_ablo = S("ab_product"), S("ab_hi_ready"), S("ab_lo_ready")
        s_yfree, s_yst = S("y_written"), S("y_stored")

        block = ctx.enter_context(nc.Block())

        @block.sync
        def _(sp):
            sp.dma_start(chan[:], d["chan"]).then_inc(s_in, 16)
            sp.dma_start(wf[:], d["w_f"][0].rearrange("g c n -> c g n")).then_inc(s_in, 16)
            sp.dma_start(u[:].rearrange("p g q n -> p g (q n)"),
                         k.rest_dram[ATTN_W // P:ATTN_W // P + GROUPS].rearrange("g p n -> p g n")).then_inc(s_u, 16)
            sp.wait_ge(s_yfree, RADIX * GROUPS)
            sp.dma_start(k.y_dram.rearrange("g p n -> p g n"), y[:].rearrange("p g n r -> p g (n r)")).then_inc(s_yst, 16)
            sp.wait_ge(s_yst, 16)

        @block.gpsimd
        def _(pool):
            for n in range(RADIX * SUBT):
                if n >= NTAB:
                    pool.wait_ge(s_tabfree, n - NTAB + 1)
                pool.dma_start(tab[n % NTAB][:], d["dft"][ORDER[n // SUBT], n % SUBT]).then_inc(s_tab[n % NTAB], 16)
            for i in range(NTAB):
                pool.wait_ge(s_tab[i], 16 * len(range(i, RADIX * SUBT, NTAB)))

        @block.scalar
        def _(act):
            act.wait_ge(s_m, 2)
            for part, (src, sign) in enumerate(((1, -1.0), (0, 1.0), (1, 1.0), (0, -1.0))):
                last = nc.scalar.activation(m_raw[:, :, part, :], m_ps[src][:].rearrange("p (g c) -> p g c", g=GROUPS),
                                            ACT.Copy, scale=sign)
            last.then_inc(s_mraw, 1)
            act.wait_ge(s_mraw, 1)
            nc.scalar.activation(m_hi[:], m_raw, ACT.Copy).then_inc(s_mhi, 1)

            def sum_hi(n):
                act.wait_ge(s_comb, n + 1)
                if n >= 2:
                    act.wait_ge(s_ab, 2 * SUBT * (n - 1))
                nc.scalar.activation(c_hi[:, n % 2], u[:, :, n, :], ACT.Copy).then_inc(s_chi, 1)

            sum_hi(0)
            sum_hi(1)
            for step, j in enumerate(ORDER):
                for n in range(2 * SUBT):
                    mt, gp = divmod(n, 2)
                    act.wait_ge(s_ab, 2 * SUBT * step + n + 1)
                    if step:
                        act.wait_ge(s_tabfree, step * SUBT)
                    nc.scalar.activation(ab_hi[:, mt, 2 * gp:2 * gp + 2, :], ab_ps[n % 4][:], ACT.Copy).then_inc(s_abhi, 1)
                if step < 2:
                    sum_hi(step + 2)
                act.wait_ge(s_tabfree, (step + 1) * SUBT)
                for g in range(GROUPS):
                    nc.scalar.activation(y[:, g, :, j], dft_ps[g][:], ACT.Copy).then_inc(s_yfree, 1)

        @block.vector
        def _(dve):
            dve.wait_ge(s_u, 16)
            q = [u[:, :, n, :] for n in range(RADIX)]
            nc.vector.tensor_tensor(e[0], q[0], q[2], ALU.add)
            nc.vector.tensor_tensor(e[1], q[1], q[3], ALU.add)
            nc.vector.tensor_tensor(q[2], q[0], q[2], ALU.subtract)
            nc.vector.tensor_tensor(q[3], q[1], q[3], ALU.subtract).then_inc(s_e, 1)
            dve.wait_ge(s_e, 1)
            nc.vector.tensor_tensor(q[0], e[0], e[1], ALU.add).then_inc(s_comb, 1)
            nc.vector.tensor_tensor(q[1], e[0], e[1], ALU.subtract).then_inc(s_comb, 3)
            dve.wait_ge(s_mhi, 1)
            nc.vector.tensor_tensor(m_lo[:], m_raw, m_hi[:].bitcast(F32), ALU.subtract).then_inc(s_mlo, 1)

            def sum_lo(n):
                dve.wait_ge(s_chi, n + 1)
                nc.vector.tensor_tensor(c_lo[:, n % 2], u[:, :, n, :], c_hi[:, n % 2].bitcast(F32),
                                        ALU.subtract).then_inc(s_clo, 1)

            sum_lo(0)
            sum_lo(1)
            for step in range(RADIX):
                for n in range(2 * SUBT):
                    mt, gp = divmod(n, 2)
                    dve.wait_ge(s_abhi, 2 * SUBT * step + n + 1)
                    hi = ab_hi[:, mt, 2 * gp:2 * gp + 2, :]
                    nc.vector.tensor_tensor(ab_lo[:, mt, 2 * gp:2 * gp + 2, :], ab_ps[n % 4][:], hi.bitcast(F32),
                                            ALU.subtract).then_inc(s_ablo, 1)
                if step < 2:
                    sum_lo(step + 2)

        @block.tensor
        def _(pe):
            pe.wait_ge(s_in, 32)
            for i in range(2):
                nc.tensor.matmul(m_ps[i][:], chan[:, i, :], wf[:].rearrange("p g c -> p (g c)"), start=True,
                                 stop=True).then_inc(s_m, 1)
            pe.wait_ge(s_mlo, 1)
            for step, j in enumerate(ORDER):
                pe.wait_ge(s_clo, (1, 2, 4, 4)[step])
                for n in range(2 * SUBT):
                    mt, gp = divmod(n, 2)
                    use = 2 * SUBT * step + n
                    if use >= 4:
                        pe.wait_ge(s_ablo, use - 3)
                    for gg in range(2):
                        g = 2 * gp + gg
                        for i, (src, part) in enumerate(PARTS[j]):
                            rows = (slice(None), src % 2, g, slice(mt * P, (mt + 1) * P))
                            last = split_matmul(nc.tensor, ab_ps[n % 4][:, gg, :], c_hi[rows], c_lo[rows],
                                                m_hi[:, g, part:part + 2, :].rearrange("p a c -> p (a c)"),
                                                m_lo[:, g, part:part + 2, :].rearrange("p a c -> p (a c)"),
                                                i == 0, i == len(PARTS[j]) - 1)
                    last.then_inc(s_ab, 1)
                if step:
                    pe.wait_ge(s_yfree, step * GROUPS)
                for mt in range(SUBT):
                    n = step * SUBT + mt
                    pe.wait_ge(s_ablo, 2 * SUBT * step + 2 * mt + 2)
                    pe.wait_ge(s_tab[n % NTAB], 16 * (n // NTAB + 1))
                    for g in range(GROUPS):
                        for cs in range(2):
                            a = (slice(None), mt, g, slice(cs * P, (cs + 1) * P))
                            last = split_matmul(nc.tensor, dft_ps[g][:], ab_hi[a], ab_lo[a], tab[n % NTAB][:, 0, cs, :],
                                                tab[n % NTAB][:, 1, cs, :], mt == 0 and cs == 0,
                                                mt == SUBT - 1 and cs == 1)
                    last.then_inc(s_tabfree, 1)


def output(nc, k, d):
    with ExitStack() as ctx:
        def sb(name, shape, dt=F32):
            return ctx.enter_context(nc.sbuf_tensor(name, shape, dt))

        TG = 2 * P
        N_TG = SEQ // TG
        AF = ATTN_W // P
        w_raw = sb("w_o_raw", [P, KD, D])
        w_hi = sb("w_o_hi", [P, KD, D], F32R)
        w_lo = sb("w_o_lo", [P, KD, D], F32R)
        den = sb("den_all", [P, NB * QB // P])
        yin = sb("yin", [P, KD, TG])
        gin = sb("gin", [P, KD, TG])
        inv = sb("inv", [P, AF, TG])
        y_hi = [sb(f"y_hi{i}", [P, KD, TG], F32R) for i in range(2)]
        y_lo = [sb(f"y_lo{i}", [P, KD, TG], F32R) for i in range(2)]
        x = [sb(f"x_res{i}", [P, D]) for i in range(2)]
        res = [sb(f"res{i}", [P, D]) for i in range(2)]
        square = sb("res_square", [P, 2, D], mybir.dt.bfloat16)
        stat = [sb(f"res_stat{i}", [P, 1]) for i in range(2)]
        mean = [sb(f"res_mean{i}", [P, 1]) for i in range(2)]
        rstd = [sb(f"res_rstd{i}", [P, 1]) for i in range(2)]
        minus_half = sb("out_minus_half", [P, 1])
        o_ps = [ctx.enter_context(nc.psum_tensor(f"o_ps{i}", [P, 2, 512], F32)) for i in range(2)]
        S = k.sem
        s_w, s_wg, s_whi, s_wlo = S("w_o_loaded"), S("w_o_gated"), S("w_o_hi_ready"), S("w_o_lo_ready")
        s_den, s_dinv, s_dst = S("den_loaded"), S("den_inverted"), S("den_inv_stored")
        s_in, s_norm, s_y, s_yhi, s_ylo = (S("y_in_loaded"), S("att_normed"), S("y_gated"), S("y_hi_ready"),
                                           S("y_lo_ready"))
        s_x = [S("x_res_loaded0"), S("x_res_loaded1")]
        s_o, s_add, s_sum, s_mean, s_rstd, s_out = (S("out_projected"), S("residual_added"), S("res_squares"),
                                                    S("res_mean_ready"), S("res_rstd_ready"), S("out_ready"))
        s_half = S("out_minus_half_set")
        s_st = [S("out_stored0"), S("out_stored1")]
        att_v = k.att_dram.rearrange("(f e b) c q -> b e c f q", e=2, b=NQB)
        inv_v = k.inv_dram.rearrange("(f e b) q -> b e f q", e=2, b=NQB)
        x_v = d["x"][0].rearrange("(t p) n -> t p n", p=P)
        out_v = d["out"][0].rearrange("(t p) n -> t p n", p=P)

        N_IT = N_TG // 2

        def run(engine, body):
            with engine.Fori(0, N_IT - 1) as i:
                body(i * 2, 0, i, False)
                body(i * 2 + 1, 1, i, False)
            body(N_TG - 2, 0, N_IT - 1, False)
            body(N_TG - 1, 1, N_IT - 1, True)

        block = ctx.enter_context(nc.Block())
        LOADS = 2 + 2 + 2 + 1

        @block.sync
        def _(sp):
            def load_group(slot, i):
                cols = slice(slot * TG, (slot + 1) * TG)
                tok = bass.ds(i * QB + slot * TG, TG)
                for e in range(2):
                    rows = slice(e * HD, (e + 1) * HD)
                    sp.dma_start(yin[rows, 0:AF, :], att_v[i][e][:, :, cols]).then_inc(s_in, 16)
                    sp.dma_start(inv[rows, :, :], inv_v[i][e][:, cols].partition_broadcast(HD)).then_inc(s_in, 16)
                sp.dma_start(yin[:, AF:, :], k.y_dram[:, :, tok].rearrange("m p t -> p m t")).then_inc(s_in, 16)
                sp.dma_start(gin[:, 0:AF, :], k.rest_dram[0:AF, :, tok].rearrange("m p t -> p m t")).then_inc(s_in, 16)
                sp.dma_start(gin[:, AF:, :], k.rest_dram[2 * AF:3 * AF, :, tok].rearrange("m p t -> p m t")).then_inc(s_in, 16)

            sp.dma_start(den[:], k.den_dram.rearrange("b (a q) -> (b a) q", q=P)).then_inc(s_den, 16)
            sp.dma_start(w_raw[:], d["w_o"][0].rearrange("(k p) n -> p k n", p=P)).then_inc(s_w, 16)
            sp.wait_ge(s_dinv, 1)
            sp.dma_start(k.inv_dram.rearrange("b (a q) -> (b a) q", q=P), den[:]).then_inc(s_dst, 16)
            sp.wait_ge(s_dst, 16)
            load_group(0, 0)

            def body(g, slot, i, last):
                for e in range(2):
                    t = g * 2 + e
                    sp.wait_ge(s_add, t + 1)
                    sp.dma_start(x[e][:], x_v[t]).then_inc(s_x[e], 16)
                if not last:
                    sp.wait_ge(s_ylo, g + 1)
                    sp.wait_ge(s_yhi, g + 1)
                    load_group(1 - slot, i + slot)
                for e in range(2):
                    t = g * 2 + e
                    sp.wait_ge(s_out, t + 1)
                    sp.dma_start(out_v[t], res[e][:]).then_inc(s_st[e], 16)

            run(sp, body)
            for e in range(2):
                sp.wait_ge(s_st[e], 16 * (N_TG + 1))

        @block.gpsimd
        def _(pool):
            nc.gpsimd.memset(minus_half[:], -0.5).then_inc(s_half, 1)
            pool.wait_ge(s_half, 1)

            def body(g, slot, i, last):
                for e in range(2):
                    pool.wait_ge(s_mean, g * 2 + (e + 1))
                    nc.gpsimd.tensor_tensor(rstd[e][:], mean[e][:], minus_half[:], ALU.pow).then_inc(s_rstd, 1)

            run(pool, body)

        @block.scalar
        def _(act):
            act.sem_inc(s_st[0], 16)
            act.sem_inc(s_st[1], 16)
            act.wait_ge(s_wg, 1)
            nc.scalar.activation(w_hi[:], w_raw[:], ACT.Copy).then_inc(s_whi, 1)

            def prepare(g, slot, first=False):
                act.wait_ge(s_y, g + 1)
                if not first:
                    act.wait_ge(s_o, g * 2)
                nc.scalar.activation(y_hi[slot][:], yin[:], ACT.Copy).then_inc(s_yhi, 1)

            prepare(0, 0, True)

            def body(g, slot, i, last):
                if not last:
                    prepare(g + 1, 1 - slot)
                for e in range(2):
                    act.wait_ge(s_add, g * 2 + (e + 3))
                    nc.scalar.activation(square[:, e, :], res[e][:], ACT.Square, accum_out=stat[e][:]).then_inc(s_sum, 1)

            run(act, body)

        @block.vector
        def _(dve):
            dve.sem_inc(s_add, 2)
            dve.wait_ge(s_den, 16)
            nc.vector.reciprocal(den[:], den[:]).then_inc(s_dinv, 1)
            dve.wait_ge(s_w, 16)
            for c in range(KD):
                last = nc.vector.tensor_tensor(w_raw[:, c, :], w_raw[:, c, :], k.gate_bc[:], ALU.mult)
            last.then_inc(s_wg, 1)
            dve.wait_ge(s_whi, 1)
            nc.vector.tensor_tensor(w_lo[:], w_raw[:], w_hi[:].bitcast(F32), ALU.subtract).then_inc(s_wlo, 1)

            def prepare(g, slot):
                dve.wait_ge(s_in, g * (16 * LOADS) + 16 * LOADS)
                nc.vector.tensor_tensor(yin[:, 0:AF, :], yin[:, 0:AF, :], inv[:], ALU.mult).then_inc(s_norm, 1)
                dve.wait_ge(s_norm, g + 1)
                nc.vector.tensor_tensor(yin[:], yin[:], gin[:], ALU.mult).then_inc(s_y, 1)
                dve.wait_ge(s_yhi, g + 1)
                nc.vector.tensor_tensor(y_lo[slot][:], yin[:], y_hi[slot][:].bitcast(F32), ALU.subtract).then_inc(s_ylo, 1)

            prepare(0, 0)

            def body(g, slot, i, last):
                if not last:
                    prepare(g + 1, 1 - slot)
                for e in range(2):
                    t = g * 2 + e
                    dve.wait_ge(s_o, t + 3)
                    dve.wait_ge(s_x[e], g * 16 + 16)
                    dve.wait_ge(s_st[e], g * 16 + 16)
                    nc.vector.tensor_tensor(res[e][:], o_ps[e][:].rearrange("p a n -> p (a n)"), x[e][:],
                                            ALU.add).then_inc(s_add, 1)
                    dve.wait_ge(s_sum, t + 1)
                    nc.vector.tensor_scalar(mean[e][:], stat[e][:], 1.0 / D, EPS, ALU.mult, ALU.add).then_inc(s_mean, 1)
                    dve.wait_ge(s_rstd, t + 1)
                    nc.vector.scalar_tensor_tensor(res[e][:], res[e][:], rstd[e][:], k.final_bc[:], ALU.mult,
                                                   ALU.mult).then_inc(s_out, 1)

            run(dve, body)

        @block.tensor
        def _(pe):
            pe.sem_inc(s_o, 2)
            pe.wait_ge(s_wlo, 1)

            def body(g, slot, i, last):
                pe.wait_ge(s_ylo, g + 1)
                for e in range(2):
                    t = g * 2 + e
                    pe.wait_ge(s_add, t + 1)
                    toks = slice(e * P, (e + 1) * P)
                    for n in range(2):
                        cols = slice(n * 512, (n + 1) * 512)
                        for c in range(KD):
                            last_mm = split_matmul(nc.tensor, o_ps[e][:, n, :], y_hi[slot][:, c, toks],
                                                   y_lo[slot][:, c, toks], w_hi[:, c, cols], w_lo[:, c, cols],
                                                   c == 0, c == KD - 1)
                    last_mm.then_inc(s_o, 1)

            run(pe, body)


class Shared:
    pass


def build(nc, d):
    with ExitStack() as ctx:
        def sb(name, shape, dt=F32):
            return ctx.enter_context(nc.sbuf_tensor(name, shape, dt))

        def dram(name, shape):
            return nc.dram_tensor(name, shape, F32, kind="Internal").ap()

        k = Shared()
        k.sem = lambda name: ctx.enter_context(nc.semaphore(name))
        k.h_dram = dram("h_scratch", (2, KD, P, SEQ))
        k.q_dram = dram("q_scratch", (NB, P, QB))
        k.att_dram = dram("att_scratch", (NB, HD, QB))
        k.den_dram = dram("den_scratch", (NB, QB))
        k.inv_dram = dram("inv_scratch", (NB, QB))
        k.rest_dram = dram("rest_scratch", (MT, P, SEQ))
        k.y_dram = dram("y_scratch", (GROUPS, P, SEQ))
        k.ident = sb("ident_sb", [P, P])
        k.gate_bc = sb("gate_bc", [P, D])
        k.final_bc = sb("final_bc", [P, D])
        with ExitStack() as inner:
            def sbi(name, shape, dt=F32):
                return inner.enter_context(nc.sbuf_tensor(name, shape, dt))

            k.ones_sq = sbi("ones_sq", [P, P], F32R)
            k.zero_one = sbi("zero_one", [P, P], F32R)
            k.k_hi2 = sbi("k_hi2", [P, HKV, KEYS], F32R)
            k.k_lo1 = sbi("k_lo1", [P, HKV, KEYS], F32R)
            k.v_hl = sbi("v_hl", [P, KT, HKV, P], F32R)
            with ExitStack() as first:
                k.scale = first.enter_context(nc.sbuf_tensor("scale", [P, 2, KD], F32))
                k.shift = first.enter_context(nc.sbuf_tensor("shift", [P, 2, KD], F32))
                k.head_bc = first.enter_context(nc.sbuf_tensor("head_bc", [P, HN * HD], F32))
                k.wqkv_hi = first.enter_context(nc.sbuf_tensor("wqkv_hi", [P, KD, QKV_W], F32R))
                k.wqkv_lo = first.enter_context(nc.sbuf_tensor("wqkv_lo", [P, KD, QKV_W], F32R))
                modulation(nc, k, d)
                project_qkv(nc, k, d)
            attention(nc, k, d)
        project_gates(nc, k, d)
        fourier(nc, k, d)
        output(nc, k, d)


def constants():
    import numpy as np
    grid_w, theta, freqs = 64, 10000.0, HD // 4
    pos = np.arange(SEQ)
    inv = np.float32(theta) ** (-np.arange(freqs, dtype=np.float32) / np.float32(freqs))
    ang = np.stack([(pos // grid_w).astype(np.float32)[:, None] * inv,
                    (pos % grid_w).astype(np.float32)[:, None] * inv], axis=1)
    ang = np.repeat(ang[:, :, None, :], 2, axis=2).reshape(SEQ, HD)
    c = np.arange(P)
    chan_ang = 2 * np.pi * np.outer(c, c) / P
    norm = 1.0 / np.sqrt(float(SEQ) * P)
    chan = np.stack([np.cos(chan_ang), np.sin(chan_ang)], axis=1) * norm
    j, m, n = np.arange(RADIX)[:, None, None], np.arange(SUB)[None, :, None], np.arange(SUB)[None, None, :]
    dft_ang = 2 * np.pi * (((RADIX * n + j) * m) % SEQ) / SEQ
    dft = np.stack([np.cos(dft_ang), -np.sin(dft_ang)], axis=2).astype(np.float32)
    bits = dft.view(np.uint32)
    hi = (((bits + np.uint32(0x7FF) + ((bits >> np.uint32(12)) & np.uint32(1))) >> np.uint32(12)) << np.uint32(12))
    hi = hi.view(np.float32)
    dft = np.stack([hi, dft - hi], axis=2).reshape(RADIX, SUBT, P, 2, 2, SUB)
    return {"ident": np.eye(P, dtype=np.float32), "cos": np.cos(ang).astype(np.float32),
            "sin": np.sin(ang).astype(np.float32), "chan": chan.astype(np.float32),
            "dft": np.ascontiguousarray(dft)}


_INS = ["x", "c", "ctx", "c_ctx", "norm_g", "w_mod", "b_mod", "w_in", "q_g", "k_g", "w_f", "w_o", "final_g"]


def kernel(**inputs):
    import numpy as np
    import concourse.bacc as bacc
    from concourse.bass_utils import run_bass_kernel_spmd as launch

    nc = bacc.Bacc("TRN2", target_bir_lowering=False, num_devices=1)
    arrays = {name: np.ascontiguousarray(inputs[name]) for name in _INS}
    arrays.update(constants())
    d = {}
    feeds = {}
    for name, a in arrays.items():
        feeds[f"in_{name}"] = a
        d[name] = nc.dram_tensor(f"in_{name}", a.shape, mybir.dt.from_np(a.dtype), kind="ExternalInput").ap()
    d["out"] = nc.dram_tensor("out_x", (1, SEQ, D), F32, kind="ExternalOutput").ap()
    build(nc, d)
    r = launch(nc, [feeds], core_ids=[0])
    return r.results[0]["out_x"]
```

```python
import concourse.bass as bass
from concourse import mybir
from contextlib import ExitStack

F32 = mybir.dt.float32
F32R = mybir.dt.float32r
ALU = mybir.AluOpType
ACT = mybir.ActivationFunctionType
X_AXIS = mybir.AxisListType.X

P = 128
D = 1024
KD = D // P
SEQ = 2048
CTX = 256
TT = SEQ // P
KEYS = SEQ + CTX
KT = KEYS // P
HD = 64
HQ = 8
HKV = 2
HN = HQ + HKV
ATTN_W = HQ * HD
KV_W = HKV * HD
QKV_W = ATTN_W + 2 * KV_W
GA0 = QKV_W
F0 = GA0 + ATTN_W
FOUR_W = 512
GF0 = F0 + FOUR_W
GROUPS = 4
REST_W = ATTN_W + 2 * FOUR_W
MT = REST_W // P
QB = 512
NQB = SEQ // QB
NB = HQ * NQB
EPS = 1e-6
RADIX = 4
SUB = SEQ // RADIX
SUBT = SUB // P
CH = 2 * P
NCH = REST_W // CH
M_ORDER = (4, 5, 6, 7, 0, 1, 2, 3, 8, 9, 10, 11)
C_ORDER = tuple(m // 2 for m in M_ORDER[::2])


def split_matmul(pe, out, lhs_hi, lhs_lo, rhs_hi, rhs_lo, first, last):
    pe.matmul(out, lhs_hi, rhs_hi, start=first, stop=False)
    pe.matmul(out, lhs_hi, rhs_lo, start=False, stop=False)
    return pe.matmul(out, lhs_lo, rhs_hi, start=False, stop=last)


def modulation(nc, k, d):
    with ExitStack() as ctx:
        def sb(name, shape, dt=F32):
            return ctx.enter_context(nc.sbuf_tensor(name, shape, dt))

        w_mod = [sb(f"w_mod{g}", [P, KD, D]) for g in range(2)]
        cond = sb("cond", [P, 2, KD])
        cond_act = sb("cond_act", [P, KD, 2])
        cond_rep = sb("cond_rep", [P, KD, P])
        mod_bias = sb("mod_bias", [P, 2, KD])
        norm_col = sb("norm_col", [P, KD])
        gate_bias = sb("gate_bias", [1, D])
        final_row = sb("final_row", [1, D])
        head_row = sb("head_row", [1, HN, HD])
        ones_row = sb("ones_row", [1, P])
        w_raw = w_mod[1][:, :, 0:QKV_W]
        col_ps = ctx.enter_context(nc.psum_tensor("col_ps", [P, 2, KD, 2], F32))
        row_ps = [ctx.enter_context(nc.psum_tensor(f"row_ps{i}", [P, 512], F32)) for i in range(6)]
        S = k.sem
        s_mod = [S("w_mod0_loaded"), S("w_mod1_loaded")]
        s_small, s_wqkv, s_whi = S("small_loaded"), S("wqkv_loaded"), S("wqkv_hi_loaded")
        s_cond, s_rep, s_ones = S("cond_ready"), S("cond_rep_ready"), S("ones_ready")
        s_cols, s_rows, s_gate_ps = S("mod_cols_done"), S("rows_done"), S("gate_rows_done")
        s_scale, s_gated, s_end = S("scale_biased"), S("shift_ready"), S("modulation_copied")
        s_hrow = S("head_row_ready")
        w_mod_v = d["w_mod"][0].rearrange("(k p) (g n) -> g p k n", p=P, g=3)
        b_mod_v = d["b_mod"][0].rearrange("(g k p) -> p g k", p=P, g=3)
        w_qkv_v = d["w_in"][0][:, 0:QKV_W].rearrange("(k p) n -> p k n", p=P)

        block = ctx.enter_context(nc.Block())

        @block.sync
        def _(sp):
            with nc.allow_non_contiguous_dma(reason="small vectors laid out one element per partition"):
                sp.dma_start(cond[:, 0, :], d["c"][0].rearrange("(k p) -> p k", p=P)).then_inc(s_small, 16)
                sp.dma_start(cond[:, 1, :], d["c_ctx"].rearrange("(k p) -> p k", p=P)).then_inc(s_small, 16)
                sp.dma_start(w_mod[0][:], w_mod_v[0]).then_inc(s_mod[0], 16)
                sp.dma_start(w_mod[1][:], w_mod_v[1]).then_inc(s_mod[1], 16)
                for g in range(2):
                    sp.dma_start(mod_bias[:, g, :], b_mod_v[:, g, :]).then_inc(s_small, 16)
                sp.dma_start(norm_col[:], d["norm_g"][0].rearrange("(k p) -> p k", p=P)).then_inc(s_small, 16)
            sp.dma_start(gate_bias[:], d["b_mod"][0:1, 2 * D:3 * D]).then_inc(s_small, 16)
            sp.dma_start(final_row[:], d["final_g"].rearrange("(a n) -> a n", a=1)).then_inc(s_small, 16)
            for h in range(HN):
                sp.dma_start(head_row[:, h, :], (d["q_g"] if h < HQ else d["k_g"])[0:1, :]).then_inc(s_small, 16)
            sp.dma_start(k.ident[:], d["ident"]).then_inc(s_small, 16)
            sp.wait_ge(s_cols, 1)
            sp.dma_start(w_mod[0][:], w_mod_v[2]).then_inc(s_mod[0], 16)
            sp.wait_ge(s_cols, 2)
            sp.dma_start(w_raw, w_qkv_v).then_inc(s_wqkv, 16)

        small = 16 * (2 + 2 + 1 + 2 + HN + 1)

        @block.gpsimd
        def _(pool):
            pool.dma_start(k.wqkv_hi[:], w_qkv_v).then_inc(s_whi, 16)
            pool.wait_ge(s_whi, 16)

        @block.scalar
        def _(act):
            act.wait_ge(s_small, small)
            nc.scalar.activation(cond_act[:].rearrange("p k c -> p c k"), cond[:], ACT.Silu).then_inc(s_cond, 1)
            act.wait_ge(s_cond, 1)
            nc.scalar.activation(cond_rep[:], cond_act[:, :, 0:1].broadcast_to([P, KD, P]),
                                 ACT.Copy).then_inc(s_rep, 1)
            act.wait_ge(s_rows, 4)
            for i in range(2):
                nc.scalar.activation(k.final_bc[:, i * 512:(i + 1) * 512], row_ps[i][:], ACT.Copy)
            nc.scalar.activation(k.head_bc[:, 0:ATTN_W], row_ps[2][:], ACT.Copy)
            nc.scalar.activation(k.head_bc[:, ATTN_W:HN * HD], row_ps[3][:, 0:KV_W], ACT.Copy).then_inc(s_end, 1)
            act.wait_ge(s_gate_ps, 2)
            for i in range(2):
                last = nc.scalar.activation(k.gate_bc[:, i * 512:(i + 1) * 512], row_ps[4 + i][:], ACT.Copy)
            last.then_inc(s_end, 1)
            act.wait_ge(s_end, 2)

        @block.vector
        def _(dve):
            nc.vector.memset(ones_row[:], 1.0).then_inc(s_ones, 1)
            nc.vector.memset(k.ones_sq[:].bitcast(F32), 1.0)
            nc.vector.memset(k.zero_one[:, 0:HD].bitcast(F32), 0.0)
            nc.vector.memset(k.zero_one[:, HD:P].bitcast(F32), 1.0)
            nc.vector.memset(k.k_lo1[HD:HD + 1, :, :].bitcast(F32), 1.0)
            dve.wait_ge(s_small, small)
            nc.vector.tensor_scalar(head_row[:, 0:HQ, :], head_row[:, 0:HQ, :], HD ** -0.5, None,
                                    ALU.mult).then_inc(s_hrow, 1)
            dve.wait_ge(s_cols, 2)
            for side in range(2):
                nc.vector.tensor_tensor(k.shift[:, side, :], col_ps[:, 0, :, side], mod_bias[:, 0, :], ALU.add)
                last = nc.vector.tensor_tensor(k.scale[:, side, :], col_ps[:, 1, :, side], mod_bias[:, 1, :],
                                               ALU.add)
            last.then_inc(s_scale, 1)
            dve.wait_ge(s_scale, 1)
            for side in range(2):
                last = nc.vector.scalar_tensor_tensor(k.scale[:, side, :], k.scale[:, side, :], 1.0, norm_col[:],
                                                      ALU.add, ALU.mult)
            last.then_inc(s_gated, 1)
            dve.wait_ge(s_wqkv, 16)
            dve.wait_ge(s_whi, 16)
            nc.vector.tensor_tensor(k.wqkv_lo[:], w_raw, k.wqkv_hi[:].bitcast(F32), ALU.subtract).then_inc(s_gated, 1)
            dve.wait_ge(s_gated, 2)

        @block.tensor
        def _(pe):
            pe.wait_ge(s_ones, 1)
            pe.wait_ge(s_small, small)
            pe.wait_ge(s_hrow, 1)
            head_flat = head_row[:].rearrange("a h d -> a (h d)")
            for i in range(2):
                nc.tensor.matmul(row_ps[i][:], ones_row[:], final_row[:, i * 512:(i + 1) * 512],
                                 start=True, stop=True).then_inc(s_rows, 1)
            nc.tensor.matmul(row_ps[2][:], ones_row[:], head_flat[:, 0:ATTN_W], start=True, stop=True).then_inc(s_rows, 1)
            nc.tensor.matmul(row_ps[3][:, 0:KV_W], ones_row[:], head_flat[:, ATTN_W:HN * HD],
                             start=True, stop=True).then_inc(s_rows, 1)
            pe.wait_ge(s_cond, 1)
            for g in range(2):
                pe.wait_ge(s_mod[g], 16)
                for f in range(KD):
                    for c in range(KD):
                        last = nc.tensor.matmul(col_ps[:, g, f, :], w_mod[g][:, c, f * P:(f + 1) * P],
                                                cond_act[:, c, :], start=(c == 0), stop=(c == KD - 1))
                last.then_inc(s_cols, 1)
            pe.wait_ge(s_rep, 1)
            pe.wait_ge(s_mod[0], 32)
            for i in range(2):
                nc.tensor.matmul(row_ps[4 + i][:], ones_row[:], gate_bias[:, i * 512:(i + 1) * 512],
                                 start=True, stop=False)
                for c in range(KD):
                    last = nc.tensor.matmul(row_ps[4 + i][:], cond_rep[:, c, :], w_mod[0][:, c, i * 512:(i + 1) * 512],
                                            start=False, stop=(c == KD - 1))
                last.then_inc(s_gate_ps, 1)


def project_qkv(nc, k, d):
    with ExitStack() as ctx:
        def sb(name, shape, dt=F32):
            return ctx.enter_context(nc.sbuf_tensor(name, shape, dt))

        def ps(name, shape):
            return ctx.enter_context(nc.psum_tensor(name, shape, F32))

        W = 2 * P
        x = [sb(f"x{i}", [P, 2, D]) for i in range(2)]
        h = sb("h", [P, KD, W])
        h_hi = [sb(f"h_hi{i}", [P, KD, W], F32R) for i in range(2)]
        h_lo = [sb(f"h_lo{i}", [P, KD, W], F32R) for i in range(2)]
        square = sb("square", [P, 2, D], mybir.dt.bfloat16)
        stat = [sb(f"stat{i}", [P, 2]) for i in range(2)]
        stat_eps = [sb(f"stat_eps{i}", [P, 2]) for i in range(2)]
        rstd = [sb(f"rstd{i}", [P, 2]) for i in range(2)]
        minus_half = sb("minus_half", [P, HN])
        qkv = [sb(f"qkv{i}", [P, QKV_W]) for i in range(2)]
        qk_sq = sb("qk_sq", [P, HN, HD])
        qk_g = sb("qk_g", [P, HN, HD])
        qk_n = sb("qk_n", [P, HN, HD])
        qk_sin = sb("qk_sin", [P, HN, HD])
        qk_rot = sb("qk_rot", [P, HN, 2, HD])
        hstat = sb("hstat", [P, HN])
        hrstd = sb("hrstd", [P, HN])
        cos_t = [sb(f"cos{i}", [P, 2, HD]) for i in range(2)]
        sin_t = [sb(f"sin{i}", [P, 2, HD]) for i in range(2)]
        q_hilo = [sb(f"q_hilo{i}", [P, HQ, P], F32R) for i in range(2)]
        xt_ps = [ps(f"xt_ps{i}", [P, 2, W]) for i in range(2)]
        q_ps = ps("q_ps", [P, ATTN_W])
        kv_ps = ps("kv_ps", [P, 2 * KV_W])
        tr_ps = [ps(f"tr_ps{i}", [P, 4, P]) for i in range(3)]

        S = k.sem
        s_x = [S("x_loaded0"), S("x_loaded1")]
        s_table = [S("rope_loaded0"), S("rope_loaded1")]
        s_const = S("minus_half_set")
        s_sum, s_eps, s_rstd, s_xhat = S("x_square_sums"), S("x_eps_added"), S("x_rstd_ready"), S("x_normed")
        s_xt, s_h, s_hhi, s_hsplit = S("x_transposed"), S("h_ready"), S("h_hi_ready"), S("h_split")
        s_qp, s_kvp, s_qc, s_kvc = S("q_projected"), S("kv_projected"), S("q_copied"), S("kv_copied")
        s_sq, s_hsum, s_hmean, s_hrstd = S("head_squares"), S("head_sums"), S("head_means"), S("head_rstd_ready")
        s_g, s_n, s_c, s_r, s_dup = (S("head_gained"), S("head_normed"), S("rope_multiplied"), S("head_rotated"),
                                     S("head_doubled"))
        s_tr, s_trhi, s_trlo = S("qk_transposed"), S("qk_hi_ready"), S("qk_lo_ready")
        s_vhi, s_v = S("v_hi_ready"), S("v_ready")
        s_qst = [S("q_stored0"), S("q_stored1")]
        s_hst = [S("h_stored0"), S("h_stored1")]
        x_v = d["x"][0].rearrange("(s t p) n -> s p t n", t=2, p=P)
        ctx_v = d["ctx"][0].rearrange("(t p) n -> p t n", p=P)
        cos_v = d["cos"].rearrange("(s t p) n -> s p t n", t=2, p=P)
        sin_v = d["sin"].rearrange("(s t p) n -> s p t n", t=2, p=P)
        q_v = k.q_dram.rearrange("(h b) p q -> b p h q", b=NQB)
        h_v = k.h_dram.rearrange("e k p (s t) -> s e p k t", t=W)
        N_IT = TT // 4

        def run(engine, body):
            with engine.Fori(0, N_IT - 1) as i:
                body(i, False)
            body(N_IT - 1, True)

        def heads(is_ctx):
            return (HQ, HN) if is_ctx else (0, HN)

        block = ctx.enter_context(nc.Block())

        @block.sync
        def _(sp):
            def load_x(p, slot):
                sp.dma_start(x[slot][:], x_v[p]).then_inc(s_x[slot], 16)

            def load_tables(p, slot):
                sp.dma_start(cos_t[slot][:], cos_v[p]).then_inc(s_table[slot], 16)
                sp.dma_start(sin_t[slot][:], sin_v[p]).then_inc(s_table[slot], 16)

            def store_h(s, slot, p):
                sp.wait_ge(s_hsplit, s + 1)
                sp.dma_start(h_v[p][0], h_hi[slot][:].bitcast(F32)).then_inc(s_hst[slot], 16)
                sp.dma_start(h_v[p][1], h_lo[slot][:].bitcast(F32)).then_inc(s_hst[slot], 16)

            def store_q(t, slot, i, tau):
                sp.wait_ge(s_trlo, t + 1)
                sp.dma_start(q_v[i][:, :, tau * P:(tau + 1) * P], q_hilo[slot][:].bitcast(F32)).then_inc(s_qst[slot], 16)

            sp.dma_start(x[0][:], ctx_v).then_inc(s_x[0], 16)
            load_x(0, 1)
            load_tables(0, 1)
            sp.wait_ge(s_xt, 4)
            load_x(1, 0)

            def body(i, last):
                if not last:
                    sp.wait_ge(s_xt, 4 * (i * 2 + 2))
                    load_x(i * 2 + 2, 1)
                sp.wait_ge(s_c, 4 * i + 2)
                load_tables(i * 2 + 1, 0)
                store_h(i * 2 + 1, 1, i * 2)
                store_q(4 * i + 2, 0, i, 0)
                store_h(i * 2 + 2, 0, i * 2 + 1)
                if not last:
                    sp.wait_ge(s_xt, 4 * (i * 2 + 3))
                    load_x(i * 2 + 3, 0)
                    sp.wait_ge(s_c, 4 * i + 4)
                    load_tables(i * 2 + 2, 1)
                for tau in range(1, 4):
                    store_q(4 * i + (2 + tau), tau % 2, i, tau)

            run(sp, body)
            for slot in range(2):
                sp.wait_ge(s_qst[slot], 16 * (TT // 2 + 1))
                sp.wait_ge(s_hst[slot], 32 * (TT // 4 + 1))

        @block.gpsimd
        def _(pool):
            nc.gpsimd.memset(minus_half[:], -0.5).then_inc(s_const, 1)
            pool.wait_ge(s_const, 1)

            def x_rstd(s, slot):
                pool.wait_ge(s_eps, s + 1)
                nc.gpsimd.tensor_tensor(rstd[slot][:], stat_eps[slot][:], minus_half[:, 0:2], ALU.pow).then_inc(s_rstd, 1)

            def head_gain(t, slot, is_ctx=False):
                h0, h1 = heads(is_ctx)
                pool.wait_ge(s_qc, t + 1)
                pool.wait_ge(s_kvc, t + 1)
                if not is_ctx or t:
                    pool.wait_ge(s_n, t)
                nc.gpsimd.tensor_tensor(qk_g[:, h0:h1, :].rearrange("p h d -> p (h d)"),
                                        qkv[slot][:, h0 * HD:h1 * HD], k.head_bc[:, h0 * HD:h1 * HD],
                                        ALU.mult).then_inc(s_g, 1)
                pool.wait_ge(s_hmean, t + 1)
                nc.gpsimd.tensor_tensor(hrstd[:, h0:h1], hstat[:, h0:h1], minus_half[:, h0:h1],
                                        ALU.pow).then_inc(s_hrstd, 1)

            x_rstd(0, 0)
            x_rstd(1, 1)
            head_gain(0, 0, True)
            head_gain(1, 1, True)
            x_rstd(2, 0)

            def body(i, last):
                head_gain(4 * i + 2, 0)
                if not last:
                    x_rstd(i * 2 + 3, 1)
                head_gain(4 * i + 3, 1)
                head_gain(4 * i + 4, 0)
                head_gain(4 * i + 5, 1)
                if not last:
                    x_rstd(i * 2 + 4, 0)

            run(pool, body)

        @block.scalar
        def _(act):
            act.sem_inc(s_qst[0], 16)
            act.sem_inc(s_qst[1], 16)
            act.sem_inc(s_h, 2)

            def x_squares(s, slot, loads):
                act.wait_ge(s_x[slot], 16 * loads)
                nc.scalar.activation(square[:, 0, :], x[slot][:, 0, :], ACT.Square, accum_out=stat[slot][:, 0:1])
                nc.scalar.activation(square[:, 1, :], x[slot][:, 1, :], ACT.Square,
                                     accum_out=stat[slot][:, 1:2]).then_inc(s_sum, 1)

            def h_evacuate(s, side):
                if side == 0:
                    act.wait_ge(s_hsplit, s)
                for u in range(4):
                    act.wait_ge(s_xt, 4 * s + (u + 1))
                    for e in range(2):
                        f = 2 * u + e
                        last = nc.scalar.activation(h[:, f, :], xt_ps[u % 2][:, e, :], ACT.Identity,
                                                    scale=k.scale[:, side, f:f + 1], bias=k.shift[:, side, f:f + 1])
                    last.then_inc(s_h, 1)

            def copy_qkv(t, slot, is_ctx=False):
                h0, h1 = heads(is_ctx)
                if not is_ctx:
                    act.wait_ge(s_g, t - 1)
                    act.wait_ge(s_v, t - 1)
                    act.wait_ge(s_qp, t + 1)
                    nc.scalar.activation(qkv[slot][:, 0:ATTN_W], q_ps[:], ACT.Copy).then_inc(s_qc, 1)
                else:
                    act.sem_inc(s_qc, 1)
                act.wait_ge(s_kvp, t + 1)
                nc.scalar.activation(qkv[slot][:, ATTN_W:QKV_W], kv_ps[:], ACT.Copy).then_inc(s_kvc, 1)
                act.wait_ge(s_kvc, t + 1)
                if not is_ctx:
                    act.wait_ge(s_qc, t + 1)
                if not is_ctx or t:
                    act.wait_ge(s_hsum, t)
                nc.scalar.activation(qk_sq[:, h0:h1, :].rearrange("p h d -> p (h d)"),
                                     qkv[slot][:, h0 * HD:h1 * HD], ACT.Square).then_inc(s_sq, 1)

            def double_heads(t, is_ctx=False):
                h0, h1 = heads(is_ctx)
                act.wait_ge(s_r, t + 1)
                nc.scalar.activation(qk_rot[:, h0:h1, 1, :], qk_rot[:, h0:h1, 0, :], ACT.Copy).then_inc(s_dup, 1)

            def qk_hi(t, slot, key0, uses=None):
                act.wait_ge(s_tr, t + 1)
                if uses is not None:
                    act.wait_ge(s_qst[slot], 16 * uses)
                    nc.scalar.activation(q_hilo[slot][:, 0:4, :], tr_ps[0][:], ACT.Copy)
                    nc.scalar.activation(q_hilo[slot][:, 4:8, :], tr_ps[1][:], ACT.Copy)
                nc.scalar.activation(k.k_hi2[:, :, bass.ds(key0, P)], tr_ps[2][:, 0:HKV, :],
                                     ACT.Copy).then_inc(s_trhi, 1)

            x_squares(0, 0, 1)
            h_evacuate(0, 1)
            x_squares(1, 1, 1)
            h_evacuate(1, 0)
            copy_qkv(0, 0, True)
            double_heads(0, True)
            qk_hi(0, 0, SEQ)
            copy_qkv(1, 1, True)
            double_heads(1, True)
            qk_hi(1, 1, SEQ + P)
            x_squares(2, 0, 2)

            def body(i, last):
                h_evacuate(i * 2 + 2, 0)
                copy_qkv(4 * i + 2, 0)
                if not last:
                    x_squares(i * 2 + 3, 1, i + 2)
                double_heads(4 * i + 2)
                copy_qkv(4 * i + 3, 1)
                qk_hi(4 * i + 2, 0, i * (4 * P), 2 * i + 1)
                if not last:
                    h_evacuate(i * 2 + 3, 0)
                double_heads(4 * i + 3)
                copy_qkv(4 * i + 4, 0)
                qk_hi(4 * i + 3, 1, i * (4 * P) + P, 2 * i + 1)
                double_heads(4 * i + 4)
                copy_qkv(4 * i + 5, 1)
                qk_hi(4 * i + 4, 0, i * (4 * P) + 2 * P, 2 * i + 2)
                if not last:
                    x_squares(i * 2 + 4, 0, i + 3)
                double_heads(4 * i + 5)
                qk_hi(4 * i + 5, 1, i * (4 * P) + 3 * P, 2 * i + 2)

            run(act, body)

        @block.vector
        def _(dve):
            dve.sem_inc(s_hst[0], 32)
            dve.sem_inc(s_hst[1], 32)

            def x_norm(s, slot):
                dve.wait_ge(s_sum, s + 1)
                nc.vector.tensor_scalar(stat_eps[slot][:], stat[slot][:], 1.0 / D, EPS, ALU.mult, ALU.add).then_inc(s_eps, 1)
                dve.wait_ge(s_rstd, s + 1)
                for e in range(2):
                    last = nc.vector.tensor_scalar(x[slot][:, e, :], x[slot][:, e, :], rstd[slot][:, e:e + 1], None,
                                                   ALU.mult)
                last.then_inc(s_xhat, 1)

            def h_split(s, slot, uses=None, s_prev_tiles=None):
                dve.wait_ge(s_h, 4 * s + 6)
                if uses is not None:
                    dve.wait_ge(s_hst[slot], 32 * uses)
                if s_prev_tiles is not None:
                    dve.wait_ge(s_kvp, s_prev_tiles)
                nc.vector.tensor_copy(h_hi[slot][:], h[:]).then_inc(s_hhi, 1)
                dve.wait_ge(s_hhi, s + 1)
                nc.vector.tensor_tensor(h_lo[slot][:], h[:], h_hi[slot][:].bitcast(F32), ALU.subtract).then_inc(s_hsplit, 1)

            def head_norm(t, slot, key_tile, rope=None):
                is_ctx = rope is None
                h0, h1 = heads(is_ctx)
                n = h1 - h0
                dve.wait_ge(s_kvc, t + 1)
                v = qkv[slot][:, ATTN_W + KV_W:QKV_W].rearrange("p (h d) -> p h d", h=HKV)
                v_hl = k.v_hl[:, bass.ds(key_tile, 1), :, :].rearrange("p a h d -> p (a h) d")
                nc.vector.tensor_copy(v_hl[:, :, 0:HD], v).then_inc(s_vhi, 1)
                dve.wait_ge(s_sq, t + 1)
                if not is_ctx or t:
                    dve.wait_ge(s_hrstd, t)
                nc.vector.reduce_sum(hstat[:, h0:h1], qk_sq[:, h0:h1, :], X_AXIS).then_inc(s_hsum, 1)
                dve.wait_ge(s_vhi, t + 1)
                nc.vector.tensor_tensor(v_hl[:, :, HD:P], v, v_hl[:, :, 0:HD].bitcast(F32), ALU.subtract).then_inc(s_v, 1)
                dve.wait_ge(s_hsum, t + 1)
                nc.vector.tensor_scalar(hstat[:, h0:h1], hstat[:, h0:h1], 1.0 / HD, EPS, ALU.mult,
                                        ALU.add).then_inc(s_hmean, 1)
                dve.wait_ge(s_g, t + 1)
                dve.wait_ge(s_hrstd, t + 1)
                if is_ctx:
                    if t:
                        dve.wait_ge(s_tr, t)
                    dve.sem_inc(s_c, 1)
                    nc.vector.tensor_tensor(qk_rot[:, h0:h1, 0, :], qk_g[:, h0:h1, :],
                                            hrstd[:, h0:h1].unsqueeze(2).broadcast_to([P, n, HD]),
                                            ALU.mult).then_inc(s_n, 1)
                    dve.wait_ge(s_n, t + 1)
                    dve.sem_inc(s_r, 1)
                    return
                nc.vector.tensor_tensor(qk_n[:], qk_g[:], hrstd[:].unsqueeze(2).broadcast_to([P, HN, HD]),
                                        ALU.mult).then_inc(s_n, 1)
                tslot, e, loads = rope
                dve.wait_ge(s_table[tslot], 32 * loads)
                dve.wait_ge(s_n, t + 1)
                nc.vector.tensor_tensor(qk_sin[:], qk_n[:], sin_t[tslot][:, e:e + 1, :].broadcast_to([P, HN, HD]), ALU.mult)
                nc.vector.tensor_tensor(qk_n[:], qk_n[:], cos_t[tslot][:, e:e + 1, :].broadcast_to([P, HN, HD]),
                                        ALU.mult).then_inc(s_c, 1)
                dve.wait_ge(s_c, t + 1)
                dve.wait_ge(s_tr, t)
                def half(buf, n_half):
                    return buf.rearrange("p h (a f) -> p h a f", a=2)[:, :, :, n_half * HD // 4:(n_half + 1) * HD // 4]
                rot = qk_rot[:, :, 0, :]
                nc.vector.tensor_tensor(half(rot, 0), half(qk_n[:], 0), half(qk_sin[:], 1), ALU.subtract)
                nc.vector.tensor_tensor(half(rot, 1), half(qk_n[:], 1), half(qk_sin[:], 0), ALU.add).then_inc(s_r, 1)

            def qk_lo(t, slot, key0, is_ctx=False):
                dve.wait_ge(s_trhi, t + 1)
                if not is_ctx:
                    for g in range(2):
                        lo = q_hilo[slot][HD:P, 4 * g:4 * g + 4, :]
                        nc.vector.tensor_tensor(lo, tr_ps[g][HD:P], lo.bitcast(F32), ALU.subtract)
                nc.vector.tensor_tensor(k.k_lo1[0:HD, :, bass.ds(key0, P)], tr_ps[2][0:HD, 0:HKV, :],
                                        k.k_hi2[0:HD, :, bass.ds(key0, P)].bitcast(F32), ALU.subtract).then_inc(s_trlo, 1)

            x_norm(0, 0)
            h_split(0, 0)
            x_norm(1, 1)
            h_split(1, 1, 1)
            head_norm(0, 0, TT)
            qk_lo(0, 0, SEQ, True)
            head_norm(1, 1, TT + 1)
            qk_lo(1, 1, SEQ + P, True)
            x_norm(2, 0)

            def body(i, last):
                h_split(i * 2 + 2, 0, i + 1, 4 * i + 2)
                head_norm(4 * i + 2, 0, 4 * i, (1, 0, i + 1))
                if not last:
                    x_norm(i * 2 + 3, 1)
                head_norm(4 * i + 3, 1, 4 * i + 1, (1, 1, i + 1))
                qk_lo(4 * i + 2, 0, i * (4 * P))
                if not last:
                    h_split(i * 2 + 3, 1, i + 2, 4 * i + 4)
                head_norm(4 * i + 4, 0, 4 * i + 2, (0, 0, i + 1))
                qk_lo(4 * i + 3, 1, i * (4 * P) + P)
                head_norm(4 * i + 5, 1, 4 * i + 3, (0, 1, i + 1))
                qk_lo(4 * i + 4, 0, i * (4 * P) + 2 * P)
                if not last:
                    x_norm(i * 2 + 4, 0)
                qk_lo(4 * i + 5, 1, i * (4 * P) + 3 * P)

            run(dve, body)

        @block.tensor
        def _(pe):
            def x_transpose(s, slot):
                pe.wait_ge(s_xhat, s + 1)
                for u in range(4):
                    pe.wait_ge(s_h, 4 * s + (u + 1))
                    for e in range(2):
                        for t in range(2):
                            f = 2 * u + e
                            last = nc.tensor.transpose(xt_ps[u % 2][:, e, t * P:(t + 1) * P],
                                                       x[slot][:, t, f * P:(f + 1) * P], k.ident[:])
                    last.then_inc(s_xt, 1)

            def project(s, t, slot, e, is_ctx=False):
                pe.wait_ge(s_hsplit, s + 1)
                hs = slice(e * P, (e + 1) * P)
                if not is_ctx:
                    pe.wait_ge(s_qc, t)
                    for c in range(KD):
                        last = split_matmul(nc.tensor, q_ps[:], h_hi[slot][:, c, hs], h_lo[slot][:, c, hs],
                                            k.wqkv_hi[:, c, 0:ATTN_W], k.wqkv_lo[:, c, 0:ATTN_W], c == 0, c == KD - 1)
                    last.then_inc(s_qp, 1)
                else:
                    pe.sem_inc(s_qp, 1)
                if not is_ctx or t:
                    pe.wait_ge(s_kvc, t)
                for c in range(KD):
                    last = split_matmul(nc.tensor, kv_ps[:], h_hi[slot][:, c, hs], h_lo[slot][:, c, hs],
                                        k.wqkv_hi[:, c, ATTN_W:QKV_W], k.wqkv_lo[:, c, ATTN_W:QKV_W],
                                        c == 0, c == KD - 1)
                last.then_inc(s_kvp, 1)

            def head_transpose(t, is_ctx=False):
                pe.wait_ge(s_dup, t + 1)
                if not is_ctx or t:
                    pe.wait_ge(s_trlo, t)
                for hh in range(*heads(is_ctx)):
                    last = nc.tensor.transpose(tr_ps[hh // 4][:, hh % 4, :],
                                               qk_rot[:, hh, :, :].rearrange("p e d -> p (e d)"), k.ident[:])
                last.then_inc(s_tr, 1)

            x_transpose(0, 0)
            x_transpose(1, 1)
            project(0, 0, 0, 0, True)
            head_transpose(0, True)
            project(0, 1, 0, 1, True)
            head_transpose(1, True)

            def body(i, last):
                x_transpose(i * 2 + 2, 0)
                project(i * 2 + 1, 4 * i + 2, 1, 0)
                project(i * 2 + 1, 4 * i + 3, 1, 1)
                head_transpose(4 * i + 2)
                if not last:
                    x_transpose(i * 2 + 3, 1)
                project(i * 2 + 2, 4 * i + 4, 0, 0)
                head_transpose(4 * i + 3)
                project(i * 2 + 2, 4 * i + 5, 0, 1)
                head_transpose(4 * i + 4)
                head_transpose(4 * i + 5)

            run(pe, body)


MAX_CHUNKS = [512, 512, 512, 512, 256]
MAX_USES = QB // P * len(MAX_CHUNKS)
MAX_AT = [3, 4, 3, 4, 3, 3, 0, 0, 0]
MAX_ROW_AT = 6
PAIRS = KT // 2
POOL_LO = (0, 2, 4, 6)


def attention(nc, k, d):
    with ExitStack() as ctx:
        def sb(name, shape, dt=F32):
            return ctx.enter_context(nc.sbuf_tensor(name, shape, dt))

        def ps(name, shape):
            return ctx.enter_context(nc.psum_tensor(name, shape, F32))

        q_hilo = [sb(f"blk_q_hilo{i}", [P, QB], F32R) for i in range(2)]
        q_negm = [sb(f"blk_q_negm{i}", [P, QB], F32R) for i in range(2)]
        chunk_max = sb("chunk_max", [P, QB // P, len(MAX_CHUNKS)])
        neg_max = sb("neg_max", [P, QB // P])
        diag = sb("diag", [P, QB], F32R)
        prob = [sb(f"prob{i}", [P, 2 * QB]) for i in range(3)]
        prob_hi = [sb(f"prob_hi{i}", [P, 2 * QB], F32R) for i in range(3)]
        prob_lo = [sb(f"prob_lo{i}", [P, 2 * QB], F32R) for i in range(3)]
        v_one = sb("v_one", [P, KT, HKV, P], F32R)
        part = sb("part", [HD, QB])
        hi_part = sb("hi_part", [HD, QB])
        lo_part = sb("lo_part", [HD, QB])
        att = [sb(f"att{i}", [HD, QB]) for i in range(2)]
        den = [sb(f"den{i}", [1, QB]) for i in range(2)]
        max_ps = [ps(f"max_ps{i}", [P, QB]) for i in range(2)]
        s_ps = [ps(f"s_ps{i}", [P, 2 * QB]) for i in range(2)]
        hi_ps = ps("hi_ps", [P, QB])
        lo_ps = ps("lo_ps", [P, QB])

        S = k.sem
        s_q = [S("blk_q_loaded0"), S("blk_q_loaded1")]
        s_mfull, s_mfree, s_mx = S("max_bank_full"), S("max_bank_free"), S("chunk_max_done")
        s_vone = S("v_one_ready")
        s_neg, s_diag = S("neg_max_done"), S("diag_ready")
        s_score, s_exp = S("scores_ready"), S("scores_exponentiated")
        s_lo_dve, s_lo_pool = S("prob_lo_dve"), S("prob_lo_pool")
        s_pv, s_part, s_lopart, s_sum = S("pv_done"), S("part_copied"), S("lo_part_copied"), S("hi_part_summed")
        s_att, s_den = S("att_ready"), S("den_ready")
        s_st = [S("att_stored0"), S("att_stored1")]
        att_v, den_v, q_v = k.att_dram, k.den_dram, k.q_dram

        HALF = NB // HKV
        N_IT = HALF // 2

        def run(engine, body):
            for kvh in range(HKV):
                with engine.Fori(0, N_IT - 1) as i:
                    body(i * 2 + HALF * kvh, 0, kvh, kvh)
                    body(i * 2 + (HALF * kvh + 1), 1, kvh, kvh)
                body(HALF * kvh + HALF - 2, 0, kvh, kvh)
                body(HALF * kvh + HALF - 1, 1, kvh, kvh + 1 if kvh + 1 < HKV else None)

        def slot2(slot, j):
            return (slot * PAIRS + j) % 2

        def slot3(j):
            return j % 3

        block = ctx.enter_context(nc.Block())

        @block.sync
        def _(sp):
            def load(b, slot):
                sp.dma_start(q_hilo[slot][:].bitcast(F32), q_v[b]).then_inc(s_q[slot], 16)
                sp.dma_start(q_negm[slot][0:HD, :].bitcast(F32), q_v[b][0:HD, :]).then_inc(s_q[slot], 16)

            load(0, 0)
            load(1, 1)
            for c in range(2):
                sp.dma_start(k.w_raw[c], k.w_rest_v[C_ORDER[c]]).then_inc(k.s_raw[c], 16)

            def body(b, slot, kvh, next_kvh):
                sp.wait_ge(s_score, b * PAIRS + PAIRS)
                if next_kvh is not None and not (isinstance(b, int) and b + 2 >= NB):
                    load(b + 2, slot)
                sp.wait_ge(s_att, b + 2)
                sp.dma_start(att_v[b], att[slot][:]).then_inc(s_st[slot], 16)
                sp.wait_ge(s_den, b + 2)
                sp.dma_start(den_v[b], den[slot][:]).then_inc(s_st[slot], 16)

            run(sp, body)
            for slot in range(2):
                sp.wait_ge(s_st[slot], 32 * (NB // 2 + 1))

        @block.gpsimd
        def _(pool):
            pool.sem_inc(s_att, 1)
            pool.sem_inc(s_st[0], 32)
            pool.sem_inc(s_st[1], 32)

            def lo(b, j):
                pool.wait_ge(s_exp, b * PAIRS + (j + 3))
                nc.gpsimd.tensor_tensor(prob_lo[slot3(j)][:], prob[slot3(j)][:], prob_hi[slot3(j)][:].bitcast(F32),
                                        ALU.subtract).then_inc(s_lo_pool, 1)

            for c in C_ORDER:
                pool.dma_start(k.w_rest_hi[:, :, c * CH:(c + 1) * CH], k.w_rest_v[c]).then_inc(k.s_rest_hi[c], 16)
            lo(0, 0)

            def body(b, slot, kvh, next_kvh):
                for j in POOL_LO[1:]:
                    lo(b, j)
                if next_kvh is not None:
                    lo(b + 1, POOL_LO[0])
                pool.wait_ge(s_lopart, b + 1)
                pool.wait_ge(s_sum, b + 2)
                pool.wait_ge(s_st[slot], (b - slot) * 16 + 32)
                nc.gpsimd.tensor_tensor(att[slot][:], hi_part[:], lo_part[:], ALU.add).then_inc(s_att, 1)

            run(pool, body)

        @block.scalar
        def _(act):
            act.sem_inc(s_exp, 2)
            act.sem_inc(s_den, 1)

            def exponentials(b, slot, j):
                act.wait_ge(s_score, b * PAIRS + (j + 1))
                act.wait_ge(s_pv, b * PAIRS + (j + 1))
                s = s_ps[slot2(slot, j)]
                nc.scalar.activation(prob_hi[slot3(j)][:], s[:], ACT.Exp)
                nc.scalar.activation(prob[slot3(j)][:], s[:], ACT.Exp).then_inc(s_exp, 1)

            def evacuate(b, slot):
                act.wait_ge(s_pv, b * PAIRS + (PAIRS + 3))
                act.wait_ge(s_sum, b + 1)
                nc.scalar.activation(part[:], hi_ps[HD:P, :], ACT.Copy).then_inc(s_part, 1)
                act.wait_ge(s_st[slot], (b - slot) * 16 + 32)
                nc.scalar.activation(den[slot][:], lo_ps[HD:HD + 1, :], ACT.Copy).then_inc(s_den, 1)

            exponentials(0, 0, 0)

            def body(b, slot, kvh, next_kvh):
                for j in range(1, PAIRS):
                    exponentials(b, slot, j)
                if next_kvh is not None:
                    exponentials(b + 1, 1 - slot, 0)
                evacuate(b, slot)

            run(act, body)

        @block.vector
        def _(dve):
            dve.sem_inc(s_mfree, 2)
            dve.sem_inc(s_sum, 1)

            def reduce(b, slot, u):
                qt, kc = divmod(u, len(MAX_CHUNKS))
                bank = max_ps[(slot * (MAX_USES + 1) + u) % 2]
                dve.wait_ge(s_mfull, b * (MAX_USES + 1) + (u + 1))
                last = nc.vector.reduce_max(chunk_max[:, qt, kc:kc + 1], bank[:, 0:MAX_CHUNKS[kc]], X_AXIS)
                return last.then_inc(s_mfree, 1)

            def negate(b, slot):
                dve.wait_ge(s_mfree, b * (MAX_USES + 1) + (MAX_USES + 2))
                nc.vector.tensor_reduce(neg_max[:], chunk_max[:], X_AXIS, ALU.max, negate=True).then_inc(s_neg, 1)
                dve.wait_ge(s_neg, b + 1)
                for qt in range(QB // P):
                    last = nc.vector.tensor_scalar(diag[:, qt * P:(qt + 1) * P], k.ident[:], neg_max[:, qt:qt + 1],
                                                   None, ALU.mult)
                last.then_inc(s_diag, 1)

            def max_row(b, slot):
                bank = max_ps[(slot * (MAX_USES + 1) + MAX_USES) % 2]
                dve.wait_ge(s_mfull, b * (MAX_USES + 1) + (MAX_USES + 1))
                dve.wait_ge(s_q[slot], (b - slot) * 16 + 32)
                nc.vector.tensor_copy(q_negm[slot][HD:HD + 1, :], bank[HD:HD + 1, :]).then_inc(s_mfree, 1)

            def lo(b, slot, j):
                if j in POOL_LO:
                    return
                dve.wait_ge(s_exp, b * PAIRS + (j + 3))
                nc.vector.tensor_tensor(prob_lo[slot3(j)][:], prob[slot3(j)][:], prob_hi[slot3(j)][:].bitcast(F32),
                                        ALU.subtract).then_inc(s_lo_dve, 1)

            def evacuate(b, slot):
                dve.wait_ge(s_pv, b * PAIRS + (PAIRS + 3))
                dve.wait_ge(s_att, b + 1)
                nc.vector.tensor_copy(lo_part[:], lo_ps[0:HD, :]).then_inc(s_lopart, 1)
                dve.wait_ge(s_part, b + 1)
                nc.vector.tensor_tensor(hi_part[:], hi_ps[0:HD, :], part[:], ALU.add).then_inc(s_sum, 1)

            nc.vector.memset(v_one[:, :, :, HD:P].bitcast(F32), 1.0)
            nc.vector.tensor_copy(v_one[:, :, :, 0:HD], k.v_hl[:, :, :, 0:HD].bitcast(F32)).then_inc(s_vone, 1)
            for u in range(MAX_USES):
                reduce(0, 0, u)
            negate(0, 0)
            max_row(0, 0)

            def body(b, slot, kvh, next_kvh):
                u = 0
                for j in range(PAIRS):
                    n_max = MAX_AT[j] if next_kvh is not None else 0
                    for n in range(max(n_max, 1)):
                        if n < n_max:
                            reduce(b + 1, 1 - slot, u)
                            u += 1
                        if n == 0 and j + 1 < PAIRS:
                            lo(b, slot, j + 1)
                    if n_max and u == MAX_USES:
                        negate(b + 1, 1 - slot)
                    if next_kvh is not None and j == MAX_ROW_AT:
                        max_row(b + 1, 1 - slot)
                evacuate(b, slot)

            run(dve, body)

        @block.tensor
        def _(pe):
            pe.sem_inc(s_pv, 3)

            def max_use(b, slot, kvh, u):
                qt, kc = divmod(u, len(MAX_CHUNKS))
                bank = max_ps[(slot * (MAX_USES + 1) + u) % 2]
                if u == 0:
                    pe.wait_ge(s_q[slot], (b - slot) * 16 + 32)
                pe.wait_ge(s_mfree, b * (MAX_USES + 1) + (u + 1))
                key0 = sum(MAX_CHUNKS[:kc])
                nc.tensor.matmul(bank[:, 0:MAX_CHUNKS[kc]], q_hilo[slot][:, qt * P:(qt + 1) * P],
                                 k.k_hi2[:, kvh, key0:key0 + MAX_CHUNKS[kc]], start=True, stop=True).then_inc(s_mfull, 1)

            def broadcast_max(b, slot):
                pe.wait_ge(s_diag, b + 1)
                pe.wait_ge(s_mfree, b * (MAX_USES + 1) + (MAX_USES + 1))
                bank = max_ps[(slot * (MAX_USES + 1) + MAX_USES) % 2]
                nc.tensor.matmul(bank[:], k.ones_sq[:], diag[:], start=True, stop=True).then_inc(s_mfull, 1)

            def scores(b, slot, kvh, j, e):
                if j == 0 and e == 0:
                    pe.wait_ge(s_mfree, (b + 1) * (MAX_USES + 1) + 2)
                if e == 0:
                    pe.wait_ge(s_exp, b * PAIRS + (j + 1))
                keys = slice((2 * j + e) * P, (2 * j + e + 1) * P)
                out = s_ps[slot2(slot, j)][:, e * QB:(e + 1) * QB]
                nc.tensor.matmul(out, k.k_hi2[:, kvh, keys], q_hilo[slot][:], start=True, stop=False)
                last = nc.tensor.matmul(out, k.k_lo1[0:HD + 1, kvh, keys], q_negm[slot][0:HD + 1, :],
                                        start=False, stop=True)
                if e == 1:
                    last.then_inc(s_score, 1)

            def pv(b, slot, kvh, j, e):
                if j == 0 and e == 0:
                    pe.wait_ge(s_sum, b + 1)
                    pe.wait_ge(s_den, b + 1)
                if e == 0:
                    pe.wait_ge(s_exp, b * PAIRS + (j + 3))
                    if j in POOL_LO:
                        pe.wait_ge(s_lo_pool, b * len(POOL_LO) + (POOL_LO.index(j) + 1))
                    else:
                        before = sum(1 for m in range(j) if m not in POOL_LO)
                        pe.wait_ge(s_lo_dve, b * (PAIRS - len(POOL_LO)) + (before + 1))
                kt = 2 * j + e
                q = slice(e * QB, (e + 1) * QB)
                hi, lo = prob_hi[slot3(j)][:, q], prob_lo[slot3(j)][:, q]
                first, final = kt == 0, kt == KT - 1
                nc.tensor.matmul(hi_ps[:], k.v_hl[:, kt, kvh, :], hi, start=first, stop=final)
                nc.tensor.matmul(lo_ps[:], k.zero_one[:], hi, start=first, stop=False)
                last = nc.tensor.matmul(lo_ps[:], v_one[:, kt, kvh, :], lo, start=False, stop=final)
                if e == 1:
                    last.then_inc(s_pv, 1)

            for u in range(MAX_USES):
                max_use(0, 0, 0, u)
            pe.wait_ge(s_vone, 1)
            broadcast_max(0, 0)
            for j in range(2):
                for e in range(2):
                    scores(0, 0, 0, j, e)

            def body(b, slot, kvh, next_kvh):
                u = 0
                for j in range(PAIRS):
                    n_max = MAX_AT[j] if next_kvh is not None else 0
                    if j + 2 < PAIRS:
                        ahead = [(scores, b, slot, kvh, j + 2, e) for e in range(2)]
                    elif next_kvh is not None:
                        ahead = [(scores, b + 1, 1 - slot, next_kvh, j + 2 - PAIRS, e) for e in range(2)]
                    else:
                        ahead = []
                    here = [(pv, b, slot, kvh, j, e) for e in range(2)]
                    for n, (f, *args) in enumerate(ahead + here):
                        if n == 2 and next_kvh is not None and j == MAX_ROW_AT:
                            broadcast_max(b + 1, 1 - slot)
                        f(*args)
                        if n < n_max:
                            max_use(b + 1, 1 - slot, next_kvh, u)
                            u += 1

            run(pe, body)


def project_gates(nc, k, d):
    with ExitStack() as ctx:
        def sb(name, shape, dt=F32):
            return ctx.enter_context(nc.sbuf_tensor(name, shape, dt))

        TG = QB
        N_TG = SEQ // TG
        NG = MT - GROUPS
        w_hi, w_raw = k.w_rest_hi, k.w_raw
        w_lo = sb("w_rest_lo", [P, KD, REST_W], F32R)
        hh = [sb(f"hh{i}", [P, KD, TG], F32R) for i in range(2)]
        hl = [sb(f"hl{i}", [P, KD, TG], F32R) for i in range(2)]
        stage = [sb(f"stage{i}", [P, TG]) for i in range(2)]
        den = sb("den_all", [P, NB * QB // P])
        acc = [ctx.enter_context(nc.psum_tensor(f"acc{i}", [P, TG], F32)) for i in range(4)]
        even = sb("even_sum", [P, SUB])
        S = k.sem
        s_wlo = S("w_rest_lo_ready")
        s_hh = [S("hh_loaded0"), S("hh_loaded1")]
        s_hl = [S("hl_loaded0"), S("hl_loaded1")]
        s_acc, s_free = S("rest_projected"), S("rest_bank_read")
        s_den, s_dinv, s_dst = S("den_loaded"), S("den_inverted"), S("den_inv_stored")
        s_comb = S("position_sums")
        s_st = [S(f"rest_stored{i}") for i in range(2)]
        h_v = k.h_dram.rearrange("e k p (g t) -> g e p k t", t=TG)
        r_v = k.rest_dram.rearrange("m p (g t) -> g m p t", t=TG)
        den_rows = [v.rearrange("b (a q) -> (b a) q", q=P) for v in (k.den_dram, k.inv_dram)]

        def run(engine, body):
            with engine.Fori(0, N_TG // 2) as i:
                for slot in range(2):
                    body(i * 2 + slot, slot, i)

        block = ctx.enter_context(nc.Block())

        @block.sync
        def _(sp):
            sp.dma_start(hh[0][:].bitcast(F32), h_v[0][0]).then_inc(s_hh[0], 16)
            sp.dma_start(hl[0][:].bitcast(F32), h_v[0][1]).then_inc(s_hl[0], 16)
            sp.dma_start(den[:], den_rows[0]).then_inc(s_den, 16)
            for c in range(2, NCH):
                sp.wait_ge(s_wlo, c - 1)
                sp.dma_start(w_raw[c % 2], k.w_rest_v[C_ORDER[c]]).then_inc(k.s_raw[c % 2], 16)
            sp.dma_start(hh[1][:].bitcast(F32), h_v[1][0]).then_inc(s_hh[1], 16)
            sp.dma_start(hl[1][:].bitcast(F32), h_v[1][1]).then_inc(s_hl[1], 16)
            sp.wait_ge(s_dinv, 1)
            sp.dma_start(den_rows[1], den[:]).then_inc(s_dst, 16)
            for tg in range(N_TG):
                for n in range(GROUPS, MT):
                    sp.wait_ge(s_free, tg * MT + (n + 5))
                    sp.dma_start(r_v[tg][M_ORDER[n]], stage[n % 2][:]).then_inc(s_st[n % 2], 16)
                if tg + 2 < N_TG:
                    sp.wait_ge(s_acc, (tg + 1) * MT)
                    sp.dma_start(hh[tg % 2][:].bitcast(F32), h_v[tg + 2][0]).then_inc(s_hh[tg % 2], 16)
                    sp.dma_start(hl[tg % 2][:].bitcast(F32), h_v[tg + 2][1]).then_inc(s_hl[tg % 2], 16)
            sp.wait_ge(s_dst, 16)
            for i in range(2):
                sp.wait_ge(s_st[i], 16 * (N_TG * NG // 2 + 1))

        @block.vector
        def _(dve):
            for n, c in enumerate(C_ORDER):
                cols = slice(c * CH, (c + 1) * CH)
                dve.wait_ge(k.s_raw[n % 2], 16 * (n // 2 + 1))
                dve.wait_ge(k.s_rest_hi[c], 16)
                nc.vector.tensor_tensor(w_lo[:, :, cols], w_raw[n % 2], w_hi[:, :, cols].bitcast(F32),
                                        ALU.subtract).then_inc(s_wlo, 1)
            dve.wait_ge(s_den, 16)
            nc.vector.reciprocal(den[:], den[:]).then_inc(s_dinv, 1)
            dve.wait_ge(s_free, (N_TG - 1) * MT + GROUPS + 4)
            for g in range(GROUPS):
                q = [k.u[n][:, g, :] for n in range(RADIX)]
                steps = ((even[:], q[0], q[2], ALU.add), (q[2], q[0], q[2], ALU.subtract),
                         (q[0], q[1], q[3], ALU.add), (q[3], q[1], q[3], ALU.subtract),
                         (q[1], even[:], q[0], ALU.subtract), (q[0], even[:], q[0], ALU.add))
                for n, (out, a, b, op) in enumerate(steps):
                    if g or n:
                        dve.wait_ge(s_comb, len(steps) * g + n)
                    nc.vector.tensor_tensor(out, a, b, op).then_inc(s_comb, 1)
            dve.wait_ge(s_comb, GROUPS * len(steps))

        @block.scalar
        def _(act):
            act.sem_inc(s_free, 4)
            for i in range(2):
                act.sem_inc(s_st[i], 16)

            def body(tg, slot, i):
                for n, m in enumerate(M_ORDER):
                    act.wait_ge(s_acc, tg * MT + (n + 1))
                    if n < GROUPS:
                        if slot:
                            act.wait_ge(s_wlo, NCH)
                        nc.scalar.activation(k.u_sides[slot][:, bass.ds(i, 1), n, :].rearrange("p a n -> p (a n)"),
                                             acc[n % 4][:], ACT.Copy).then_inc(s_free, 1)
                    else:
                        act.wait_ge(s_st[n % 2], tg * (16 * NG // 2) + 16 * ((n - GROUPS) // 2 + 1))
                        nc.scalar.activation(stage[n % 2][:], acc[n % 4][:], ACT.Silu).then_inc(s_free, 1)

            run(act, body)

        @block.tensor
        def _(pe):
            def body(tg, slot, i):
                pe.wait_ge(s_hh[slot], i * 16 + 16)
                pe.wait_ge(s_hl[slot], i * 16 + 16)
                for n, m in enumerate(M_ORDER):
                    cols = slice(m * P, (m + 1) * P)
                    pe.wait_ge(s_wlo, n // 2 + 1)
                    pe.wait_ge(s_free, tg * MT + (n + 1))
                    for c in range(KD):
                        last = split_matmul(nc.tensor, acc[n % 4][:], w_hi[:, c, cols], w_lo[:, c, cols],
                                            hh[slot][:, c, :], hl[slot][:, c, :], c == 0, c == KD - 1)
                    last.then_inc(s_acc, 1)

            run(pe, body)


def fourier(nc, k, d):
    with ExitStack() as ctx:
        def sb(name, shape, dt=F32):
            return ctx.enter_context(nc.sbuf_tensor(name, shape, dt))

        def ps(name, shape):
            return ctx.enter_context(nc.psum_tensor(name, shape, F32))

        ORDER = (0, 2, 1, 3)
        PARTS = {0: ((0, 1),), 2: ((1, 1),), 1: ((2, 1), (3, 0)), 3: ((2, 1), (3, 2))}
        NTAB = 6
        u = k.u
        c_hi = sb("c_hi", [P, 2, GROUPS, SUB], F32R)
        c_lo = sb("c_lo", [P, 2, GROUPS, SUB], F32R)
        ab_hi = sb("ab_hi", [P, SUBT, GROUPS, 2 * P], F32R)
        ab_lo = sb("ab_lo", [P, SUBT, GROUPS, 2 * P], F32R)
        tab = [sb(f"tab{i}", [P, 2, 2, SUB], F32R) for i in range(NTAB)]
        wf = sb("wf", [P, GROUPS, P])
        chan = sb("chan", [P, 2, P])
        m_hi = sb("m_hi", [P, GROUPS, 4, P], F32R)
        m_lo = sb("m_lo", [P, GROUPS, 4, P], F32R)
        y = sb("y", [P, GROUPS, SUB, RADIX])
        ab_ps = [ps(f"ab_ps{i}", [P, 2, 2 * P]) for i in range(4)]
        dft_ps = [ps(f"dft_ps{i}", [P, SUB]) for i in range(GROUPS)]
        m_ps = dft_ps[0:2]

        S = k.sem
        s_in = S("fourier_small_loaded")
        s_tab = [S(f"table_loaded{i}") for i in range(NTAB)]
        s_tabfree, s_dft = S("table_used"), S("dft_bank_done")
        s_m, s_mhi, s_mlo, s_mneg = S("channel_product"), S("m_hi_ready"), S("m_lo_ready"), S("m_negated")
        s_chi, s_clo = S("sum_hi_ready"), S("sum_lo_ready")
        s_ab, s_abhi, s_ablo = S("ab_product"), S("ab_hi_ready"), S("ab_lo_ready")
        s_y, s_yst = S("y_written"), S("y_stored")
        s_w, s_wg = S("w_o_loaded"), S("w_o_gated")

        block = ctx.enter_context(nc.Block())

        @block.sync
        def _(sp):
            sp.dma_start(chan[:], d["chan"]).then_inc(s_in, 16)
            sp.dma_start(wf[:], d["w_f"][0].rearrange("g c n -> c g n")).then_inc(s_in, 16)
            sp.wait_ge(s_clo, RADIX)
            w_o_v = d["w_o"][0].rearrange("(a k p) n -> a p k n", a=2, p=P)
            for a in range(2):
                sp.dma_start(k.w_o_half[a], w_o_v[a]).then_inc(s_w, 16)
            for g in range(GROUPS):
                sp.wait_ge(s_y, (RADIX - 1) * GROUPS + g + 1)
                sp.dma_start(k.y_dram[g], y[:, g].rearrange("p n r -> p (n r)")).then_inc(s_yst, 16)
            sp.wait_ge(s_yst, 16 * GROUPS)

        @block.gpsimd
        def _(pool):
            for n in range(RADIX * SUBT):
                if n >= NTAB:
                    pool.wait_ge(s_tabfree, n - NTAB + 1)
                pool.dma_start(tab[n % NTAB][:], d["dft"][ORDER[n // SUBT], n % SUBT]).then_inc(s_tab[n % NTAB], 16)
            for i in range(NTAB):
                pool.wait_ge(s_tab[i], 16 * len(range(i, RADIX * SUBT, NTAB)))

        @block.scalar
        def _(act):
            def sum_hi(n):
                if n >= 2:
                    act.wait_ge(s_ab, 2 * SUBT * (n - 1))
                nc.scalar.activation(c_hi[:, n % 2], u[n], ACT.Copy).then_inc(s_chi, 1)

            sum_hi(0)
            act.wait_ge(s_m, 2)
            for i in range(2):
                nc.scalar.activation(m_hi[:, :, 1 + i, :], m_ps[i][:].rearrange("p (g c) -> p g c", g=GROUPS),
                                     ACT.Copy).then_inc(s_mhi, 1)
            sum_hi(1)
            act.wait_ge(s_mlo, 2)
            for part, of in ((0, 2), (3, 1)):
                nc.scalar.activation(m_hi[:, :, part, :], m_hi[:, :, of, :].bitcast(F32), ACT.Copy, scale=-1.0)
                last = nc.scalar.activation(m_lo[:, :, part, :], m_lo[:, :, of, :].bitcast(F32), ACT.Copy, scale=-1.0)
            last.then_inc(s_mneg, 1)
            for step, j in enumerate(ORDER):
                for n in range(2 * SUBT):
                    mt, gp = divmod(n, 2)
                    act.wait_ge(s_ab, 2 * SUBT * step + n + 1)
                    if step:
                        act.wait_ge(s_tabfree, step * SUBT)
                    nc.scalar.activation(ab_hi[:, mt, 2 * gp:2 * gp + 2, :], ab_ps[n % 4][:], ACT.Copy).then_inc(s_abhi, 1)
                if step < 2:
                    sum_hi(step + 2)
                for g in range(GROUPS):
                    act.wait_ge(s_dft, GROUPS * step + g + 1)
                    nc.scalar.activation(y[:, g, :, j], dft_ps[g][:], ACT.Copy).then_inc(s_y, 1)

        @block.vector
        def _(dve):
            def sum_lo(n):
                dve.wait_ge(s_chi, n + 1)
                nc.vector.tensor_tensor(c_lo[:, n % 2], u[n], c_hi[:, n % 2].bitcast(F32),
                                        ALU.subtract).then_inc(s_clo, 1)

            sum_lo(0)
            for i in range(2):
                dve.wait_ge(s_mhi, i + 1)
                nc.vector.tensor_tensor(m_lo[:, :, 1 + i, :], m_ps[i][:].rearrange("p (g c) -> p g c", g=GROUPS),
                                        m_hi[:, :, 1 + i, :].bitcast(F32), ALU.subtract).then_inc(s_mlo, 1)
            sum_lo(1)
            for step in range(RADIX):
                for n in range(2 * SUBT):
                    mt, gp = divmod(n, 2)
                    dve.wait_ge(s_abhi, 2 * SUBT * step + n + 1)
                    hi = ab_hi[:, mt, 2 * gp:2 * gp + 2, :]
                    nc.vector.tensor_tensor(ab_lo[:, mt, 2 * gp:2 * gp + 2, :], ab_ps[n % 4][:], hi.bitcast(F32),
                                            ALU.subtract).then_inc(s_ablo, 1)
                if step < 2:
                    sum_lo(step + 2)
                if step >= 2:
                    dve.wait_ge(s_w, 32)
                    for c in range((step - 2) * KD // 2, (step - 1) * KD // 2):
                        nc.vector.tensor_tensor(k.w_o_raw[c], k.w_o_raw[c], k.gate_bc[:],
                                                ALU.mult).then_inc(s_wg, 1)
            dve.wait_ge(s_wg, KD)

        @block.tensor
        def _(pe):
            pe.wait_ge(s_in, 32)
            for i in range(2):
                nc.tensor.matmul(m_ps[i][:], chan[:, i, :], wf[:].rearrange("p g c -> p (g c)"), start=True,
                                 stop=True).then_inc(s_m, 1)
            pe.wait_ge(s_mlo, 2)
            for step, j in enumerate(ORDER):
                pe.wait_ge(s_clo, (1, 2, 4, 4)[step])
                if step == 2:
                    pe.wait_ge(s_mneg, 1)
                for n in range(2 * SUBT):
                    mt, gp = divmod(n, 2)
                    use = 2 * SUBT * step + n
                    if use >= 4:
                        pe.wait_ge(s_ablo, use - 3)
                    for gg in range(2):
                        g = 2 * gp + gg
                        for i, (src, part) in enumerate(PARTS[j]):
                            rows = (slice(None), src % 2, g, slice(mt * P, (mt + 1) * P))
                            last = split_matmul(nc.tensor, ab_ps[n % 4][:, gg, :], c_hi[rows], c_lo[rows],
                                                m_hi[:, g, part:part + 2, :].rearrange("p a c -> p (a c)"),
                                                m_lo[:, g, part:part + 2, :].rearrange("p a c -> p (a c)"),
                                                i == 0, i == len(PARTS[j]) - 1)
                    last.then_inc(s_ab, 1)
                if step:
                    pe.wait_ge(s_y, step * GROUPS)

                def dft(mt, g):
                    n = step * SUBT + mt
                    pe.wait_ge(s_ablo, 2 * SUBT * step + 2 * mt + 2)
                    pe.wait_ge(s_tab[n % NTAB], 16 * (n // NTAB + 1))
                    for cs in range(2):
                        a = (slice(None), mt, g, slice(cs * P, (cs + 1) * P))
                        last = split_matmul(nc.tensor, dft_ps[g][:], ab_hi[a], ab_lo[a], tab[n % NTAB][:, 0, cs, :],
                                            tab[n % NTAB][:, 1, cs, :], mt == 0 and cs == 0,
                                            mt == SUBT - 1 and cs == 1)
                    return last

                if step < RADIX - 1:
                    for mt in range(SUBT):
                        for g in range(GROUPS):
                            last = dft(mt, g)
                            if mt == SUBT - 1:
                                last.then_inc(s_dft, 1)
                        if mt < SUBT - 1:
                            last.then_inc(s_tabfree, 1)
                    pe.wait_ge(s_dft, GROUPS * (step + 1))
                    pe.sem_inc(s_tabfree, 1)
                else:
                    for g in range(GROUPS):
                        for mt in range(SUBT):
                            last = dft(mt, g)
                        last.then_inc(s_dft, 1)


def output(nc, k, d):
    with ExitStack() as ctx:
        def sb(name, shape, dt=F32):
            return ctx.enter_context(nc.sbuf_tensor(name, shape, dt))

        TG = 2 * P
        N_TG = SEQ // TG
        AF = ATTN_W // P
        ATT, FOU = slice(0, AF), slice(AF, KD)
        w_raw = k.w_o_raw
        w_hi = sb("w_o_hi", [P, KD, D], F32R)
        w_lo = sb("w_o_lo", [P, KD, D], F32R)
        yin = [sb(f"yin{i}", [P, KD, TG]) for i in range(2)]
        gin = [sb(f"gin{i}", [P, KD, TG]) for i in range(2)]
        inv = [sb(f"inv{i}", [P, AF, TG]) for i in range(2)]
        y_hi = [sb(f"y_hi{i}", [P, KD, TG], F32R) for i in range(2)]
        y_lo = [sb(f"y_lo{i}", [P, KD, TG], F32R) for i in range(2)]
        x = [sb(f"x_res{i}", [P, D]) for i in range(2)]
        res = [sb(f"res{i}", [P, D]) for i in range(2)]
        square = sb("res_square", [P, 2, D], mybir.dt.bfloat16)
        stat = [sb(f"res_stat{i}", [P, 1]) for i in range(2)]
        mean = [sb(f"res_mean{i}", [P, 1]) for i in range(2)]
        rstd = [sb(f"res_rstd{i}", [P, 1]) for i in range(2)]
        minus_half = sb("out_minus_half", [P, 1])
        o_ps = [ctx.enter_context(nc.psum_tensor(f"o_ps{i}", [P, 2, 512], F32)) for i in range(2)]
        S = k.sem
        s_whi, s_wlo = S("w_o_hi_ready"), S("w_o_lo_ready")
        s_att_in = [S("att_inputs_loaded0"), S("att_inputs_loaded1")]
        s_fou_in = [S("fourier_inputs_loaded0"), S("fourier_inputs_loaded1")]
        s_norm, s_y, s_yhi, s_ylo = S("att_normed"), S("y_gated"), S("y_hi_ready"), S("y_lo_ready")
        s_x = [S("x_res_loaded0"), S("x_res_loaded1")]
        s_o, s_add, s_sum, s_mean, s_rstd, s_out = (S("out_projected"), S("residual_added"), S("res_squares"),
                                                    S("res_mean_ready"), S("res_rstd_ready"), S("out_ready"))
        s_half = S("out_minus_half_set")
        s_st = [S("out_stored0"), S("out_stored1")]
        att_v = k.att_dram.rearrange("(f e b) c q -> b e c f q", e=2, b=NQB)
        inv_v = k.inv_dram.rearrange("(f e b) q -> b e f q", e=2, b=NQB)
        x_v = d["x"][0].rearrange("(t p) n -> t p n", p=P)
        out_v = d["out"][0].rearrange("(t p) n -> t p n", p=P)
        ATT_LOADS, FOU_LOADS = 5, 2
        PREP0 = 2

        def run(engine, body):
            body(0, 0, 0, True, True)
            with engine.Fori(0, (N_TG - 4) // 2) as i:
                body(i * 2 + 1, 1, i + 1, True, True)
                body(i * 2 + 2, 0, i + 1, True, True)
            for g in range(N_TG - 3, N_TG):
                body(g, g % 2, (g + 1) // 2, g + 2 < N_TG, g + 1 < N_TG)

        block = ctx.enter_context(nc.Block())

        @block.sync
        def _(sp):
            def load_group(slot, blk):
                cols = slice(slot * TG, (slot + 1) * TG)
                tok = bass.ds(blk * QB + slot * TG, TG)
                for e in range(2):
                    rows = slice(e * HD, (e + 1) * HD)
                    sp.dma_start(yin[slot][rows, ATT, :], att_v[blk][e][:, :, cols]).then_inc(s_att_in[slot], 16)
                    sp.dma_start(inv[slot][rows, :, :], inv_v[blk][e][:, cols].partition_broadcast(HD)).then_inc(s_att_in[slot], 16)
                sp.dma_start(gin[slot][:, ATT, :],
                             k.rest_dram[0:AF, :, tok].rearrange("m p t -> p m t")).then_inc(s_att_in[slot], 16)
                sp.dma_start(yin[slot][:, FOU, :], k.y_dram[:, :, tok].rearrange("m p t -> p m t")).then_inc(s_fou_in[slot], 16)
                sp.dma_start(gin[slot][:, FOU, :],
                             k.rest_dram[2 * AF:3 * AF, :, tok].rearrange("m p t -> p m t")).then_inc(s_fou_in[slot], 16)

            load_group(0, 0)
            for e in range(2):
                sp.dma_start(x[e][:], x_v[e]).then_inc(s_x[e], 16)
            load_group(1, 0)

            def body(g, slot, m, ahead, after):
                if ahead:
                    sp.wait_ge(s_ylo, g + PREP0)
                    sp.wait_ge(s_yhi, g + PREP0)
                    load_group(slot, m + (1 - slot))
                for e in range(2):
                    t = g * 2 + e
                    if after:
                        sp.wait_ge(s_add, t + 3)
                        sp.dma_start(x[e][:], x_v[t + 2]).then_inc(s_x[e], 16)
                    sp.wait_ge(s_out, t + 1)
                    sp.dma_start(out_v[t], res[e][:]).then_inc(s_st[e], 16)

            run(sp, body)
            for e in range(2):
                sp.wait_ge(s_st[e], 16 * (N_TG + 1))

        @block.gpsimd
        def _(pool):
            nc.gpsimd.memset(minus_half[:], -0.5).then_inc(s_half, 1)
            pool.wait_ge(s_half, 1)

            def body(g, slot, m, ahead, after):
                for e in range(2):
                    pool.wait_ge(s_mean, g * 2 + (e + 1))
                    nc.gpsimd.tensor_tensor(rstd[e][:], mean[e][:], minus_half[:], ALU.pow).then_inc(s_rstd, 1)

            run(pool, body)

        @block.scalar
        def _(act):
            act.sem_inc(s_st[0], 16)
            act.sem_inc(s_st[1], 16)
            for half, part in enumerate((ATT, FOU)):
                for c in range(part.start, part.stop):
                    nc.scalar.activation(w_hi[:, c, :], w_raw[c], ACT.Copy).then_inc(s_whi, 1)
                act.wait_ge(s_y, half + 1)
                nc.scalar.activation(y_hi[0][:, part, :], yin[0][:, part, :], ACT.Copy).then_inc(s_yhi, 1)

            def body(g, slot, m, ahead, after):
                if after:
                    act.wait_ge(s_y, g + (1 + PREP0))
                    act.wait_ge(s_o, g * 2 + 2)
                    nc.scalar.activation(y_hi[1 - slot][:], yin[1 - slot][:], ACT.Copy).then_inc(s_yhi, 1)
                for e in range(2):
                    act.wait_ge(s_add, g * 2 + (e + 3))
                    nc.scalar.activation(square[:, e, :], res[e][:], ACT.Square, accum_out=stat[e][:]).then_inc(s_sum, 1)

            run(act, body)

        @block.vector
        def _(dve):
            dve.sem_inc(s_add, 2)

            for half, part in enumerate((ATT, FOU)):
                for c in range(part.start, part.stop):
                    dve.wait_ge(s_whi, c + 1)
                    nc.vector.tensor_tensor(w_lo[:, c, :], w_raw[c], w_hi[:, c, :].bitcast(F32),
                                            ALU.subtract).then_inc(s_wlo, 1)
                if half == 0:
                    dve.wait_ge(s_att_in[0], 16 * ATT_LOADS)
                    nc.vector.tensor_tensor(yin[0][:, ATT, :], yin[0][:, ATT, :], inv[0][:], ALU.mult).then_inc(s_norm, 1)
                    dve.wait_ge(s_norm, 1)
                else:
                    dve.wait_ge(s_fou_in[0], 16 * FOU_LOADS)
                nc.vector.tensor_tensor(yin[0][:, part, :], yin[0][:, part, :], gin[0][:, part, :],
                                        ALU.mult).then_inc(s_y, 1)
                dve.wait_ge(s_yhi, half + 1)
                nc.vector.tensor_tensor(y_lo[0][:, part, :], yin[0][:, part, :], y_hi[0][:, part, :].bitcast(F32),
                                        ALU.subtract).then_inc(s_ylo, 1)

            def body(g, slot, m, ahead, after):
                if after:
                    nxt = 1 - slot
                    dve.wait_ge(s_att_in[nxt], m * (16 * ATT_LOADS) + 16 * ATT_LOADS)
                    dve.wait_ge(s_fou_in[nxt], m * (16 * FOU_LOADS) + 16 * FOU_LOADS)
                    nc.vector.tensor_tensor(yin[nxt][:, ATT, :], yin[nxt][:, ATT, :], inv[nxt][:],
                                            ALU.mult).then_inc(s_norm, 1)
                    dve.wait_ge(s_norm, g + 2)
                    nc.vector.tensor_tensor(yin[nxt][:], yin[nxt][:], gin[nxt][:], ALU.mult).then_inc(s_y, 1)
                    dve.wait_ge(s_yhi, g + (1 + PREP0))
                    nc.vector.tensor_tensor(y_lo[nxt][:], yin[nxt][:], y_hi[nxt][:].bitcast(F32),
                                            ALU.subtract).then_inc(s_ylo, 1)
                for e in range(2):
                    t = g * 2 + e
                    dve.wait_ge(s_o, t + 3)
                    dve.wait_ge(s_x[e], g * 16 + 16)
                    dve.wait_ge(s_st[e], g * 16 + 16)
                    nc.vector.tensor_tensor(res[e][:], o_ps[e][:].rearrange("p a n -> p (a n)"), x[e][:],
                                            ALU.add).then_inc(s_add, 1)
                    dve.wait_ge(s_sum, t + 1)
                    nc.vector.tensor_scalar(mean[e][:], stat[e][:], 1.0 / D, EPS, ALU.mult, ALU.add).then_inc(s_mean, 1)
                    dve.wait_ge(s_rstd, t + 1)
                    nc.vector.scalar_tensor_tensor(res[e][:], res[e][:], rstd[e][:], k.final_bc[:], ALU.mult,
                                                   ALU.mult).then_inc(s_out, 1)

            run(dve, body)

        @block.tensor
        def _(pe):
            pe.sem_inc(s_o, 2)

            def product(slot, e, n, c):
                cols = slice(n * 512, (n + 1) * 512)
                toks = slice(e * P, (e + 1) * P)
                return split_matmul(nc.tensor, o_ps[e][:, n, :], y_hi[slot][:, c, toks], y_lo[slot][:, c, toks],
                                    w_hi[:, c, cols], w_lo[:, c, cols], c == 0, c == KD - 1)

            def body(g, slot, m, ahead, after):
                if isinstance(g, int) and g == 0:
                    for c in range(KD):
                        pe.wait_ge(s_wlo, c + 1)
                        pe.wait_ge(s_ylo, c // AF + 1)
                        for e in range(2):
                            for n in range(2):
                                last = product(slot, e, n, c)
                            if c == KD - 1:
                                last.then_inc(s_o, 1)
                    return
                pe.wait_ge(s_ylo, g + PREP0)
                for e in range(2):
                    pe.wait_ge(s_add, g * 2 + (e + 1))
                    for n in range(2):
                        for c in range(KD):
                            last = product(slot, e, n, c)
                    last.then_inc(s_o, 1)

            run(pe, body)


class Shared:
    pass


def build(nc, d):
    with ExitStack() as ctx:
        def sb(name, shape, dt=F32):
            return ctx.enter_context(nc.sbuf_tensor(name, shape, dt))

        def dram(name, shape):
            return nc.dram_tensor(name, shape, F32, kind="Internal").ap()

        k = Shared()
        k.sem = lambda name: ctx.enter_context(nc.semaphore(name))
        k.h_dram = dram("h_scratch", (2, KD, P, SEQ))
        k.q_dram = dram("q_scratch", (NB, P, QB))
        k.att_dram = dram("att_scratch", (NB, HD, QB))
        k.den_dram = dram("den_scratch", (NB, QB))
        k.inv_dram = dram("inv_scratch", (NB, QB))
        k.rest_dram = dram("rest_scratch", (MT, P, SEQ))
        k.y_dram = dram("y_scratch", (GROUPS, P, SEQ))
        k.ident = sb("ident_sb", [P, P])
        k.gate_bc = sb("gate_bc", [P, D])
        k.final_bc = sb("final_bc", [P, D])
        outer = ctx.enter_context(ExitStack())
        right = ctx.enter_context(ExitStack())
        with ExitStack() as inner:
            def sbi(name, shape, dt=F32):
                return inner.enter_context(nc.sbuf_tensor(name, shape, dt))

            k.ones_sq = sbi("ones_sq", [P, P], F32R)
            k.zero_one = sbi("zero_one", [P, P], F32R)
            k.k_hi2 = sbi("k_hi2", [P, HKV, KEYS], F32R)
            k.k_lo1 = sbi("k_lo1", [P, HKV, KEYS], F32R)
            k.v_hl = sbi("v_hl", [P, KT, HKV, P], F32R)
            with ExitStack() as first:
                k.scale = first.enter_context(nc.sbuf_tensor("scale", [P, 2, KD], F32))
                k.shift = first.enter_context(nc.sbuf_tensor("shift", [P, 2, KD], F32))
                k.head_bc = first.enter_context(nc.sbuf_tensor("head_bc", [P, HN * HD], F32))
                k.wqkv_hi = first.enter_context(nc.sbuf_tensor("wqkv_hi", [P, KD, QKV_W], F32R))
                k.wqkv_lo = first.enter_context(nc.sbuf_tensor("wqkv_lo", [P, KD, QKV_W], F32R))
                modulation(nc, k, d)
                project_qkv(nc, k, d)
            k.u_odd = outer.enter_context(nc.sbuf_tensor("u_odd", [P, 2, GROUPS, SUB], F32, side="right"))
            k.w_rest_hi = right.enter_context(nc.sbuf_tensor("w_rest_hi", [P, KD, REST_W], F32R, side="right"))
            k.w_raw = [k.u_odd[:, i].rearrange("p g (a n) -> p (g a) n", n=CH) for i in range(2)]
            k.w_rest_v = d["w_in"][0][:, GA0:GA0 + REST_W].rearrange("(k p) (c n) -> c p k n", p=P, n=CH)
            k.s_raw = [k.sem("w_rest_loaded0"), k.sem("w_rest_loaded1")]
            k.s_rest_hi = [k.sem(f"w_rest_hi{c}") for c in range(NCH)]
            attention(nc, k, d)
        with ExitStack() as branch:
            k.u_even = branch.enter_context(nc.sbuf_tensor("u_even", [P, 2, GROUPS, SUB], F32))
            k.u_sides = (k.u_even, k.u_odd)
            k.u = [k.u_sides[n % 2][:, n // 2] for n in range(RADIX)]
            project_gates(nc, k, d)
            right.close()
            k.w_o_half = [side[:].rearrange("p m g n -> p (m g n)").rearrange("p (k n) -> p k n", n=D)
                          for side in k.u_sides]
            k.w_o_raw = [k.w_o_half[c * 2 // KD][:, c % (KD // 2), :] for c in range(KD)]
            fourier(nc, k, d)
            output(nc, k, d)


def constants():
    import numpy as np
    grid_w, theta, freqs = 64, 10000.0, HD // 4
    pos = np.arange(SEQ)
    inv = np.float32(theta) ** (-np.arange(freqs, dtype=np.float32) / np.float32(freqs))
    ang = np.stack([(pos // grid_w).astype(np.float32)[:, None] * inv,
                    (pos % grid_w).astype(np.float32)[:, None] * inv], axis=1)
    ang = np.repeat(ang[:, :, None, :], 2, axis=2).reshape(SEQ, HD)
    c = np.arange(P)
    chan_ang = 2 * np.pi * np.outer(c, c) / P
    norm = 1.0 / np.sqrt(float(SEQ) * P)
    chan = np.stack([np.cos(chan_ang), np.sin(chan_ang)], axis=1) * norm
    j, m, n = np.arange(RADIX)[:, None, None], np.arange(SUB)[None, :, None], np.arange(SUB)[None, None, :]
    dft_ang = 2 * np.pi * (((RADIX * n + j) * m) % SEQ) / SEQ
    dft = np.stack([np.cos(dft_ang), -np.sin(dft_ang)], axis=2).astype(np.float32)
    bits = dft.view(np.uint32)
    hi = (((bits + np.uint32(0x7FF) + ((bits >> np.uint32(12)) & np.uint32(1))) >> np.uint32(12)) << np.uint32(12))
    hi = hi.view(np.float32)
    dft = np.stack([hi, dft - hi], axis=2).reshape(RADIX, SUBT, P, 2, 2, SUB)
    return {"ident": np.eye(P, dtype=np.float32), "cos": np.cos(ang).astype(np.float32),
            "sin": np.sin(ang).astype(np.float32), "chan": chan.astype(np.float32),
            "dft": np.ascontiguousarray(dft)}


_INS = ["x", "c", "ctx", "c_ctx", "norm_g", "w_mod", "b_mod", "w_in", "q_g", "k_g", "w_f", "w_o", "final_g"]


def kernel(**inputs):
    import numpy as np
    import concourse.bacc as bacc
    from concourse.bass_utils import run_bass_kernel_spmd as launch

    nc = bacc.Bacc("TRN2", target_bir_lowering=False, num_devices=1)
    arrays = {name: np.ascontiguousarray(inputs[name]) for name in _INS}
    arrays.update(constants())
    d = {}
    feeds = {}
    for name, a in arrays.items():
        feeds[f"in_{name}"] = a
        d[name] = nc.dram_tensor(f"in_{name}", a.shape, mybir.dt.from_np(a.dtype), kind="ExternalInput").ap()
    d["out"] = nc.dram_tensor("out_x", (1, SEQ, D), F32, kind="ExternalOutput").ap()
    build(nc, d)
    r = launch(nc, [feeds], core_ids=[0])
    return r.results[0]["out_x"]
```

```python
import concourse.bass as bass
from concourse import mybir
from contextlib import ExitStack

F32 = mybir.dt.float32
F32R = mybir.dt.float32r
ALU = mybir.AluOpType
ACT = mybir.ActivationFunctionType
X_AXIS = mybir.AxisListType.X

P = 128
D = 1024
KD = D // P
SEQ = 2048
CTX = 256
TT = SEQ // P
KEYS = SEQ + CTX
KT = KEYS // P
HD = 64
HQ = 8
HKV = 2
HN = HQ + HKV
ATTN_W = HQ * HD
KV_W = HKV * HD
QKV_W = ATTN_W + 2 * KV_W
GA0 = QKV_W
F0 = GA0 + ATTN_W
FOUR_W = 512
GF0 = F0 + FOUR_W
GROUPS = 4
REST_W = ATTN_W + 2 * FOUR_W
MT = REST_W // P
QB = 512
NQB = SEQ // QB
NB = HQ * NQB
EPS = 1e-6
RADIX = 4
SUB = SEQ // RADIX
SUBT = SUB // P
CH = 2 * P
NCH = REST_W // CH
M_ORDER = (4, 5, 6, 7, 0, 1, 2, 3, 8, 9, 10, 11)
C_ORDER = tuple(m // 2 for m in M_ORDER[::2])


def split_matmul(pe, out, lhs_hi, lhs_lo, rhs_hi, rhs_lo, first, last):
    pe.matmul(out, lhs_hi, rhs_hi, start=first, stop=False)
    pe.matmul(out, lhs_hi, rhs_lo, start=False, stop=False)
    return pe.matmul(out, lhs_lo, rhs_hi, start=False, stop=last)


def x_squares(nc, act, k, s, slot, loads):
    act.wait_ge(k.s_x[slot], 16 * loads)
    if not isinstance(s, int) or s:
        act.wait_ge(k.s_sum, s)
    nc.scalar.activation(k.square[:, 0, :], k.x[slot][:, 0, :], ACT.Square, accum_out=k.stat[slot][:, 0:1])
    nc.scalar.activation(k.square[:, 1, :], k.x[slot][:, 1, :], ACT.Square,
                         accum_out=k.stat[slot][:, 1:2]).then_inc(k.s_sum, 1)


def x_rstd(nc, pool, k, s, slot):
    pool.wait_ge(k.s_eps, s + 1)
    nc.gpsimd.tensor_tensor(k.rstd[slot][:], k.stat_eps[slot][:], k.minus_half[:, 0:2], ALU.pow).then_inc(k.s_rstd, 1)


def x_norm(nc, dve, k, s, slot):
    dve.wait_ge(k.s_sum, s + 1)
    nc.vector.tensor_scalar(k.stat_eps[slot][:], k.stat[slot][:], 1.0 / D, EPS, ALU.mult, ALU.add).then_inc(k.s_eps, 1)
    dve.wait_ge(k.s_rstd, s + 1)
    for e in range(2):
        last = nc.vector.tensor_scalar(k.x[slot][:, e, :], k.x[slot][:, e, :], k.rstd[slot][:, e:e + 1], None,
                                       ALU.mult)
    last.then_inc(k.s_xhat, 1)


def modulation(nc, k, d):
    with ExitStack() as ctx:
        def sb(name, shape, dt=F32):
            return ctx.enter_context(nc.sbuf_tensor(name, shape, dt))

        HALF_D = D // 2
        w_mod = [sb(f"w_mod{g}", [P, KD, D]) for g in range(2)]
        cond = sb("cond", [P, 2, KD])
        cond_act = sb("cond_act", [P, KD, 2])
        cond_rep = sb("cond_rep", [P, KD, P])
        mod_row = [buf[0:2, h * HALF_D:(h + 1) * HALF_D] for buf in (k.gate_bc, k.final_bc) for h in range(2)]
        mod_bias = sb("mod_bias", [P, 2, KD])
        norm_col = sb("norm_col", [P, KD])
        gate_bias = sb("gate_bias", [1, D])
        ones_row = sb("ones_row", [1, P])
        w_raw = w_mod[1][:, :, 0:QKV_W]
        col_ps = ctx.enter_context(nc.psum_tensor("col_ps", [P, 2, KD, 2], F32))
        row_ps = [ctx.enter_context(nc.psum_tensor(f"row_ps{i}", [P, 512], F32)) for i in range(6)]
        S = k.sem
        s_mod = [S(f"w_mod_loaded{i}") for i in range(4)]
        s_gate_in = [S("w_gate_loaded0"), S("w_gate_loaded1")]
        s_cond_in, s_small, s_row_in = S("cond_loaded"), S("small_loaded"), S("gate_bias_loaded")
        s_head_in, s_final_in = S("head_gains_loaded"), S("final_gain_loaded")
        WCH = 4
        s_wqkv = [S(f"wqkv_loaded{i}") for i in range(WCH)]
        s_whi, s_wlo = S("wqkv_hi_ready"), S("wqkv_lo_ready")
        s_cond, s_rep, s_ones = S("cond_ready"), S("cond_rep_ready"), S("ones_ready")
        s_mrow, s_mrow_sb, s_cols = S("mod_rows_done"), S("mod_rows_copied"), S("mod_cols_done")
        s_gate_ps = S("gate_rows_done")
        s_scale, s_gated, s_end = S("scale_biased"), S("shift_ready"), S("modulation_copied")
        s_hrow, s_half = S("head_gains_scaled"), S("minus_half_set")
        w_mod_v = d["w_mod"][0].rearrange("(k p) (g h n) -> g h p k n", p=P, g=3, h=2)
        b_mod_v = d["b_mod"][0].rearrange("(g k p) -> p g k", p=P, g=3)
        w_qkv_v = d["w_in"][0][:, 0:QKV_W].rearrange("(k p) n -> p k n", p=P)

        def rows(i):
            return slice(i * KD // WCH, (i + 1) * KD // WCH)

        block = ctx.enter_context(nc.Block())

        @block.sync
        def _(sp):
            with nc.allow_non_contiguous_dma(reason="small vectors laid out one element per partition"):
                sp.dma_start(cond[:, 0, :], d["c"][0].rearrange("(k p) -> p k", p=P)).then_inc(s_cond_in, 16)
                sp.dma_start(cond[:, 1, :], d["c_ctx"].rearrange("(k p) -> p k", p=P)).then_inc(s_cond_in, 16)
                for i in range(4):
                    g, h = divmod(i, 2)
                    sp.dma_start(w_mod[g][:, :, h * HALF_D:(h + 1) * HALF_D], w_mod_v[g][h]).then_inc(s_mod[i], 16)
                sp.dma_start(k.ident[:], d["ident"]).then_inc(s_small, 16)
                for g in range(2):
                    sp.dma_start(mod_bias[:, g, :], b_mod_v[:, g, :]).then_inc(s_small, 16)
                sp.dma_start(norm_col[:], d["norm_g"][0].rearrange("(k p) -> p k", p=P)).then_inc(s_small, 16)
            sp.dma_start(gate_bias[:], d["b_mod"][0:1, 2 * D:3 * D]).then_inc(s_row_in, 16)
            for h in range(HN):
                gain = d["q_g"] if h < HQ else d["k_g"]
                sp.dma_start(k.head_bc[:, h * HD:(h + 1) * HD], gain[0].partition_broadcast(P)).then_inc(s_head_in, 16)
            for h in range(2):
                sp.wait_ge(s_mrow, h + 1)
                sp.dma_start(w_mod[0][:, :, h * HALF_D:(h + 1) * HALF_D], w_mod_v[2][h]).then_inc(s_gate_in[h], 16)
            sp.dma_start(k.x[0][:], d["ctx"][0].rearrange("(t p) n -> p t n", p=P)).then_inc(k.s_x[0], 16)
            sp.dma_start(k.x[1][:], d["x"][0].rearrange("(s t p) n -> s p t n", t=2, p=P)[0]).then_inc(k.s_x[1], 16)
            sp.wait_ge(s_mrow, 4)
            for i in range(WCH):
                sp.dma_start(w_raw[:, rows(i), :], w_qkv_v[:, rows(i), :]).then_inc(s_wqkv[i], 16)
            sp.wait_ge(s_cols, 1)
            sp.dma_start(k.final_bc[:], d["final_g"].partition_broadcast(P)).then_inc(s_final_in, 16)
            sp.wait_ge(s_final_in, 16)

        @block.gpsimd
        def _(pool):
            nc.gpsimd.memset(k.minus_half[:], -0.5).then_inc(s_half, 1)
            pool.wait_ge(s_half, 1)
            x_rstd(nc, pool, k, 0, 0)
            x_rstd(nc, pool, k, 1, 1)

        @block.scalar
        def _(act):
            act.wait_ge(s_cond_in, 32)
            nc.scalar.activation(cond_act[:].rearrange("p k c -> p c k"), cond[:], ACT.Silu).then_inc(s_cond, 1)
            act.wait_ge(s_cond, 1)
            nc.scalar.activation(cond_rep[:], cond_act[:, :, 0:1].broadcast_to([P, KD, P]),
                                 ACT.Copy).then_inc(s_rep, 1)
            for i in range(4):
                act.wait_ge(s_mrow, i + 1)
                nc.scalar.activation(mod_row[i], row_ps[i][0:2, :], ACT.Copy).then_inc(s_mrow_sb, 1)
            x_squares(nc, act, k, 0, 0, 1)
            x_squares(nc, act, k, 1, 1, 1)
            for i in range(WCH):
                act.wait_ge(s_wqkv[i], 16)
                nc.scalar.activation(k.wqkv_hi[:, rows(i), :], w_raw[:, rows(i), :], ACT.Copy).then_inc(s_whi, 1)
            act.wait_ge(s_gate_ps, 2)
            for i in range(2):
                last = nc.scalar.activation(k.gate_bc[:, i * 512:(i + 1) * 512], row_ps[4 + i][:], ACT.Copy)
            last.then_inc(s_end, 1)
            act.wait_ge(s_end, 1)

        @block.vector
        def _(dve):
            nc.vector.memset(ones_row[:], 1.0).then_inc(s_ones, 1)
            nc.vector.memset(k.ones_sq[:].bitcast(F32), 1.0)
            nc.vector.memset(k.zero_one[:, 0:HD].bitcast(F32), 0.0)
            nc.vector.memset(k.zero_one[:, HD:P].bitcast(F32), 1.0)
            nc.vector.memset(k.k_lo1[HD:HD + 1, :, :].bitcast(F32), 1.0)
            dve.wait_ge(s_head_in, 16 * HN)
            nc.vector.tensor_scalar(k.head_bc[:, 0:ATTN_W], k.head_bc[:, 0:ATTN_W], HD ** -0.5, None,
                                    ALU.mult).then_inc(s_hrow, 1)
            x_norm(nc, dve, k, 0, 0)
            dve.wait_ge(s_small, 16 * 4)
            dve.wait_ge(s_cols, 1)
            for side in range(2):
                nc.vector.tensor_tensor(k.shift[:, side, :], col_ps[:, 0, :, side], mod_bias[:, 0, :], ALU.add)
                last = nc.vector.tensor_tensor(k.scale[:, side, :], col_ps[:, 1, :, side], mod_bias[:, 1, :],
                                               ALU.add)
            last.then_inc(s_scale, 1)
            dve.wait_ge(s_scale, 1)
            for side in range(2):
                last = nc.vector.scalar_tensor_tensor(k.scale[:, side, :], k.scale[:, side, :], 1.0, norm_col[:],
                                                      ALU.add, ALU.mult)
            last.then_inc(s_gated, 1)
            x_norm(nc, dve, k, 1, 1)
            for i in range(WCH):
                dve.wait_ge(s_whi, i + 1)
                nc.vector.tensor_tensor(k.wqkv_lo[:, rows(i), :], w_raw[:, rows(i), :],
                                        k.wqkv_hi[:, rows(i), :].bitcast(F32), ALU.subtract).then_inc(s_wlo, 1)
            dve.wait_ge(s_gated, 1)
            dve.wait_ge(s_wlo, WCH)
            dve.wait_ge(s_hrow, 1)

        @block.tensor
        def _(pe):
            pe.wait_ge(s_cond, 1)
            for i in range(4):
                g, h = divmod(i, 2)
                pe.wait_ge(s_mod[i], 16)
                for c in range(KD):
                    last = nc.tensor.matmul(row_ps[i][0:2, :], cond_act[:, c, :],
                                            w_mod[g][:, c, h * HALF_D:(h + 1) * HALF_D], start=(c == 0),
                                            stop=(c == KD - 1))
                last.then_inc(s_mrow, 1)
            pe.wait_ge(s_small, 16 * 4)
            pe.wait_ge(s_mrow_sb, 4)
            for i in range(4):
                g, h = divmod(i, 2)
                for f in range(KD // 2):
                    last = nc.tensor.transpose(col_ps[:, g, h * (KD // 2) + f, :], mod_row[i][:, f * P:(f + 1) * P],
                                               k.ident[0:2, 0:2])
            last.then_inc(s_cols, 1)
            pe.wait_ge(s_ones, 1)
            pe.wait_ge(s_row_in, 16)
            pe.wait_ge(s_rep, 1)
            for i in range(2):
                pe.wait_ge(s_gate_in[i], 16)
                nc.tensor.matmul(row_ps[4 + i][:], ones_row[:], gate_bias[:, i * 512:(i + 1) * 512],
                                 start=True, stop=False)
                for c in range(KD):
                    last_gate = nc.tensor.matmul(row_ps[4 + i][:], cond_rep[:, c, :],
                                                 w_mod[0][:, c, i * 512:(i + 1) * 512],
                                                 start=False, stop=(c == KD - 1))
                last_gate.then_inc(s_gate_ps, 1)


def project_qkv(nc, k, d):
    with ExitStack() as ctx:
        def sb(name, shape, dt=F32):
            return ctx.enter_context(nc.sbuf_tensor(name, shape, dt))

        def ps(name, shape):
            return ctx.enter_context(nc.psum_tensor(name, shape, F32))

        W = 2 * P
        x = k.x
        h = sb("h", [P, KD, W])
        h_hi = [sb(f"h_hi{i}", [P, KD, W], F32R) for i in range(2)]
        h_lo = [sb(f"h_lo{i}", [P, KD, W], F32R) for i in range(2)]
        qkv = [sb(f"qkv{i}", [P, QKV_W]) for i in range(2)]
        qk_sq = sb("qk_sq", [P, HN, HD])
        qk_g = sb("qk_g", [P, HN, HD])
        qk_n = sb("qk_n", [P, HN, HD])
        qk_sin = sb("qk_sin", [P, HN, HD])
        qk_rot = sb("qk_rot", [P, HN, 2, HD])
        hstat = sb("hstat", [P, HN])
        hrstd = sb("hrstd", [P, HN])
        cos_t = [sb(f"cos{i}", [P, 2, HD]) for i in range(2)]
        sin_t = [sb(f"sin{i}", [P, 2, HD]) for i in range(2)]
        q_hilo = [sb(f"q_hilo{i}", [P, HQ, P], F32R) for i in range(2)]
        xt_ps = [ps(f"xt_ps{i}", [P, 2, W]) for i in range(2)]
        q_ps = ps("q_ps", [P, ATTN_W])
        kv_ps = ps("kv_ps", [P, 2 * KV_W])
        tr_ps = [ps(f"tr_ps{i}", [P, 4, P]) for i in range(3)]

        S = k.sem
        s_x, s_xhat = k.s_x, k.s_xhat
        s_table = [S("rope_loaded0"), S("rope_loaded1")]
        s_xt, s_h, s_hhi, s_hsplit = S("x_transposed"), S("h_ready"), S("h_hi_ready"), S("h_split")
        s_qp, s_kvp, s_qc, s_kvc = S("q_projected"), S("kv_projected"), S("q_copied"), S("kv_copied")
        s_sq, s_hsum, s_hmean, s_hrstd = S("head_squares"), S("head_sums"), S("head_means"), S("head_rstd_ready")
        s_g, s_n, s_c, s_r, s_dup = (S("head_gained"), S("head_normed"), S("rope_multiplied"), S("head_rotated"),
                                     S("head_doubled"))
        s_tr, s_trhi, s_trlo = S("qk_transposed"), S("qk_hi_ready"), S("qk_lo_ready")
        s_vhi, s_v = S("v_hi_ready"), S("v_ready")
        s_qst = [S("q_stored0"), S("q_stored1")]
        s_hst = [S("h_stored0"), S("h_stored1")]
        x_v = d["x"][0].rearrange("(s t p) n -> s p t n", t=2, p=P)
        cos_v = d["cos"].rearrange("(s t p) n -> s p t n", t=2, p=P)
        sin_v = d["sin"].rearrange("(s t p) n -> s p t n", t=2, p=P)
        q_v = k.q_dram.rearrange("(h b) p q -> b p h q", b=NQB)
        h_v = k.h_dram.rearrange("e k p (s t) -> s e p k t", t=W)
        PAIR_N = TT // 2

        def run(engine, window):
            window(1, 1, 0)
            with engine.Fori(0, (PAIR_N - 4) // 2) as i:
                window(i * 2 + 2, 0, i + 1)
                window(i * 2 + 3, 1, i + 1)
            for s in range(PAIR_N - 2, PAIR_N + 2):
                window(s, s % 2, s // 2)

        def exists(s):
            return not isinstance(s, int) or s <= PAIR_N

        def heads(is_ctx):
            return (HQ, HN) if is_ctx else (0, HN)

        block = ctx.enter_context(nc.Block())

        @block.sync
        def _(sp):
            def load_x(s, slot):
                sp.dma_start(x[slot][:], x_v[s - 1]).then_inc(s_x[slot], 16)

            def load_tables(s, slot):
                sp.dma_start(cos_t[slot][:], cos_v[s - 1]).then_inc(s_table[slot], 16)
                sp.dma_start(sin_t[slot][:], sin_v[s - 1]).then_inc(s_table[slot], 16)

            def store_h(s, slot):
                sp.wait_ge(s_hsplit, s + 1)
                sp.dma_start(h_v[s - 1][0], h_hi[slot][:].bitcast(F32)).then_inc(s_hst[slot], 16)
                sp.dma_start(h_v[s - 1][1], h_lo[slot][:].bitcast(F32)).then_inc(s_hst[slot], 16)

            def store_q(t, slot, blk, tau):
                sp.wait_ge(s_trlo, t + 1)
                sp.dma_start(q_v[blk][:, :, tau * P:(tau + 1) * P], q_hilo[slot][:].bitcast(F32)).then_inc(s_qst[slot], 16)

            load_tables(1, 1)
            sp.wait_ge(s_xt, 4)
            load_x(2, 0)
            sp.wait_ge(s_xt, 8)
            load_x(3, 1)
            store_h(1, 1)

            def window(s, par, m):
                if exists(s + 1):
                    sp.wait_ge(s_c, s * 2)
                    load_tables(s + 1, 1 - par)
                if exists(s + 3):
                    sp.wait_ge(s_xt, s * 4 + 8)
                    load_x(s + 3, 1 - par)
                latent = not (isinstance(s, int) and s == 1)
                if latent:
                    store_q(s * 2 - 2, 0, m - 1, 2 * par)
                if exists(s + 1):
                    store_h(s + 1, 1 - par)
                if latent:
                    store_q(s * 2 - 1, 1, m - 1, 2 * par + 1)

            run(sp, window)
            for slot in range(2):
                sp.wait_ge(s_qst[slot], 16 * (TT // 2 + 1))
                sp.wait_ge(s_hst[slot], 32 * (TT // 4 + 1))

        @block.gpsimd
        def _(pool):
            def head_gain(t, slot, is_ctx=False):
                h0, h1 = heads(is_ctx)
                pool.wait_ge(s_qc, t + 1)
                pool.wait_ge(s_kvc, t + 1)
                if not is_ctx or t:
                    pool.wait_ge(s_n, t)
                nc.gpsimd.tensor_tensor(qk_g[:, h0:h1, :].rearrange("p h d -> p (h d)"),
                                        qkv[slot][:, h0 * HD:h1 * HD], k.head_bc[:, h0 * HD:h1 * HD],
                                        ALU.mult).then_inc(s_g, 1)
                pool.wait_ge(s_hmean, t + 1)
                nc.gpsimd.tensor_tensor(hrstd[:, h0:h1], hstat[:, h0:h1], k.minus_half[:, h0:h1],
                                        ALU.pow).then_inc(s_hrstd, 1)

            x_rstd(nc, pool, k, 2, 0)
            head_gain(0, 0, True)

            def window(s, par, m):
                head_gain(s * 2 - 1, 1, isinstance(s, int) and s == 1)
                if exists(s + 2):
                    x_rstd(nc, pool, k, s + 2, par)
                if exists(s):
                    head_gain(s * 2, 0)

            run(pool, window)

        @block.scalar
        def _(act):
            act.sem_inc(s_qst[0], 16)
            act.sem_inc(s_qst[1], 16)
            act.sem_inc(s_h, 2)

            def h_evacuate(s, side, units):
                if side == 0 and units[0] == 0:
                    act.wait_ge(s_hsplit, s)
                for u in units:
                    act.wait_ge(s_xt, s * 4 + (u + 1))
                    for e in range(2):
                        f = 2 * u + e
                        last = nc.scalar.activation(h[:, f, :], xt_ps[u % 2][:, e, :], ACT.Identity,
                                                    scale=k.scale[:, side, f:f + 1], bias=k.shift[:, side, f:f + 1])
                    last.then_inc(s_h, 1)

            def copy_q(t, slot):
                act.wait_ge(s_g, t - 1)
                act.wait_ge(s_v, t - 1)
                act.wait_ge(s_qp, t + 1)
                nc.scalar.activation(qkv[slot][:, 0:ATTN_W], q_ps[:], ACT.Copy).then_inc(s_qc, 1)

            def copy_kv(t, slot, is_ctx=False):
                h0, h1 = heads(is_ctx)
                if is_ctx:
                    act.sem_inc(s_qc, 1)
                act.wait_ge(s_kvp, t + 1)
                nc.scalar.activation(qkv[slot][:, ATTN_W:QKV_W], kv_ps[:], ACT.Copy).then_inc(s_kvc, 1)
                act.wait_ge(s_kvc, t + 1)
                if not is_ctx:
                    act.wait_ge(s_qc, t + 1)
                if not is_ctx or t:
                    act.wait_ge(s_hsum, t)
                nc.scalar.activation(qk_sq[:, h0:h1, :].rearrange("p h d -> p (h d)"),
                                     qkv[slot][:, h0 * HD:h1 * HD], ACT.Square).then_inc(s_sq, 1)

            def double_heads(t, is_ctx=False):
                h0, h1 = heads(is_ctx)
                act.wait_ge(s_r, t + 1)
                nc.scalar.activation(qk_rot[:, h0:h1, 1, :], qk_rot[:, h0:h1, 0, :], ACT.Copy).then_inc(s_dup, 1)

            def qk_hi(t, slot, key0, uses=None):
                act.wait_ge(s_tr, t + 1)
                if uses is not None:
                    act.wait_ge(s_qst[slot], uses * 16)
                    nc.scalar.activation(q_hilo[slot][:, 0:4, :], tr_ps[0][:], ACT.Copy)
                    nc.scalar.activation(q_hilo[slot][:, 4:8, :], tr_ps[1][:], ACT.Copy)
                nc.scalar.activation(k.k_hi2[:, :, bass.ds(key0, P)], tr_ps[2][:, 0:HKV, :],
                                     ACT.Copy).then_inc(s_trhi, 1)

            h_evacuate(0, 1, range(4))
            h_evacuate(1, 0, range(4))
            x_squares(nc, act, k, 2, 0, 2)
            copy_kv(0, 0, True)
            copy_kv(1, 1, True)

            def window(s, par, m):
                is_ctx = isinstance(s, int) and s == 1
                uses = None if is_ctx else s - 1
                key0 = SEQ if is_ctx else (s - 2) * (2 * P)
                if exists(s + 1):
                    h_evacuate(s + 1, 0, (0, 1))
                double_heads(s * 2 - 2, is_ctx)
                if exists(s + 2):
                    x_squares(nc, act, k, s + 2, par, m + 2)
                if exists(s):
                    copy_q(s * 2, 0)
                qk_hi(s * 2 - 2, 0, key0, uses)
                if exists(s + 1):
                    h_evacuate(s + 1, 0, (2, 3))
                double_heads(s * 2 - 1, is_ctx)
                if exists(s):
                    copy_kv(s * 2, 0)
                    copy_q(s * 2 + 1, 1)
                qk_hi(s * 2 - 1, 1, key0 + P, uses)
                if exists(s):
                    copy_kv(s * 2 + 1, 1)

            run(act, window)

        @block.vector
        def _(dve):
            dve.sem_inc(s_hst[0], 32)
            dve.sem_inc(s_hst[1], 32)

            def h_split(s, slot, uses=None, s_prev_tiles=None):
                dve.wait_ge(s_h, s * 4 + 6)
                if uses is not None:
                    dve.wait_ge(s_hst[slot], uses * 32)
                if s_prev_tiles is not None:
                    dve.wait_ge(s_kvp, s_prev_tiles)
                nc.vector.tensor_copy(h_hi[slot][:], h[:]).then_inc(s_hhi, 1)
                dve.wait_ge(s_hhi, s + 1)
                nc.vector.tensor_tensor(h_lo[slot][:], h[:], h_hi[slot][:].bitcast(F32), ALU.subtract).then_inc(s_hsplit, 1)

            def head_norm(t, slot, key_tile, rope=None):
                is_ctx = rope is None
                h0, h1 = heads(is_ctx)
                n = h1 - h0
                dve.wait_ge(s_kvc, t + 1)
                v = qkv[slot][:, ATTN_W + KV_W:QKV_W].rearrange("p (h d) -> p h d", h=HKV)
                v_hl = k.v_hl[:, bass.ds(key_tile, 1), :, :].rearrange("p a h d -> p (a h) d")
                nc.vector.tensor_copy(v_hl[:, :, 0:HD], v).then_inc(s_vhi, 1)
                dve.wait_ge(s_sq, t + 1)
                if not is_ctx or t:
                    dve.wait_ge(s_hrstd, t)
                nc.vector.reduce_sum(hstat[:, h0:h1], qk_sq[:, h0:h1, :], X_AXIS).then_inc(s_hsum, 1)
                dve.wait_ge(s_vhi, t + 1)
                nc.vector.tensor_tensor(v_hl[:, :, HD:P], v, v_hl[:, :, 0:HD].bitcast(F32), ALU.subtract).then_inc(s_v, 1)
                dve.wait_ge(s_hsum, t + 1)
                nc.vector.tensor_scalar(hstat[:, h0:h1], hstat[:, h0:h1], 1.0 / HD, EPS, ALU.mult,
                                        ALU.add).then_inc(s_hmean, 1)
                dve.wait_ge(s_g, t + 1)
                dve.wait_ge(s_hrstd, t + 1)
                if is_ctx:
                    if t:
                        dve.wait_ge(s_tr, t)
                    dve.sem_inc(s_c, 1)
                    nc.vector.tensor_tensor(qk_rot[:, h0:h1, 0, :], qk_g[:, h0:h1, :],
                                            hrstd[:, h0:h1].unsqueeze(2).broadcast_to([P, n, HD]),
                                            ALU.mult).then_inc(s_n, 1)
                    dve.wait_ge(s_n, t + 1)
                    dve.sem_inc(s_r, 1)
                    return
                nc.vector.tensor_tensor(qk_n[:], qk_g[:], hrstd[:].unsqueeze(2).broadcast_to([P, HN, HD]),
                                        ALU.mult).then_inc(s_n, 1)
                tslot, e, loads = rope
                dve.wait_ge(s_table[tslot], loads * 32)
                dve.wait_ge(s_n, t + 1)
                nc.vector.tensor_tensor(qk_sin[:], qk_n[:], sin_t[tslot][:, e:e + 1, :].broadcast_to([P, HN, HD]), ALU.mult)
                nc.vector.tensor_tensor(qk_n[:], qk_n[:], cos_t[tslot][:, e:e + 1, :].broadcast_to([P, HN, HD]),
                                        ALU.mult).then_inc(s_c, 1)
                dve.wait_ge(s_c, t + 1)
                dve.wait_ge(s_tr, t)
                def half(buf, n_half):
                    return buf.rearrange("p h (a f) -> p h a f", a=2)[:, :, :, n_half * HD // 4:(n_half + 1) * HD // 4]
                rot = qk_rot[:, :, 0, :]
                nc.vector.tensor_tensor(half(rot, 0), half(qk_n[:], 0), half(qk_sin[:], 1), ALU.subtract)
                nc.vector.tensor_tensor(half(rot, 1), half(qk_n[:], 1), half(qk_sin[:], 0), ALU.add).then_inc(s_r, 1)

            def qk_lo(t, slot, key0, is_ctx=False):
                dve.wait_ge(s_trhi, t + 1)
                if not is_ctx:
                    for g in range(2):
                        lo = q_hilo[slot][HD:P, 4 * g:4 * g + 4, :]
                        nc.vector.tensor_tensor(lo, tr_ps[g][HD:P], lo.bitcast(F32), ALU.subtract)
                nc.vector.tensor_tensor(k.k_lo1[0:HD, :, bass.ds(key0, P)], tr_ps[2][0:HD, 0:HKV, :],
                                        k.k_hi2[0:HD, :, bass.ds(key0, P)].bitcast(F32), ALU.subtract).then_inc(s_trlo, 1)

            h_split(0, 0)
            h_split(1, 1, 1)
            x_norm(nc, dve, k, 2, 0)
            head_norm(0, 0, TT)

            def window(s, par, m):
                if isinstance(s, int) and s == 1:
                    head_norm(1, 1, TT + 1)
                    qk_lo(0, 0, SEQ, True)
                else:
                    head_norm(s * 2 - 1, 1, s * 2 - 3, (1 - par, 1, m))
                    qk_lo(s * 2 - 2, 0, (s - 2) * (2 * P))
                if exists(s + 2):
                    x_norm(nc, dve, k, s + 2, par)
                if exists(s + 1):
                    h_split(s + 1, 1 - par, m + 1, s * 2)
                if exists(s):
                    head_norm(s * 2, 0, s * 2 - 2, (par, 0, m + par))
                if isinstance(s, int) and s == 1:
                    qk_lo(1, 1, SEQ + P, True)
                else:
                    qk_lo(s * 2 - 1, 1, (s - 2) * (2 * P) + P)

            run(dve, window)

        @block.tensor
        def _(pe):
            def x_transpose(s, slot, units):
                pe.wait_ge(s_xhat, s + 1)
                for u in units:
                    pe.wait_ge(s_h, s * 4 + (u + 1))
                    for e in range(2):
                        for t in range(2):
                            f = 2 * u + e
                            last = nc.tensor.transpose(xt_ps[u % 2][:, e, t * P:(t + 1) * P],
                                                       x[slot][:, t, f * P:(f + 1) * P], k.ident[:])
                    last.then_inc(s_xt, 1)

            def project_q(s, t, slot, e):
                pe.wait_ge(s_hsplit, s + 1)
                pe.wait_ge(s_qc, t)
                hs = slice(e * P, (e + 1) * P)
                for c in range(KD):
                    last = split_matmul(nc.tensor, q_ps[:], h_hi[slot][:, c, hs], h_lo[slot][:, c, hs],
                                        k.wqkv_hi[:, c, 0:ATTN_W], k.wqkv_lo[:, c, 0:ATTN_W], c == 0, c == KD - 1)
                last.then_inc(s_qp, 1)

            def project_kv(s, t, slot, e):
                pe.wait_ge(s_hsplit, s + 1)
                if not isinstance(t, int) or t:
                    pe.wait_ge(s_kvc, t)
                hs = slice(e * P, (e + 1) * P)
                for c in range(KD):
                    last = split_matmul(nc.tensor, kv_ps[:], h_hi[slot][:, c, hs], h_lo[slot][:, c, hs],
                                        k.wqkv_hi[:, c, ATTN_W:QKV_W], k.wqkv_lo[:, c, ATTN_W:QKV_W],
                                        c == 0, c == KD - 1)
                last.then_inc(s_kvp, 1)

            def head_transpose(t, is_ctx=False):
                pe.wait_ge(s_dup, t + 1)
                if not is_ctx or t:
                    pe.wait_ge(s_trlo, t)
                for hh in range(*heads(is_ctx)):
                    last = nc.tensor.transpose(tr_ps[hh // 4][:, hh % 4, :],
                                               qk_rot[:, hh, :, :].rearrange("p e d -> p (e d)"), k.ident[:])
                last.then_inc(s_tr, 1)

            pe.sem_inc(s_qp, 2)
            x_transpose(0, 0, range(4))
            x_transpose(1, 1, range(4))
            for e in range(2):
                project_kv(0, e, 0, e)

            def window(s, par, m):
                is_ctx = isinstance(s, int) and s == 1
                if exists(s + 1):
                    x_transpose(s + 1, 1 - par, (0, 1))
                if exists(s):
                    project_q(s, s * 2, par, 0)
                head_transpose(s * 2 - 2, is_ctx)
                if exists(s + 1):
                    x_transpose(s + 1, 1 - par, (2, 3))
                if exists(s):
                    project_kv(s, s * 2, par, 0)
                    project_q(s, s * 2 + 1, par, 1)
                head_transpose(s * 2 - 1, is_ctx)
                if exists(s):
                    project_kv(s, s * 2 + 1, par, 1)

            run(pe, window)


MAX_CHUNKS = [512, 512, 512, 512, 256]
MAX_USES = QB // P * len(MAX_CHUNKS)
MAX_AT = (4, 4, 3, 4, 3, 2, 0, 0, 0)
LO_AFTER = (2, 0, 1, 0, 1, 0, 0, 0, 0)
MAX_ROW_AT = 6
PAIRS = KT // 2
POOL_LO = (0, 2, 4, 6)


def attention(nc, k, d):
    with ExitStack() as ctx:
        def sb(name, shape, dt=F32):
            return ctx.enter_context(nc.sbuf_tensor(name, shape, dt))

        def ps(name, shape):
            return ctx.enter_context(nc.psum_tensor(name, shape, F32))

        q_hilo = [sb(f"blk_q_hilo{i}", [P, QB], F32R) for i in range(2)]
        q_negm = [sb(f"blk_q_negm{i}", [P, QB], F32R) for i in range(2)]
        chunk_max = sb("chunk_max", [P, QB // P, len(MAX_CHUNKS)])
        neg_max = sb("neg_max", [P, QB // P])
        diag = sb("diag", [P, QB], F32R)
        prob = [sb(f"prob{i}", [P, 2 * QB]) for i in range(3)]
        prob_hi = [sb(f"prob_hi{i}", [P, 2 * QB], F32R) for i in range(3)]
        prob_lo = [sb(f"prob_lo{i}", [P, 2 * QB], F32R) for i in range(3)]
        v_one = sb("v_one", [P, KT, HKV, P], F32R)
        part = sb("part", [HD, QB])
        hi_sum = sb("hi_sum", [P, QB])
        lo_sum = [sb(f"lo_sum{i}", [HD + 1, QB]) for i in range(2)]
        att = [sb(f"att{i}", [HD, QB]) for i in range(2)]
        max_ps = [ps(f"max_ps{i}", [P, QB]) for i in range(2)]
        s_ps = [ps(f"s_ps{i}", [P, 2 * QB]) for i in range(2)]
        hi_ps = ps("hi_ps", [P, QB])
        lo_ps = ps("lo_ps", [P, QB])

        S = k.sem
        s_q = [S("blk_q_loaded0"), S("blk_q_loaded1")]
        s_mfull, s_mfree = S("max_bank_full"), S("max_bank_free")
        s_vone = S("v_one_ready")
        s_neg, s_diag = S("neg_max_done"), S("diag_ready")
        s_score, s_exp = S("scores_ready"), S("scores_exponentiated")
        s_lo_dve, s_lo_pool = S("prob_lo_dve"), S("prob_lo_pool")
        s_pv, s_hisum, s_losum = S("pv_done"), S("hi_sum_copied"), S("lo_sum_copied")
        s_part, s_add, s_att = S("v_lo_part_moved"), S("first_att_sum"), S("att_ready")
        s_st = [S("att_stored0"), S("att_stored1")]
        att_v, den_v, q_v = k.att_dram, k.den_dram, k.q_dram

        HALF = NB // HKV
        N_IT = HALF // 2

        def run(engine, body):
            for kvh in range(HKV):
                with engine.Fori(0, N_IT - 1) as i:
                    body(i * 2 + HALF * kvh, 0, kvh, kvh)
                    body(i * 2 + (HALF * kvh + 1), 1, kvh, kvh)
                body(HALF * kvh + HALF - 2, 0, kvh, kvh)
                body(HALF * kvh + HALF - 1, 1, kvh, kvh + 1 if kvh + 1 < HKV else None)

        def slot2(slot, j):
            return (slot * PAIRS + j) % 2

        def slot3(j):
            return j % 3

        block = ctx.enter_context(nc.Block())

        @block.sync
        def _(sp):
            def load(b, slot):
                sp.dma_start(q_hilo[slot][:].bitcast(F32), q_v[b]).then_inc(s_q[slot], 16)
                sp.dma_start(q_negm[slot][0:HD, :].bitcast(F32), q_v[b][0:HD, :]).then_inc(s_q[slot], 16)

            load(0, 0)
            load(1, 1)
            for c in range(2):
                sp.dma_start(k.w_raw[c], k.w_rest_v[C_ORDER[c]]).then_inc(k.s_raw[c], 16)
            sp.dma_start(k.hh0[:].bitcast(F32), k.h_v[0][0]).then_inc(k.s_hh[0], 16)
            sp.dma_start(k.hl0[:].bitcast(F32), k.h_v[0][1]).then_inc(k.s_hl[0], 16)

            def body(b, slot, kvh, next_kvh):
                sp.wait_ge(s_score, b * PAIRS + PAIRS)
                if next_kvh is not None and not (isinstance(b, int) and b + 2 >= NB):
                    load(b + 2, slot)
                sp.wait_ge(s_att, b + 2)
                sp.dma_start(att_v[b], att[slot][:]).then_inc(s_st[slot], 16)
                sp.wait_ge(s_losum, b + 2)
                sp.dma_start(den_v[b], lo_sum[slot][HD:HD + 1, :]).then_inc(s_st[slot], 16)

            run(sp, body)
            for slot in range(2):
                sp.wait_ge(s_st[slot], 32 * (NB // 2 + 1))

        @block.gpsimd
        def _(pool):
            pool.sem_inc(s_att, 1)
            pool.sem_inc(s_st[0], 32)
            pool.sem_inc(s_st[1], 32)

            def lo(b, j):
                pool.wait_ge(s_exp, b * PAIRS + (j + 3))
                nc.gpsimd.tensor_tensor(prob_lo[slot3(j)][:], prob[slot3(j)][:], prob_hi[slot3(j)][:].bitcast(F32),
                                        ALU.subtract).then_inc(s_lo_pool, 1)

            for n in range(2):
                pool.dma_start(k.w_rest_hi[n][:], k.w_rest_v[C_ORDER[n]]).then_inc(k.s_rest_hi[n], 16)
            lo(0, 0)

            def body(b, slot, kvh, next_kvh):
                for j in POOL_LO[1:]:
                    lo(b, j)
                if next_kvh is not None:
                    lo(b + 1, POOL_LO[0])
                pool.wait_ge(s_hisum, b + 2)
                pool.wait_ge(s_losum, b + 2)
                pool.wait_ge(s_st[slot], (b - slot) * 16 + 32)
                nc.gpsimd.tensor_tensor(att[slot][:], hi_sum[0:HD, :], lo_sum[slot][0:HD, :], ALU.add).then_inc(s_add, 1)
                pool.wait_ge(s_add, b + 1)
                pool.wait_ge(s_part, b + 2)
                nc.gpsimd.tensor_tensor(att[slot][:], att[slot][:], part[:], ALU.add).then_inc(s_att, 1)

            run(pool, body)

        @block.scalar
        def _(act):
            act.sem_inc(s_exp, 2)
            act.sem_inc(s_losum, 1)

            def exponentials(b, slot, j):
                act.wait_ge(s_score, b * PAIRS + (j + 1))
                act.wait_ge(s_pv, b * PAIRS + (j + 1))
                s = s_ps[slot2(slot, j)]
                nc.scalar.activation(prob_hi[slot3(j)][:], s[:], ACT.Exp)
                nc.scalar.activation(prob[slot3(j)][:], s[:], ACT.Exp).then_inc(s_exp, 1)

            def evacuate(b, slot):
                act.wait_ge(s_pv, b * PAIRS + (PAIRS + 3))
                act.wait_ge(s_st[slot], (b - slot) * 16 + 32)
                nc.scalar.activation(lo_sum[slot][:], lo_ps[0:HD + 1, :], ACT.Copy).then_inc(s_losum, 1)

            def move_part(b):
                act.wait_ge(s_hisum, b + 1)
                nc.scalar.activation(part[:], hi_sum[HD:P, :], ACT.Copy).then_inc(s_part, 1)

            exponentials(0, 0, 0)

            def body(b, slot, kvh, next_kvh):
                for j in range(1, PAIRS):
                    exponentials(b, slot, j)
                    if j == 1:
                        move_part(b)
                if next_kvh is not None:
                    exponentials(b + 1, 1 - slot, 0)
                evacuate(b, slot)
                if next_kvh is None:
                    move_part(b + 1)

            run(act, body)

        @block.vector
        def _(dve):
            dve.sem_inc(s_mfree, 2)
            nc.vector.memset(hi_sum[:], 0.0).then_inc(s_hisum, 1)

            def reduce(b, slot, u):
                qt, kc = divmod(u, len(MAX_CHUNKS))
                bank = max_ps[(slot * (MAX_USES + 1) + u) % 2]
                dve.wait_ge(s_mfull, b * (MAX_USES + 1) + (u + 1))
                last = nc.vector.reduce_max(chunk_max[:, qt, kc:kc + 1], bank[:, 0:MAX_CHUNKS[kc]], X_AXIS)
                return last.then_inc(s_mfree, 1)

            def negate(b, slot):
                dve.wait_ge(s_mfree, b * (MAX_USES + 1) + (MAX_USES + 2))
                nc.vector.tensor_reduce(neg_max[:], chunk_max[:], X_AXIS, ALU.max, negate=True).then_inc(s_neg, 1)
                dve.wait_ge(s_neg, b + 1)
                for qt in range(QB // P):
                    last = nc.vector.tensor_scalar(diag[:, qt * P:(qt + 1) * P], k.ident[:], neg_max[:, qt:qt + 1],
                                                   None, ALU.mult)
                last.then_inc(s_diag, 1)

            def max_row(b, slot):
                bank = max_ps[(slot * (MAX_USES + 1) + MAX_USES) % 2]
                dve.wait_ge(s_mfull, b * (MAX_USES + 1) + (MAX_USES + 1))
                dve.wait_ge(s_q[slot], (b - slot) * 16 + 32)
                nc.vector.tensor_copy(q_negm[slot][HD:HD + 1, :], bank[HD:HD + 1, :]).then_inc(s_mfree, 1)

            def lo(b, slot, j):
                if j in POOL_LO:
                    return
                dve.wait_ge(s_exp, b * PAIRS + (j + 3))
                nc.vector.tensor_tensor(prob_lo[slot3(j)][:], prob[slot3(j)][:], prob_hi[slot3(j)][:].bitcast(F32),
                                        ALU.subtract).then_inc(s_lo_dve, 1)

            def evacuate(b, slot):
                dve.wait_ge(s_pv, b * PAIRS + (PAIRS + 3))
                dve.wait_ge(s_att, b + 1)
                nc.vector.tensor_copy(hi_sum[:], hi_ps[:]).then_inc(s_hisum, 1)

            nc.vector.memset(v_one[:, :, :, HD:P].bitcast(F32), 1.0)
            nc.vector.tensor_copy(v_one[:, :, :, 0:HD], k.v_hl[:, :, :, 0:HD].bitcast(F32)).then_inc(s_vone, 1)
            for u in range(MAX_USES):
                reduce(0, 0, u)
            negate(0, 0)
            max_row(0, 0)

            def body(b, slot, kvh, next_kvh):
                u = 0
                for j in range(PAIRS):
                    n_max = MAX_AT[j] if next_kvh is not None else 0
                    for n in range(max(n_max, 1)):
                        if n < n_max:
                            reduce(b + 1, 1 - slot, u)
                            u += 1
                        if n == min(LO_AFTER[j], max(n_max, 1) - 1) and j + 1 < PAIRS:
                            lo(b, slot, j + 1)
                    if n_max and u == MAX_USES:
                        negate(b + 1, 1 - slot)
                    if next_kvh is not None and j == MAX_ROW_AT:
                        max_row(b + 1, 1 - slot)
                evacuate(b, slot)

            run(dve, body)

        @block.tensor
        def _(pe):
            pe.sem_inc(s_pv, 3)

            def max_use(b, slot, kvh, u):
                qt, kc = divmod(u, len(MAX_CHUNKS))
                bank = max_ps[(slot * (MAX_USES + 1) + u) % 2]
                if u == 0:
                    pe.wait_ge(s_q[slot], (b - slot) * 16 + 32)
                pe.wait_ge(s_mfree, b * (MAX_USES + 1) + (u + 1))
                key0 = sum(MAX_CHUNKS[:kc])
                nc.tensor.matmul(bank[:, 0:MAX_CHUNKS[kc]], q_hilo[slot][:, qt * P:(qt + 1) * P],
                                 k.k_hi2[:, kvh, key0:key0 + MAX_CHUNKS[kc]], start=True, stop=True).then_inc(s_mfull, 1)

            def broadcast_max(b, slot):
                pe.wait_ge(s_diag, b + 1)
                pe.wait_ge(s_mfree, b * (MAX_USES + 1) + (MAX_USES + 1))
                bank = max_ps[(slot * (MAX_USES + 1) + MAX_USES) % 2]
                nc.tensor.matmul(bank[:], k.ones_sq[:], diag[:], start=True, stop=True).then_inc(s_mfull, 1)

            def scores(b, slot, kvh, j, e):
                if j == 0 and e == 0:
                    pe.wait_ge(s_mfree, (b + 1) * (MAX_USES + 1) + 2)
                if e == 0:
                    pe.wait_ge(s_exp, b * PAIRS + (j + 1))
                keys = slice((2 * j + e) * P, (2 * j + e + 1) * P)
                out = s_ps[slot2(slot, j)][:, e * QB:(e + 1) * QB]
                nc.tensor.matmul(out, k.k_hi2[:, kvh, keys], q_hilo[slot][:], start=True, stop=False)
                last = nc.tensor.matmul(out, k.k_lo1[0:HD + 1, kvh, keys], q_negm[slot][0:HD + 1, :],
                                        start=False, stop=True)
                if e == 1:
                    last.then_inc(s_score, 1)

            def pv(b, slot, kvh, j, e):
                if j == 0 and e == 0:
                    pe.wait_ge(s_hisum, b + 1)
                    pe.wait_ge(s_losum, b + 1)
                if e == 0:
                    pe.wait_ge(s_exp, b * PAIRS + (j + 3))
                    if j in POOL_LO:
                        pe.wait_ge(s_lo_pool, b * len(POOL_LO) + (POOL_LO.index(j) + 1))
                    else:
                        before = sum(1 for m in range(j) if m not in POOL_LO)
                        pe.wait_ge(s_lo_dve, b * (PAIRS - len(POOL_LO)) + (before + 1))
                kt = 2 * j + e
                q = slice(e * QB, (e + 1) * QB)
                hi, lo = prob_hi[slot3(j)][:, q], prob_lo[slot3(j)][:, q]
                first, final = kt == 0, kt == KT - 1
                nc.tensor.matmul(hi_ps[:], k.v_hl[:, kt, kvh, :], hi, start=first, stop=final)
                nc.tensor.matmul(lo_ps[:], k.zero_one[:], hi, start=first, stop=False)
                last = nc.tensor.matmul(lo_ps[:], v_one[:, kt, kvh, :], lo, start=False, stop=final)
                if e == 1:
                    last.then_inc(s_pv, 1)

            for u in range(MAX_USES):
                max_use(0, 0, 0, u)
            pe.wait_ge(s_vone, 1)
            broadcast_max(0, 0)
            for j in range(2):
                for e in range(2):
                    scores(0, 0, 0, j, e)

            def body(b, slot, kvh, next_kvh):
                u = 0
                for j in range(PAIRS):
                    n_max = MAX_AT[j] if next_kvh is not None else 0
                    if j + 2 < PAIRS:
                        ahead = [(scores, b, slot, kvh, j + 2, e) for e in range(2)]
                    elif next_kvh is not None:
                        ahead = [(scores, b + 1, 1 - slot, next_kvh, j + 2 - PAIRS, e) for e in range(2)]
                    else:
                        ahead = []
                    here = [(pv, b, slot, kvh, j, e) for e in range(2)]
                    for n, (f, *args) in enumerate(ahead + here):
                        if n == 2 and next_kvh is not None and j == MAX_ROW_AT:
                            broadcast_max(b + 1, 1 - slot)
                        f(*args)
                        if n < n_max:
                            max_use(b + 1, 1 - slot, next_kvh, u)
                            u += 1

            run(pe, body)


def project_gates(nc, k, d):
    with ExitStack() as ctx:
        def sb(name, shape, dt=F32):
            return ctx.enter_context(nc.sbuf_tensor(name, shape, dt))

        TG = QB
        N_TG = SEQ // TG
        NG = MT - GROUPS
        w_raw = k.w_raw
        w_hi = k.w_rest_hi + [sb(f"w_rest_hi{n}", [P, KD, CH], F32R) for n in range(2, NCH)]
        w_lo = sb("w_rest_lo", [P, KD, REST_W], F32R)
        hh = [k.hh0, sb("hh1", [P, KD, TG], F32R)]
        hl = [k.hl0, sb("hl1", [P, KD, TG], F32R)]
        stage = [sb(f"stage{i}", [P, TG]) for i in range(2)]
        den = sb("den_all", [P, NB * QB // P])
        acc = [ctx.enter_context(nc.psum_tensor(f"acc{i}", [P, TG], F32)) for i in range(4)]
        even = sb("even_sum", [P, SUB])
        S = k.sem
        s_wlo = S("w_rest_lo_ready")
        s_hh, s_hl = k.s_hh, k.s_hl
        s_acc, s_free = S("rest_projected"), S("rest_bank_read")
        s_den, s_dinv, s_dst = S("den_loaded"), S("den_inverted"), S("den_inv_stored")
        s_comb = S("position_sums")
        s_st = [S(f"rest_stored{i}") for i in range(2)]
        h_v = k.h_v
        r_v = k.rest_dram.rearrange("m p (g t) -> g m p t", t=TG)
        den_rows = [v.rearrange("b (a q) -> (b a) q", q=P) for v in (k.den_dram, k.inv_dram)]

        def run(engine, body):
            with engine.Fori(0, N_TG // 2) as i:
                for slot in range(2):
                    body(i * 2 + slot, slot, i)

        block = ctx.enter_context(nc.Block())

        @block.sync
        def _(sp):
            sp.dma_start(den[:], den_rows[0]).then_inc(s_den, 16)
            for c in range(2, NCH):
                sp.wait_ge(s_wlo, c - 1)
                sp.dma_start(w_raw[c % 2], k.w_rest_v[C_ORDER[c]]).then_inc(k.s_raw[c % 2], 16)
            sp.dma_start(hh[1][:].bitcast(F32), h_v[1][0]).then_inc(s_hh[1], 16)
            sp.dma_start(hl[1][:].bitcast(F32), h_v[1][1]).then_inc(s_hl[1], 16)
            sp.wait_ge(s_dinv, 1)
            sp.dma_start(den_rows[1], den[:]).then_inc(s_dst, 16)
            for tg in range(N_TG):
                for n in range(GROUPS, MT):
                    sp.wait_ge(s_free, tg * MT + (n + 5))
                    sp.dma_start(r_v[tg][M_ORDER[n]], stage[n % 2][:]).then_inc(s_st[n % 2], 16)
                if tg + 2 < N_TG:
                    sp.wait_ge(s_acc, (tg + 1) * MT)
                    sp.dma_start(hh[tg % 2][:].bitcast(F32), h_v[tg + 2][0]).then_inc(s_hh[tg % 2], 16)
                    sp.dma_start(hl[tg % 2][:].bitcast(F32), h_v[tg + 2][1]).then_inc(s_hl[tg % 2], 16)
            sp.wait_ge(s_dst, 16)
            for i in range(2):
                sp.wait_ge(s_st[i], 16 * (N_TG * NG // 2 + 1))

        @block.gpsimd
        def _(pool):
            for n in range(2, NCH):
                pool.dma_start(w_hi[n][:], k.w_rest_v[C_ORDER[n]]).then_inc(k.s_rest_hi[n], 16)
            for n in range(2, NCH):
                pool.wait_ge(k.s_rest_hi[n], 16)

        @block.vector
        def _(dve):
            for n in range(NCH):
                cols = slice(n * CH, (n + 1) * CH)
                dve.wait_ge(k.s_raw[n % 2], 16 * (n // 2 + 1))
                dve.wait_ge(k.s_rest_hi[n], 16)
                nc.vector.tensor_tensor(w_lo[:, :, cols], w_raw[n % 2], w_hi[n][:].bitcast(F32),
                                        ALU.subtract).then_inc(s_wlo, 1)
            dve.wait_ge(s_den, 16)
            nc.vector.reciprocal(den[:], den[:]).then_inc(s_dinv, 1)
            dve.wait_ge(s_free, (N_TG - 1) * MT + GROUPS + 4)
            for g in range(GROUPS):
                q = [k.u[n][:, g, :] for n in range(RADIX)]
                steps = ((even[:], q[0], q[2], ALU.add), (q[2], q[0], q[2], ALU.subtract),
                         (q[0], q[1], q[3], ALU.add), (q[3], q[1], q[3], ALU.subtract),
                         (q[1], even[:], q[0], ALU.subtract), (q[0], even[:], q[0], ALU.add))
                for n, (out, a, b, op) in enumerate(steps):
                    if g or n:
                        dve.wait_ge(s_comb, len(steps) * g + n)
                    nc.vector.tensor_tensor(out, a, b, op).then_inc(s_comb, 1)
            dve.wait_ge(s_comb, GROUPS * len(steps))

        @block.scalar
        def _(act):
            act.sem_inc(s_free, 4)
            for i in range(2):
                act.sem_inc(s_st[i], 16)

            def body(tg, slot, i):
                for n in range(MT):
                    act.wait_ge(s_acc, tg * MT + (n + 1))
                    if n < GROUPS:
                        if slot:
                            act.wait_ge(s_wlo, NCH)
                        nc.scalar.activation(k.u_sides[slot][:, bass.ds(i, 1), n, :].rearrange("p a n -> p (a n)"),
                                             acc[n % 4][:], ACT.Copy).then_inc(s_free, 1)
                    else:
                        act.wait_ge(s_st[n % 2], tg * (16 * NG // 2) + 16 * ((n - GROUPS) // 2 + 1))
                        nc.scalar.activation(stage[n % 2][:], acc[n % 4][:], ACT.Silu).then_inc(s_free, 1)

            run(act, body)

        @block.tensor
        def _(pe):
            def body(tg, slot, i):
                pe.wait_ge(s_hh[slot], i * 16 + 16)
                pe.wait_ge(s_hl[slot], i * 16 + 16)
                for n in range(MT):
                    cols = slice(n % 2 * P, (n % 2 + 1) * P)
                    pe.wait_ge(s_wlo, n // 2 + 1)
                    pe.wait_ge(s_free, tg * MT + (n + 1))
                    for c in range(KD):
                        last = split_matmul(nc.tensor, acc[n % 4][:], w_hi[n // 2][:, c, cols], w_lo[:, c, n * P:(n + 1) * P],
                                            hh[slot][:, c, :], hl[slot][:, c, :], c == 0, c == KD - 1)
                    last.then_inc(s_acc, 1)

            run(pe, body)


def fourier(nc, k, d):
    with ExitStack() as ctx:
        def sb(name, shape, dt=F32):
            return ctx.enter_context(nc.sbuf_tensor(name, shape, dt))

        def ps(name, shape):
            return ctx.enter_context(nc.psum_tensor(name, shape, F32))

        ORDER = (0, 2, 1, 3)
        PARTS = {0: ((0, 1),), 2: ((1, 1),), 1: ((2, 1), (3, 0)), 3: ((2, 1), (3, 2))}
        NTAB = 5
        u = k.u
        c_hi = sb("c_hi", [P, 2, GROUPS, SUB], F32R)
        c_lo = sb("c_lo", [P, 2, GROUPS, SUB], F32R)
        ab_hi = sb("ab_hi", [P, SUBT, GROUPS, 2 * P], F32R)
        ab_lo = sb("ab_lo", [P, SUBT, GROUPS, 2 * P], F32R)
        tab = [sb(f"tab{i}", [P, 2, 2, SUB], F32R) for i in range(NTAB)]
        wf = sb("wf", [P, GROUPS, P])
        chan = sb("chan", [P, 2, P])
        m_hi = sb("m_hi", [P, GROUPS, 4, P], F32R)
        m_lo = sb("m_lo", [P, GROUPS, 4, P], F32R)
        y = k.y
        ab_ps = [ps(f"ab_ps{i}", [P, 2, 2 * P]) for i in range(4)]
        dft_ps = [ps(f"dft_ps{i}", [P, SUB]) for i in range(GROUPS)]
        m_ps = dft_ps[0:2]

        S = k.sem
        s_in = S("fourier_small_loaded")
        s_tab = [S(f"table_loaded{i}") for i in range(NTAB)]
        s_tabfree, s_dft = S("table_used"), S("dft_bank_done")
        s_m, s_mhi, s_mlo, s_mneg = S("channel_product"), S("m_hi_ready"), S("m_lo_ready"), S("m_negated")
        s_chi, s_clo = S("sum_hi_ready"), S("sum_lo_ready")
        s_ab, s_abhi, s_ablo = S("ab_product"), S("ab_hi_ready"), S("ab_lo_ready")
        s_y = S("y_written")
        s_norm = S("att0_normed")
        s_w, s_wg = S("w_o_loaded"), S("w_o_gated")

        block = ctx.enter_context(nc.Block())

        @block.sync
        def _(sp):
            sp.dma_start(chan[:], d["chan"]).then_inc(s_in, 16)
            sp.dma_start(wf[:], d["w_f"][0].rearrange("g c n -> c g n")).then_inc(s_in, 16)
            sp.wait_ge(s_clo, RADIX)
            w_o_v = d["w_o"][0].rearrange("(a k p) n -> a p k n", a=2, p=P)
            for a in range(2):
                sp.dma_start(k.w_o_half[a], w_o_v[a]).then_inc(s_w, 16)
            load_attention(sp, k, 0, 0, k.att0, k.inv0, k.gate0, k.s_att0)
            for g in range(GROUPS):
                sp.wait_ge(s_y, (RADIX - 1) * GROUPS + g + 1)
                sp.dma_start(k.y_dram[g], y[:, g].rearrange("p n r -> p (n r)")).then_inc(k.s_yst, 16)

        @block.gpsimd
        def _(pool):
            for n in range(RADIX * SUBT):
                if n >= NTAB:
                    pool.wait_ge(s_tabfree, n - NTAB + 1)
                pool.dma_start(tab[n % NTAB][:], d["dft"][ORDER[n // SUBT], n % SUBT]).then_inc(s_tab[n % NTAB], 16)
            for i in range(NTAB):
                pool.wait_ge(s_tab[i], 16 * len(range(i, RADIX * SUBT, NTAB)))

        @block.scalar
        def _(act):
            def sum_hi(n):
                if n >= 2:
                    act.wait_ge(s_ab, 2 * SUBT * (n - 1))
                nc.scalar.activation(c_hi[:, n % 2], u[n], ACT.Copy).then_inc(s_chi, 1)

            sum_hi(0)
            act.wait_ge(s_m, 2)
            for i in range(2):
                nc.scalar.activation(m_hi[:, :, 1 + i, :], m_ps[i][:].rearrange("p (g c) -> p g c", g=GROUPS),
                                     ACT.Copy).then_inc(s_mhi, 1)
            sum_hi(1)
            act.wait_ge(s_mlo, 2)
            for part, of in ((0, 2), (3, 1)):
                nc.scalar.activation(m_hi[:, :, part, :], m_hi[:, :, of, :].bitcast(F32), ACT.Copy, scale=-1.0)
                last = nc.scalar.activation(m_lo[:, :, part, :], m_lo[:, :, of, :].bitcast(F32), ACT.Copy, scale=-1.0)
            last.then_inc(s_mneg, 1)
            for step, j in enumerate(ORDER):
                for n in range(2 * SUBT):
                    mt, gp = divmod(n, 2)
                    act.wait_ge(s_ab, 2 * SUBT * step + n + 1)
                    if step:
                        act.wait_ge(s_tabfree, step * SUBT)
                    nc.scalar.activation(ab_hi[:, mt, 2 * gp:2 * gp + 2, :], ab_ps[n % 4][:], ACT.Copy).then_inc(s_abhi, 1)
                if step < 2:
                    sum_hi(step + 2)
                for g in range(GROUPS):
                    act.wait_ge(s_dft, GROUPS * step + g + 1)
                    nc.scalar.activation(y[:, g, :, j], dft_ps[g][:], ACT.Copy).then_inc(s_y, 1)

        @block.vector
        def _(dve):
            def sum_lo(n):
                dve.wait_ge(s_chi, n + 1)
                nc.vector.tensor_tensor(c_lo[:, n % 2], u[n], c_hi[:, n % 2].bitcast(F32),
                                        ALU.subtract).then_inc(s_clo, 1)

            sum_lo(0)
            for i in range(2):
                dve.wait_ge(s_mhi, i + 1)
                nc.vector.tensor_tensor(m_lo[:, :, 1 + i, :], m_ps[i][:].rearrange("p (g c) -> p g c", g=GROUPS),
                                        m_hi[:, :, 1 + i, :].bitcast(F32), ALU.subtract).then_inc(s_mlo, 1)
            sum_lo(1)
            for step in range(RADIX):
                for n in range(2 * SUBT):
                    mt, gp = divmod(n, 2)
                    dve.wait_ge(s_abhi, 2 * SUBT * step + n + 1)
                    hi = ab_hi[:, mt, 2 * gp:2 * gp + 2, :]
                    nc.vector.tensor_tensor(ab_lo[:, mt, 2 * gp:2 * gp + 2, :], ab_ps[n % 4][:], hi.bitcast(F32),
                                            ALU.subtract).then_inc(s_ablo, 1)
                if step < 2:
                    sum_lo(step + 2)
                if step >= 2:
                    dve.wait_ge(s_w, 32)
                    for c in range((step - 2) * KD // 2, (step - 1) * KD // 2):
                        nc.vector.tensor_tensor(k.w_o_raw[c], k.w_o_raw[c], k.gate_bc[:],
                                                ALU.mult).then_inc(s_wg, 1)
            dve.wait_ge(k.s_att0, 16 * ATT_LOADS)
            nc.vector.tensor_tensor(k.att0[:], k.att0[:], k.inv0[:], ALU.mult).then_inc(s_norm, 1)
            dve.wait_ge(s_norm, 1)
            nc.vector.tensor_tensor(k.att0[:], k.att0[:], k.gate0[:], ALU.mult).then_inc(s_norm, 1)
            dve.wait_ge(s_norm, 2)
            dve.wait_ge(s_wg, KD)

        @block.tensor
        def _(pe):
            pe.wait_ge(s_in, 32)
            for i in range(2):
                nc.tensor.matmul(m_ps[i][:], chan[:, i, :], wf[:].rearrange("p g c -> p (g c)"), start=True,
                                 stop=True).then_inc(s_m, 1)
            pe.wait_ge(s_mlo, 2)
            for step, j in enumerate(ORDER):
                pe.wait_ge(s_clo, (1, 2, 4, 4)[step])
                if step == 2:
                    pe.wait_ge(s_mneg, 1)
                for n in range(2 * SUBT):
                    mt, gp = divmod(n, 2)
                    use = 2 * SUBT * step + n
                    if use >= 4:
                        pe.wait_ge(s_ablo, use - 3)
                    for gg in range(2):
                        g = 2 * gp + gg
                        for i, (src, part) in enumerate(PARTS[j]):
                            rows = (slice(None), src % 2, g, slice(mt * P, (mt + 1) * P))
                            last = split_matmul(nc.tensor, ab_ps[n % 4][:, gg, :], c_hi[rows], c_lo[rows],
                                                m_hi[:, g, part:part + 2, :].rearrange("p a c -> p (a c)"),
                                                m_lo[:, g, part:part + 2, :].rearrange("p a c -> p (a c)"),
                                                i == 0, i == len(PARTS[j]) - 1)
                    last.then_inc(s_ab, 1)
                if step:
                    pe.wait_ge(s_y, step * GROUPS)

                def dft(mt, g):
                    n = step * SUBT + mt
                    pe.wait_ge(s_ablo, 2 * SUBT * step + 2 * mt + 2)
                    pe.wait_ge(s_tab[n % NTAB], 16 * (n // NTAB + 1))
                    for cs in range(2):
                        a = (slice(None), mt, g, slice(cs * P, (cs + 1) * P))
                        last = split_matmul(nc.tensor, dft_ps[g][:], ab_hi[a], ab_lo[a], tab[n % NTAB][:, 0, cs, :],
                                            tab[n % NTAB][:, 1, cs, :], mt == 0 and cs == 0,
                                            mt == SUBT - 1 and cs == 1)
                    return last

                if step < RADIX - 1:
                    for mt in range(SUBT):
                        for g in range(GROUPS):
                            last = dft(mt, g)
                            if mt == SUBT - 1:
                                last.then_inc(s_dft, 1)
                        if mt < SUBT - 1:
                            last.then_inc(s_tabfree, 1)
                    pe.wait_ge(s_dft, GROUPS * (step + 1))
                    pe.sem_inc(s_tabfree, 1)
                else:
                    for g in range(GROUPS):
                        for mt in range(SUBT):
                            last = dft(mt, g)
                        last.then_inc(s_dft, 1)


ATT_LOADS = 5


def load_attention(sp, k, slot, blk, att, inv, gate, sem):
    half = QB // 2
    cols = slice(slot * half, (slot + 1) * half)
    att_v = k.att_dram.rearrange("(f e b) c q -> b e c f q", e=2, b=NQB)
    inv_v = k.inv_dram.rearrange("(f e b) q -> b e f q", e=2, b=NQB)
    for e in range(2):
        rows = slice(e * HD, (e + 1) * HD)
        sp.dma_start(att[rows], att_v[blk][e][:, :, cols]).then_inc(sem, 16)
        sp.dma_start(inv[rows], inv_v[blk][e][:, cols].partition_broadcast(HD)).then_inc(sem, 16)
    sp.dma_start(gate[:], k.rest_dram[0:ATTN_W // P, :, bass.ds(blk * QB + slot * half, half)]
                 .rearrange("m p t -> p m t")).then_inc(sem, 16)


def output(nc, k, d):
    with ExitStack() as ctx:
        def sb(name, shape, dt=F32):
            return ctx.enter_context(nc.sbuf_tensor(name, shape, dt))

        TG = 2 * P
        N_TG = SEQ // TG
        AF = ATTN_W // P
        ATT, FOU = slice(0, AF), slice(AF, KD)
        w_raw = k.w_o_raw
        w_hi = sb("w_o_hi", [P, KD, D], F32R)
        w_lo = sb("w_o_lo", [P, KD, D], F32R)
        spare = k.y[:].rearrange("p g n r -> p (g n r)")
        yin1, gin1 = (spare[:, i * KD * TG:(i + 1) * KD * TG].rearrange("p (k t) -> p k t", k=KD) for i in range(2))
        x0, x1, res0, res1 = (spare[:, 2 * KD * TG + i * D:2 * KD * TG + (i + 1) * D] for i in range(4))
        yin = [sb("yin0", [P, KD, TG])[:], yin1]
        gin = [sb("gin0", [P, KD, TG])[:], gin1]
        x, res = [x0, x1], [res0, res1]
        inv = [k.inv0, sb("inv1", [P, AF, TG])]
        y_hi = [sb(f"y_hi{i}", [P, KD, TG], F32R) for i in range(2)]
        y_lo = [sb(f"y_lo{i}", [P, KD, TG], F32R) for i in range(2)]
        square = sb("res_square", [P, 2, D], mybir.dt.bfloat16)
        stat = [sb(f"res_stat{i}", [P, 1]) for i in range(2)]
        mean = [sb(f"res_mean{i}", [P, 1]) for i in range(2)]
        rstd = [sb(f"res_rstd{i}", [P, 1]) for i in range(2)]
        minus_half = sb("out_minus_half", [P, 1])
        o_ps = [ctx.enter_context(nc.psum_tensor(f"o_ps{i}", [P, 2, 512], F32)) for i in range(2)]
        S = k.sem
        s_whi, s_wlo = S("w_o_hi_ready"), S("w_o_lo_ready")
        s_att_in = [S("att_inputs_loaded0"), S("att_inputs_loaded1")]
        s_fou_in = [S("fourier_inputs_loaded0"), S("fourier_inputs_loaded1")]
        s_norm, s_y, s_yhi, s_ylo = S("att_normed"), S("y_gated"), S("y_hi_ready"), S("y_lo_ready")
        s_x = [S("x_res_loaded0"), S("x_res_loaded1")]
        s_o, s_add, s_sum, s_mean, s_rstd, s_out = (S("out_projected"), S("residual_added"), S("res_squares"),
                                                    S("res_mean_ready"), S("res_rstd_ready"), S("out_ready"))
        s_half = S("out_minus_half_set")
        s_st = [S("out_stored0"), S("out_stored1")]
        x_v = d["x"][0].rearrange("(t p) n -> t p n", p=P)
        out_v = d["out"][0].rearrange("(t p) n -> t p n", p=P)
        FOU_LOADS = 2
        PREP0 = 2

        def run(engine, body):
            body(0, 0, 0, True, True)
            with engine.Fori(0, (N_TG - 4) // 2) as i:
                body(i * 2 + 1, 1, i + 1, True, True)
                body(i * 2 + 2, 0, i + 1, True, True)
            for g in range(N_TG - 3, N_TG):
                body(g, g % 2, (g + 1) // 2, g + 2 < N_TG, g + 1 < N_TG)

        block = ctx.enter_context(nc.Block())

        @block.sync
        def _(sp):
            def load_fourier(slot, blk):
                tok = bass.ds(blk * QB + slot * TG, TG)
                sp.dma_start(yin[slot][:, FOU, :], k.y_dram[:, :, tok].rearrange("m p t -> p m t")).then_inc(s_fou_in[slot], 16)
                sp.dma_start(gin[slot][:, FOU, :],
                             k.rest_dram[2 * AF:3 * AF, :, tok].rearrange("m p t -> p m t")).then_inc(s_fou_in[slot], 16)

            def load_group(slot, blk):
                load_attention(sp, k, slot, blk, yin[slot][:, ATT, :], inv[slot], gin[slot][:, ATT, :], s_att_in[slot])
                load_fourier(slot, blk)

            sp.wait_ge(k.s_yst, 16 * GROUPS)
            load_fourier(0, 0)
            for e in range(2):
                sp.dma_start(x[e], x_v[e]).then_inc(s_x[e], 16)
            load_group(1, 0)

            def body(g, slot, m, ahead, after):
                if ahead:
                    sp.wait_ge(s_ylo, g + PREP0)
                    sp.wait_ge(s_yhi, g + PREP0)
                    load_group(slot, m + (1 - slot))
                for e in range(2):
                    t = g * 2 + e
                    if after:
                        sp.wait_ge(s_add, t + 3)
                        sp.dma_start(x[e], x_v[t + 2]).then_inc(s_x[e], 16)
                    sp.wait_ge(s_out, t + 1)
                    sp.dma_start(out_v[t], res[e]).then_inc(s_st[e], 16)

            run(sp, body)
            for e in range(2):
                sp.wait_ge(s_st[e], 16 * (N_TG + 1))

        @block.gpsimd
        def _(pool):
            nc.gpsimd.memset(minus_half[:], -0.5).then_inc(s_half, 1)
            pool.wait_ge(s_half, 1)

            def body(g, slot, m, ahead, after):
                for e in range(2):
                    pool.wait_ge(s_mean, g * 2 + (e + 1))
                    nc.gpsimd.tensor_tensor(rstd[e][:], mean[e][:], minus_half[:], ALU.pow).then_inc(s_rstd, 1)

            run(pool, body)

        @block.scalar
        def _(act):
            act.sem_inc(s_st[0], 16)
            act.sem_inc(s_st[1], 16)
            nc.scalar.activation(y_hi[0][:, ATT, :], k.att0[:], ACT.Copy).then_inc(s_yhi, 1)
            for c in range(KD):
                nc.scalar.activation(w_hi[:, c, :], w_raw[c], ACT.Copy).then_inc(s_whi, 1)
            act.wait_ge(s_y, 1)
            nc.scalar.activation(y_hi[0][:, FOU, :], yin[0][:, FOU, :], ACT.Copy).then_inc(s_yhi, 1)

            def body(g, slot, m, ahead, after):
                if after:
                    act.wait_ge(s_y, g + 2)
                    act.wait_ge(s_o, g * 2 + 2)
                    nc.scalar.activation(y_hi[1 - slot][:], yin[1 - slot][:], ACT.Copy).then_inc(s_yhi, 1)
                for e in range(2):
                    act.wait_ge(s_add, g * 2 + (e + 3))
                    nc.scalar.activation(square[:, e, :], res[e], ACT.Square, accum_out=stat[e][:]).then_inc(s_sum, 1)

            run(act, body)

        @block.vector
        def _(dve):
            dve.sem_inc(s_add, 2)

            dve.wait_ge(s_yhi, 1)
            nc.vector.tensor_tensor(y_lo[0][:, ATT, :], k.att0[:], y_hi[0][:, ATT, :].bitcast(F32),
                                    ALU.subtract).then_inc(s_ylo, 1)
            for c in range(KD):
                dve.wait_ge(s_whi, c + 1)
                nc.vector.tensor_tensor(w_lo[:, c, :], w_raw[c], w_hi[:, c, :].bitcast(F32),
                                        ALU.subtract).then_inc(s_wlo, 1)
            dve.wait_ge(s_fou_in[0], 16 * FOU_LOADS)
            nc.vector.tensor_tensor(yin[0][:, FOU, :], yin[0][:, FOU, :], gin[0][:, FOU, :], ALU.mult).then_inc(s_y, 1)
            dve.wait_ge(s_yhi, 2)
            nc.vector.tensor_tensor(y_lo[0][:, FOU, :], yin[0][:, FOU, :], y_hi[0][:, FOU, :].bitcast(F32),
                                    ALU.subtract).then_inc(s_ylo, 1)

            def body(g, slot, m, ahead, after):
                if after:
                    nxt = 1 - slot
                    dve.wait_ge(s_att_in[nxt], m * (16 * ATT_LOADS) + (16 * ATT_LOADS if nxt else 0))
                    dve.wait_ge(s_fou_in[nxt], m * (16 * FOU_LOADS) + 16 * FOU_LOADS)
                    nc.vector.tensor_tensor(yin[nxt][:, ATT, :], yin[nxt][:, ATT, :], inv[nxt][:],
                                            ALU.mult).then_inc(s_norm, 1)
                    dve.wait_ge(s_norm, g + 1)
                    nc.vector.tensor_tensor(yin[nxt][:], yin[nxt][:], gin[nxt][:], ALU.mult).then_inc(s_y, 1)
                    dve.wait_ge(s_yhi, g + (1 + PREP0))
                    nc.vector.tensor_tensor(y_lo[nxt][:], yin[nxt][:], y_hi[nxt][:].bitcast(F32),
                                            ALU.subtract).then_inc(s_ylo, 1)
                for e in range(2):
                    t = g * 2 + e
                    dve.wait_ge(s_o, t + 3)
                    dve.wait_ge(s_x[e], g * 16 + 16)
                    dve.wait_ge(s_st[e], g * 16 + 16)
                    nc.vector.tensor_tensor(res[e], o_ps[e][:].rearrange("p a n -> p (a n)"), x[e],
                                            ALU.add).then_inc(s_add, 1)
                    dve.wait_ge(s_sum, t + 1)
                    nc.vector.tensor_scalar(mean[e][:], stat[e][:], 1.0 / D, EPS, ALU.mult, ALU.add).then_inc(s_mean, 1)
                    dve.wait_ge(s_rstd, t + 1)
                    nc.vector.scalar_tensor_tensor(res[e], res[e], rstd[e][:], k.final_bc[:], ALU.mult,
                                                   ALU.mult).then_inc(s_out, 1)

            run(dve, body)

        @block.tensor
        def _(pe):
            pe.sem_inc(s_o, 2)

            def product(slot, e, n, c):
                cols = slice(n * 512, (n + 1) * 512)
                toks = slice(e * P, (e + 1) * P)
                return split_matmul(nc.tensor, o_ps[e][:, n, :], y_hi[slot][:, c, toks], y_lo[slot][:, c, toks],
                                    w_hi[:, c, cols], w_lo[:, c, cols], c == 0, c == KD - 1)

            def body(g, slot, m, ahead, after):
                if isinstance(g, int) and g == 0:
                    for c in range(KD):
                        pe.wait_ge(s_wlo, c + 1)
                        pe.wait_ge(s_ylo, c // AF + 1)
                        for e in range(2):
                            for n in range(2):
                                last = product(slot, e, n, c)
                            if c == KD - 1:
                                last.then_inc(s_o, 1)
                    return
                pe.wait_ge(s_ylo, g + PREP0)
                for e in range(2):
                    pe.wait_ge(s_add, g * 2 + (e + 1))
                    for n in range(2):
                        for c in range(KD):
                            last = product(slot, e, n, c)
                    last.then_inc(s_o, 1)

            run(pe, body)


class Shared:
    pass


def build(nc, d):
    with ExitStack() as ctx:
        def sb(name, shape, dt=F32):
            return ctx.enter_context(nc.sbuf_tensor(name, shape, dt))

        def dram(name, shape):
            return nc.dram_tensor(name, shape, F32, kind="Internal").ap()

        k = Shared()
        k.sem = lambda name: ctx.enter_context(nc.semaphore(name))
        k.h_dram = dram("h_scratch", (2, KD, P, SEQ))
        k.q_dram = dram("q_scratch", (NB, P, QB))
        k.att_dram = dram("att_scratch", (NB, HD, QB))
        k.den_dram = dram("den_scratch", (NB, QB))
        k.inv_dram = dram("inv_scratch", (NB, QB))
        k.rest_dram = dram("rest_scratch", (MT, P, SEQ))
        k.y_dram = dram("y_scratch", (GROUPS, P, SEQ))
        k.ident = sb("ident_sb", [P, P])
        k.gate_bc = sb("gate_bc", [P, D])
        k.final_bc = sb("final_bc", [P, D])
        outer = ctx.enter_context(ExitStack())
        right = ctx.enter_context(ExitStack())
        with ExitStack() as inner:
            def sbi(name, shape, dt=F32):
                return inner.enter_context(nc.sbuf_tensor(name, shape, dt))

            k.ones_sq = sbi("ones_sq", [P, P], F32R)
            k.zero_one = sbi("zero_one", [P, P], F32R)
            k.k_hi2 = sbi("k_hi2", [P, HKV, KEYS], F32R)
            k.k_lo1 = sbi("k_lo1", [P, HKV, KEYS], F32R)
            k.v_hl = sbi("v_hl", [P, KT, HKV, P], F32R)
            with ExitStack() as first:
                k.scale = first.enter_context(nc.sbuf_tensor("scale", [P, 2, KD], F32))
                k.shift = first.enter_context(nc.sbuf_tensor("shift", [P, 2, KD], F32))
                k.head_bc = first.enter_context(nc.sbuf_tensor("head_bc", [P, HN * HD], F32))
                k.wqkv_hi = first.enter_context(nc.sbuf_tensor("wqkv_hi", [P, KD, QKV_W], F32R))
                k.wqkv_lo = first.enter_context(nc.sbuf_tensor("wqkv_lo", [P, KD, QKV_W], F32R))
                k.x = [first.enter_context(nc.sbuf_tensor(f"x{i}", [P, 2, D], F32)) for i in range(2)]
                k.square = first.enter_context(nc.sbuf_tensor("square", [P, 2, D], mybir.dt.bfloat16))
                k.stat, k.stat_eps, k.rstd = ([first.enter_context(nc.sbuf_tensor(f"{name}{i}", [P, 2], F32))
                                               for i in range(2)] for name in ("stat", "stat_eps", "rstd"))
                k.minus_half = first.enter_context(nc.sbuf_tensor("minus_half", [P, HN], F32))
                k.s_x = [k.sem("x_loaded0"), k.sem("x_loaded1")]
                k.s_sum, k.s_eps, k.s_rstd, k.s_xhat = (k.sem("x_square_sums"), k.sem("x_eps_added"),
                                                        k.sem("x_rstd_ready"), k.sem("x_normed"))
                modulation(nc, k, d)
                project_qkv(nc, k, d)
            k.u_odd = outer.enter_context(nc.sbuf_tensor("u_odd", [P, 2, GROUPS, SUB], F32, side="right"))
            k.w_rest_hi = [right.enter_context(nc.sbuf_tensor(f"w_rest_hi{n}", [P, KD, CH], F32R, side="right"))
                           for n in range(2)]
            k.hh0, k.hl0 = (right.enter_context(nc.sbuf_tensor(name, [P, KD, QB], F32R, side="right"))
                            for name in ("hh0", "hl0"))
            k.w_raw = [k.u_odd[:, i].rearrange("p g (a n) -> p (g a) n", n=CH) for i in range(2)]
            k.w_rest_v = d["w_in"][0][:, GA0:GA0 + REST_W].rearrange("(k p) (c n) -> c p k n", p=P, n=CH)
            k.s_raw = [k.sem("w_rest_loaded0"), k.sem("w_rest_loaded1")]
            k.s_rest_hi = [k.sem(f"w_rest_hi_loaded{n}") for n in range(NCH)]
            k.h_v = k.h_dram.rearrange("e k p (g t) -> g e p k t", t=QB)
            k.s_hh = [k.sem("hh_loaded0"), k.sem("hh_loaded1")]
            k.s_hl = [k.sem("hl_loaded0"), k.sem("hl_loaded1")]
            attention(nc, k, d)
        with ExitStack() as branch:
            k.u_even = branch.enter_context(nc.sbuf_tensor("u_even", [P, 2, GROUPS, SUB], F32))
            k.u_sides = (k.u_even, k.u_odd)
            k.u = [k.u_sides[n % 2][:, n // 2] for n in range(RADIX)]
            project_gates(nc, k, d)
            right.close()
            k.w_o_half = [side[:].rearrange("p m g n -> p (m g n)").rearrange("p (k n) -> p k n", n=D)
                          for side in k.u_sides]
            k.w_o_raw = [k.w_o_half[c * 2 // KD][:, c % (KD // 2), :] for c in range(KD)]
            k.att0, k.inv0, k.gate0 = (branch.enter_context(nc.sbuf_tensor(name, [P, ATTN_W // P, QB // 2], F32))
                                       for name in ("first_att", "first_inv", "first_gate"))
            k.y = branch.enter_context(nc.sbuf_tensor("y", [P, GROUPS, SUB, RADIX], F32))
            k.s_att0, k.s_yst = k.sem("att0_inputs_loaded"), k.sem("y_stored")
            fourier(nc, k, d)
            output(nc, k, d)


def constants():
    import numpy as np
    grid_w, theta, freqs = 64, 10000.0, HD // 4
    pos = np.arange(SEQ)
    inv = np.float32(theta) ** (-np.arange(freqs, dtype=np.float32) / np.float32(freqs))
    ang = np.stack([(pos // grid_w).astype(np.float32)[:, None] * inv,
                    (pos % grid_w).astype(np.float32)[:, None] * inv], axis=1)
    ang = np.repeat(ang[:, :, None, :], 2, axis=2).reshape(SEQ, HD)
    c = np.arange(P)
    chan_ang = 2 * np.pi * np.outer(c, c) / P
    norm = 1.0 / np.sqrt(float(SEQ) * P)
    chan = np.stack([np.cos(chan_ang), np.sin(chan_ang)], axis=1) * norm
    j, m, n = np.arange(RADIX)[:, None, None], np.arange(SUB)[None, :, None], np.arange(SUB)[None, None, :]
    dft_ang = 2 * np.pi * (((RADIX * n + j) * m) % SEQ) / SEQ
    dft = np.stack([np.cos(dft_ang), -np.sin(dft_ang)], axis=2).astype(np.float32)
    bits = dft.view(np.uint32)
    hi = (((bits + np.uint32(0x7FF) + ((bits >> np.uint32(12)) & np.uint32(1))) >> np.uint32(12)) << np.uint32(12))
    hi = hi.view(np.float32)
    dft = np.stack([hi, dft - hi], axis=2).reshape(RADIX, SUBT, P, 2, 2, SUB)
    return {"ident": np.eye(P, dtype=np.float32), "cos": np.cos(ang).astype(np.float32),
            "sin": np.sin(ang).astype(np.float32), "chan": chan.astype(np.float32),
            "dft": np.ascontiguousarray(dft)}


_INS = ["x", "c", "ctx", "c_ctx", "norm_g", "w_mod", "b_mod", "w_in", "q_g", "k_g", "w_f", "w_o", "final_g"]


def kernel(**inputs):
    import numpy as np
    import concourse.bacc as bacc
    from concourse.bass_utils import run_bass_kernel_spmd as launch

    nc = bacc.Bacc("TRN2", target_bir_lowering=False, num_devices=1)
    arrays = {name: np.ascontiguousarray(inputs[name]) for name in _INS}
    arrays.update(constants())
    d = {}
    feeds = {}
    for name, a in arrays.items():
        feeds[f"in_{name}"] = a
        d[name] = nc.dram_tensor(f"in_{name}", a.shape, mybir.dt.from_np(a.dtype), kind="ExternalInput").ap()
    d["out"] = nc.dram_tensor("out_x", (1, SEQ, D), F32, kind="ExternalOutput").ap()
    build(nc, d)
    r = launch(nc, [feeds], core_ids=[0])
    return r.results[0]["out_x"]
```
